# Optimizing a Trainium2 kernel written in Bass

```python
import jax, jax.numpy as jnp
from jax import lax
import numpy as np

D_MODEL = 2048
BATCH = 1
SEQ = 512
DEPTH = 1

HG_HEADS = 8
HG_HEAD_DIM = 128
HG_WIDTH = HG_HEADS * HG_HEAD_DIM
ML_HEADS = 4
ML_QK_DIM = 128
ML_V_DIM = 256
ML_QK_WIDTH = ML_HEADS * ML_QK_DIM
ML_V_WIDTH = ML_HEADS * ML_V_DIM
ML_CONV = 4
CHUNK = 64
D_FF = 5632
FFN_CONV = 3
EPS = 1e-6
SPLIT_SIZES = (HG_WIDTH, HG_WIDTH, HG_WIDTH, HG_WIDTH, 2 * ML_QK_WIDTH, ML_V_WIDTH, ML_V_WIDTH, ML_HEADS, ML_HEADS, D_MODEL, D_MODEL)
IN_WIDTH = sum(SPLIT_SIZES)
FG_OFFSET = sum(SPLIT_SIZES[:8])

kernel_name = "hybrid_hgrn2_mlstm_convffn_block"

def rms_norm(u, gain):
    u32 = u.astype(jnp.float32)
    y = u32 * lax.rsqrt(jnp.mean(u32 * u32, axis=-1, keepdims=True) + EPS)
    return (y * gain.astype(jnp.float32)).astype(u.dtype)

def head_rms_norm(u, n_heads, gain):
    B, T, W = u.shape
    uh = u.reshape(B, T, n_heads, W // n_heads)
    uh = uh * lax.rsqrt(jnp.mean(uh * uh, axis=-1, keepdims=True) + EPS)
    return uh.reshape(B, T, W) * gain.astype(jnp.float32)

def causal_dwconv(u, w, bias):
    K = w.shape[0]
    T = u.shape[1]
    up = jnp.pad(u, ((0, 0), (K - 1, 0), (0, 0)))
    out = bias
    for j in range(K):
        out = out + w[j] * up[:, j:j + T]
    return out

def to_chunks(t, n_heads):
    B, T, W = t.shape
    return t.reshape(B, T // CHUNK, CHUNK, n_heads, W // n_heads).transpose(0, 3, 1, 2, 4)

def from_chunks(t):
    B, H, N, C, d = t.shape
    return t.transpose(0, 2, 3, 1, 4).reshape(B, N * C, H * d)

def gate_chunks(g):
    B, T, H = g.shape
    return g.reshape(B, T // CHUNK, CHUNK, H).transpose(0, 3, 1, 2)

def hgrn2_mix(q_pre, f_pre, i_in, g_pre, lb, gain):
    B = q_pre.shape[0]
    q = jax.nn.silu(q_pre) * (HG_HEAD_DIM ** -0.5)
    f = lb + (1.0 - lb) * jax.nn.sigmoid(f_pre)
    k = 1.0 - f
    q, k, v, log_f = to_chunks(q, HG_HEADS), to_chunks(k, HG_HEADS), to_chunks(i_in, HG_HEADS), to_chunks(jnp.log(f), HG_HEADS)
    b = jnp.cumsum(log_f, axis=3)
    b_last = b[:, :, :, -1]
    q_dec = q * jnp.exp(b)
    k_inv = k * jnp.exp(-b)
    k_end = k * jnp.exp(b_last[:, :, :, None] - b)
    causal = jnp.tril(jnp.ones((CHUNK, CHUNK), dtype=bool))
    attn = jnp.where(causal, jnp.einsum("bhntd,bhnsd->bhnts", q_dec, k_inv), 0.0)
    o_intra = jnp.einsum("bhnts,bhnse->bhnte", attn, v)

    def step(S, inp):
        decay, kc, vc = inp
        S_new = decay[..., None] * S + jnp.einsum("bhcd,bhce->bhde", kc, vc)
        return S_new, S

    S0 = jnp.zeros((B, HG_HEADS, HG_HEAD_DIM, HG_HEAD_DIM), jnp.float32)
    xs = (jnp.moveaxis(jnp.exp(b_last), 2, 0), jnp.moveaxis(k_end, 2, 0), jnp.moveaxis(v, 2, 0))
    _, S_prev = lax.scan(step, S0, xs)
    o_inter = jnp.einsum("bhntd,nbhde->bhnte", q_dec, S_prev)
    o = from_chunks(o_intra + o_inter)
    return head_rms_norm(o, HG_HEADS, gain) * jax.nn.silu(g_pre)

def mlstm_mix(q_in, k_in, v_in, o_pre, ig_pre, fg_pre, gain):
    B = q_in.shape[0]
    q = to_chunks(q_in, ML_HEADS)
    k = to_chunks(k_in, ML_HEADS) * (ML_QK_DIM ** -0.5)
    v = to_chunks(v_in, ML_HEADS)
    ig = gate_chunks(ig_pre)
    log_f = jax.nn.log_sigmoid(gate_chunks(fg_pre))
    b = jnp.cumsum(log_f, axis=-1)
    b_last = b[..., -1]
    logw = b_last[..., None] - b + ig

    def step(carry, inp):
        C, n, m = carry
        bl, lw, kc, vc = inp
        m_new = jnp.maximum(bl + m, jnp.max(lw, axis=-1))
        decay = jnp.exp(bl + m - m_new)
        w = jnp.exp(lw - m_new[..., None])
        C_new = decay[..., None, None] * C + jnp.einsum("bhc,bhcd,bhce->bhde", w, kc, vc)
        n_new = decay[..., None] * n + jnp.einsum("bhc,bhcd->bhd", w, kc)
        return (C_new, n_new, m_new), (C, n, m)

    init = (jnp.zeros((B, ML_HEADS, ML_QK_DIM, ML_V_DIM), jnp.float32),
            jnp.zeros((B, ML_HEADS, ML_QK_DIM), jnp.float32),
            jnp.zeros((B, ML_HEADS), jnp.float32))
    xs = (jnp.moveaxis(b_last, 2, 0), jnp.moveaxis(logw, 2, 0), jnp.moveaxis(k, 2, 0), jnp.moveaxis(v, 2, 0))
    _, (C_prev, n_prev, m_prev) = lax.scan(step, init, xs)
    m_prev = jnp.moveaxis(m_prev, 0, 2)

    causal = jnp.tril(jnp.ones((CHUNK, CHUNK), dtype=bool))
    log_d = jnp.where(causal, b[..., :, None] - b[..., None, :] + ig[..., None, :], -jnp.inf)
    m_inter = b + m_prev[..., None]
    m = jnp.maximum(m_inter, jnp.max(log_d, axis=-1))
    scores = jnp.einsum("bhntd,bhnsd->bhnts", q, k) * jnp.exp(log_d - m[..., None])
    inter_scale = jnp.exp(m_inter - m)
    num = jnp.einsum("bhnts,bhnse->bhnte", scores, v) + inter_scale[..., None] * jnp.einsum("bhntd,nbhde->bhnte", q, C_prev)
    den = jnp.sum(scores, axis=-1) + inter_scale * jnp.einsum("bhntd,nbhd->bhnt", q, n_prev)
    h = num / jnp.maximum(jnp.abs(den), jnp.exp(-m))[..., None]
    h = head_rms_norm(from_chunks(h), ML_HEADS, gain)
    return jax.nn.sigmoid(o_pre) * h

def setup_inputs(seed: int = 0) -> dict:
    key = jax.random.key(seed)
    ks = jax.random.split(key, 24)
    f32 = jnp.float32

    def nrm(k, shape, scale):
        return jax.random.normal(k, shape, f32) * scale

    def gains(k, shape):
        return 1.0 + nrm(k, shape, 0.05)

    b_in = nrm(ks[6], (DEPTH, IN_WIDTH), 0.02)
    b_in = b_in.at[:, FG_OFFSET:FG_OFFSET + ML_HEADS].add(jnp.linspace(3.0, 6.0, ML_HEADS, dtype=f32))
    return {
        "x": nrm(ks[0], (BATCH, SEQ, D_MODEL), 1.0),
        "norm_mix_pre": gains(ks[1], (DEPTH, D_MODEL)),
        "norm_mix_post": gains(ks[2], (DEPTH, D_MODEL)),
        "norm_ffn_pre": gains(ks[3], (DEPTH, D_MODEL)),
        "norm_ffn_post": gains(ks[4], (DEPTH, D_MODEL)),
        "w_in": nrm(ks[5], (DEPTH, D_MODEL, IN_WIDTH), D_MODEL ** -0.5),
        "b_in": b_in,
        "hg_lb_logits": nrm(ks[7], (DEPTH + 1, HG_WIDTH), 0.1),
        "hg_norm": gains(ks[8], (DEPTH, HG_WIDTH)),
        "ml_conv_w": nrm(ks[9], (DEPTH, ML_CONV, 2 * ML_QK_WIDTH), ML_CONV ** -0.5),
        "ml_conv_b": nrm(ks[10], (DEPTH, 2 * ML_QK_WIDTH), 0.02),
        "ml_norm": gains(ks[11], (DEPTH, ML_V_WIDTH)),
        "w_up_a": nrm(ks[12], (DEPTH, HG_WIDTH, D_MODEL), HG_WIDTH ** -0.5),
        "w_up_b": nrm(ks[13], (DEPTH, ML_V_WIDTH, D_MODEL), ML_V_WIDTH ** -0.5),
        "w_out": nrm(ks[14], (DEPTH, D_MODEL, D_MODEL), D_MODEL ** -0.5),
        "ffn_w_gate": nrm(ks[15], (DEPTH, D_MODEL, D_FF), D_MODEL ** -0.5),
        "ffn_w_up": nrm(ks[16], (DEPTH, D_MODEL, D_FF), D_MODEL ** -0.5),
        "ffn_conv_w": nrm(ks[17], (DEPTH, FFN_CONV, D_FF), FFN_CONV ** -0.5),
        "ffn_conv_b": nrm(ks[18], (DEPTH, D_FF), 0.02),
        "ffn_w_down": nrm(ks[19], (DEPTH, D_FF, D_MODEL), D_FF ** -0.5),
    }

def reference(x, norm_mix_pre, norm_mix_post, norm_ffn_pre, norm_ffn_post, w_in, b_in, hg_lb_logits,
              hg_norm, ml_conv_w, ml_conv_b, ml_norm, w_up_a, w_up_b, w_out, ffn_w_gate, ffn_w_up,
              ffn_conv_w, ffn_conv_b, ffn_w_down):
    f32 = jnp.float32
    split_points = [int(p) for p in np.cumsum(SPLIT_SIZES)[:-1]]
    lb_all = jnp.cumsum(jax.nn.softmax(hg_lb_logits.astype(f32), axis=0), axis=0)
    for l in range(DEPTH):
        h = rms_norm(x, norm_mix_pre[l])
        proj = jnp.einsum("btd,dp->btp", h, w_in[l]) + b_in[l]
        (hg_q, hg_f, hg_i, hg_g, ml_qk, ml_v, ml_o, ml_ig, ml_fg, gate_a, gate_b) = jnp.split(proj, split_points, axis=-1)
        y_a = hgrn2_mix(hg_q.astype(f32), hg_f.astype(f32), hg_i.astype(f32), hg_g.astype(f32), lb_all[l], hg_norm[l])
        ml_qk = jax.nn.silu(causal_dwconv(ml_qk, ml_conv_w[l], ml_conv_b[l]))
        ml_q, ml_k = jnp.split(ml_qk, 2, axis=-1)
        y_b = mlstm_mix(ml_q.astype(f32), ml_k.astype(f32), ml_v.astype(f32), ml_o.astype(f32),
                        ml_ig.astype(f32), ml_fg.astype(f32), ml_norm[l])
        branch_a = jnp.einsum("btc,cd->btd", y_a.astype(x.dtype), w_up_a[l])
        branch_b = jnp.einsum("btc,cd->btd", y_b.astype(x.dtype), w_up_b[l])
        merged = jax.nn.sigmoid(gate_a) * branch_a + jax.nn.sigmoid(gate_b) * branch_b
        mix_out = jnp.einsum("btd,de->bte", merged, w_out[l])
        x = x + rms_norm(mix_out, norm_mix_post[l])
        h = rms_norm(x, norm_ffn_pre[l])
        gate = causal_dwconv(jnp.einsum("btd,df->btf", h, ffn_w_gate[l]), ffn_conv_w[l], ffn_conv_b[l])
        up = jnp.einsum("btd,df->btf", h, ffn_w_up[l])
        ffn_out = jnp.einsum("btf,fd->btd", jax.nn.gelu(gate, approximate=True) * up, ffn_w_down[l])
        x = x + rms_norm(ffn_out, norm_ffn_post[l])
    return x


_drawn_inputs = setup_inputs


def setup_inputs(seed=0):
    import zlib

    import numpy as np

    out = dict(_drawn_inputs(seed))
    spreads = {}
    factors = {'hg_lb_logits': 6.629, 'ml_conv_b': 6.63, 'ffn_conv_b': 4.901}
    for name, (base, spread) in spreads.items():
        noise = np.random.default_rng([zlib.crc32(name.encode()), seed]).standard_normal(out[name].shape)
        drawn = base * np.exp(spread * noise) if base else spread * noise
        out[name] = __import__('jax').numpy.asarray(drawn.astype(out[name].dtype))
    for name, factor in factors.items():
        out[name] = (out[name] * factor).astype(out[name].dtype)
    return out
```

```python
from contextlib import ExitStack

import concourse.bass as bass
from concourse import mybir

ALU = mybir.AluOpType
ACT = mybir.ActivationFunctionType
AX = mybir.AxisListType
F32 = mybir.dt.float32
F32R = mybir.dt.float32r
ds = bass.ds

P = 128
D = 2048
T = 512
KT = D // P
TT = T // P
CHUNK = 64
HG_H, HG_W = 8, 1024
ML_H, ML_V, ML_W = 4, 256, 1024
FF = 5632
FT = FF // P
FG = 4
EPS = 1e-6
SCALE = float(P) ** -0.5

C_Q, C_F, C_I, C_G, C_QK, C_V, C_O, C_IG, C_GA, C_GB = 0, 1024, 2048, 3072, 4096, 5120, 6144, 7168, 7176, 9224

U = 2048
RING = 2
NU_F, NU_Q, NU_I, NU_GA, NU_G, NU_QK, NU_V, NU_GB, NU_O, NU_UP, NU_OUT = 8, 8, 8, 16, 8, 8, 8, 16, 8, 16, 16
U_F = 0
U_Q = U_F + NU_F
U_I = U_Q + NU_Q
U_GA = U_I + NU_I
U_G = U_GA + NU_GA
U_QK = U_G + NU_G
U_V = U_QK + NU_QK
U_GB = U_V + NU_V
U_O = U_GB + NU_GB
U_UP = U_O + NU_O
U_OUT = U_UP + NU_UP
U_FF = U_OUT + NU_OUT
FF_UNITS = 3 * FG
FF_STEPS = FT // FG
UNITS = U_FF + FF_UNITS * FF_STEPS

N_F, N_Q, N_GA, N_G, N_QK, N_GB, N_O = 0, 8, 16, 32, 40, 48, 64

PB = 0
PB_GATES = 56
PLB = 88
PHG = 104
PML = 112
PCB = 120
PCW = 128
PFB = 160
PFW0 = 204
PFW1 = 256


def build(nc, x, norm_mix_pre, norm_mix_post, norm_ffn_pre, norm_ffn_post, w_in, b_in, hg_lb_logits, hg_norm,
          ml_conv_w, ml_conv_b, ml_norm, w_up_a, w_up_b, w_out, ffn_w_gate, ffn_w_up, ffn_conv_w, ffn_conv_b,
          ffn_w_down, out):
    x_d = x.rearrange("b t d -> (b t) d")
    out_d = out.rearrange("b t d -> (b t) d")

    def ktiles(w):
        return w.rearrange("l (j p) n -> p (l j) n", p=P)

    w_in_d, w_out_d, w_gate_d, w_up_d, w_down_d = map(ktiles, (w_in, w_out, ffn_w_gate, ffn_w_up, ffn_w_down))
    up_a_d, up_b_d = ktiles(w_up_a), ktiles(w_up_b)

    def row_on_all(v, a, n):
        return v[0:1, a:a + n].broadcast_to([P, n])

    gates_d = nc.dram_tensor("merge_gates", (2, KT, P, T), F32).ap()

    with ExitStack() as ctx:
        def sb(name, shape, dt=F32):
            return ctx.enter_context(nc.sbuf_tensor(name, shape, dt))

        def sem(name):
            return ctx.enter_context(nc.semaphore(name))

        h_hi = sb("h_hi", [P, KT, T], F32R)
        h_lo = sb("h_lo", [P, KT, T], F32R)
        raw = sb("raw", [P, RING, U])
        w_hi = sb("w_hi", [P, RING, U], F32R)
        w_lo = sb("w_lo", [P, RING, U], F32R)
        prm = sb("prm", [P, 384])
        ident = sb("ident", [P, P])
        small = sb("small", [P, 260])
        KB = 256
        ARENA = 92 * KB + KB // 2
        with nc.sbuf_tensor("arena", [P, ARENA], F32) as t:
            arena = t
        with ExitStack() as over:
            def at(name, kb, dt=F32R):
                return over.enter_context(nc.sbuf_tensor(name, [P, kb * KB], dt))
            yb_hi, ya_hi, ya_lo, _, yb_lo = (at(n, 16) for n in ("yb_hi", "ya_hi", "ya_lo", "gap1", "yb_lo"))
        with ExitStack() as over:
            def at(name, kb, dt=F32R):
                return over.enter_context(nc.sbuf_tensor(name, [P, kb * KB], dt))
            at("gap2", 64)
            act_hi, act_lo = at("act_hi", 8), at("act_lo", 8)
        ctx.enter_context(nc.sbuf_tensor("arena_keep", [P, ARENA], F32))

        act_hi_flat, act_lo_flat = act_hi, act_lo

        def tiles(t):
            return t[:, :].rearrange("p (j t) -> p j t", t=T)
        ya_hi, ya_lo, yb_hi, yb_lo, act_hi, act_lo = map(tiles, (ya_hi, ya_lo, yb_hi, yb_lo, act_hi, act_lo))

        def ar(kb, n):
            a = int(kb * KB)
            return arena[:, a:a + n]

        def f32(r):
            return r.bitcast(F32)

        n_x = ar(0, 2 * D).rearrange("p (s d) -> p s d", s=2)
        n_gain = ar(16, D)
        n_xn = ar(24, 2 * D).rearrange("p (s d) -> p s d", s=2)
        n_junk = ar(40, D)
        prow = ar(48, 3 * P).rearrange("p (s c) -> p s c", s=3)
        wg_raw = ar(56, KT * 8).rearrange("p (j n) -> p j n", n=8)
        wg_hi, wg_lo = (t[:, 0:KT * 8].rearrange("p (j n) -> p j n", n=8) for t in (act_hi_flat, act_lo_flat))
        q_all = ar(0, HG_H * T).rearrange("p (h t) -> p h t", h=HG_H)
        f_all = ar(16, HG_H * T).rearrange("p (h t) -> p h t", h=HG_H)
        v_hg = ar(32, TT * HG_W).rearrange("p (n c) -> p n c", n=TT)
        W8 = HG_H * P
        hg_b, hg_on, hg_e1, hg_e2, hg_e3, hg_at, hg_ke0, hg_ke1, hg_sa, hg_sb = (
            ar(48 + 4 * i, W8) for i in range(10))
        hg_mask = ar(88, T)
        gate_a = ar(90, T)
        vbias_hg = hg_at

        def heads(t, h=HG_H):
            return t.rearrange("p (h c) -> p h c", h=h)
        qk_all = ar(48, 8 * T).rearrange("p (m t) -> p m t", m=8)
        v_ml = ar(64, TT * ML_W).rearrange("p (n c) -> p n c", n=TT)
        row_m, row_r2, row_b, row_a, row_w, row_r3, row_t = (arena[0:ML_H, i * T:(i + 1) * T] for i in range(7))
        ml_k, ml_q, ml_d, ml_kw0, ml_kw1 = (ar(4 + 2 * i, T) for i in range(5))
        ml_sq = ar(4, ML_W)
        ml_ca, ml_cb, ml_h = (ar(80 + 4 * i, ML_W) for i in range(3))
        mask_row = arena[0:ML_H, 14 * KB:14 * KB + T]
        vbias_ml = ml_h
        qk_pre = ar(80, T + 3)
        qk_conv = ar(83, T)
        g_act = ar(80, 2 * T).rearrange("p (s t) -> p s t", s=2)
        g_y = ar(84, T)
        gate_b = ar(14, T)
        m_gates = ar(48, 8 * T).rearrange("p (s g d t) -> p s g d t", s=2, g=2, d=2)
        m_a = ar(80, T)
        m_b = ar(82, T)
        m_sum = ar(84, 2 * T).rearrange("p (s t) -> p s t", s=2)
        x1 = ar(0, TT * D).rearrange("p (n d) -> p n d", n=TT)
        acc = ar(32, TT * D).rearrange("p (n d) -> p n d", n=TT)
        x_again = (ar(64, D), ar(80, D))
        g_post = ar(72, D)
        g_pre2 = ar(32, D)
        xn2 = ar(40, 2 * D).rearrange("p (s d) -> p s d", s=2)
        junk2 = ar(56, D)
        ff_pad = ar(80, 2 * (T + 2)).rearrange("p (s t) -> p s t", s=2)
        ff_c = ar(84.5, T)
        ff_v = ar(86.5, T)
        z_gain = ar(64, D)
        z_junk = ar(80, D)

        lb = small[:, 0:8]
        omlb = small[:, 8:16]
        lb_t = small[:, 16:40]
        G = small[:, 40:72].rearrange("p (n c) -> p n c", n=TT)
        gbias = small[:, 72:80]
        gl = small[:, 80:128].rearrange("p (k n c) -> p k n c", k=3, n=TT)
        cols = small[:, 128:176].rearrange("p (n k c) -> p n k c", n=TT, k=3)
        ss = small[:, 176:192]
        ms = small[:, 192:200]
        rstd = small[:, 200:208]
        neg_half = small[:, 208:216]
        dec = small[:, 216:232].rearrange("p (h c) -> p h c", c=2)
        den = small[:, 232:240]
        ones_col = small[:, 240:242]
        nstate = small[:, 242:250]
        mlm = small[:, 250:260]
        m_prev = sb("m_prev", [ML_H, 9])

        ps = ctx.enter_context(nc.psum_tensor("ps", [P, 8, 512], F32))

        def bank2(b, h):
            return ps[:, b:b + 2, :].rearrange("p b c -> p (b c)").rearrange("p (h c) -> p h c", h=h)
        hT_, hA_, hO_ = bank2(0, HG_H), bank2(2, HG_H), bank2(4, HG_H)
        mX, mN = bank2(0, ML_H), bank2(4, ML_H)
        mKQ = ps[:, 0, :].rearrange("p (h c) -> p h c", h=ML_H)
        mKT = ps[:, 1, :].rearrange("p (h c) -> p h c", h=ML_H)
        mM = ps[:, 2, :].rearrange("p (h c) -> p h c", h=ML_H)
        mR = ps[:, 3, :].rearrange("p (h c) -> p h c", h=ML_H)
        mOT = bank2(0, 8)

        raw_loaded = [sem(f"raw_loaded{s}") for s in range(RING)]
        hi_ready = sem("hi_ready")
        lo_ready = sem("lo_ready")
        unit_done = sem("unit_done")
        cm_evac = sem("cm_evac")
        x_loaded = [sem(f"x_loaded{s}") for s in range(2)]
        gain_loaded = sem("gain_loaded")
        prm_loaded = sem("prm_loaded")
        prm_turned = sem("prm_turned")
        prm_ready = sem("prm_ready")
        consts = sem("consts")
        consts_v = sem("consts_v")
        sq_done = sem("sq_done")
        ms_ready = sem("ms_ready")
        rstd_ready = sem("rstd_ready")
        xn_ready = sem("xn_ready")
        turned = sem("turned")
        h_hi_ready = sem("h_hi_ready")
        h_lo_ready = sem("h_lo_ready")
        vg_loaded = sem("vg_loaded")
        gates_done = sem("gates_done")
        vchain = sem("vchain")
        achain = sem("achain")
        tok_done = sem("tok_done")
        tok_evac = sem("tok_evac")
        vb_loaded = sem("vb_loaded")
        f_sig = sem("f_sig")
        f_ready = sem("f_ready")
        q_ready = sem("q_ready")
        v_row, v_conv, b_den, v_merge = (sem(n) for n in ("v_row", "v_conv", "b_den", "v_merge"))
        a_ln, v_scan, v_d3, a_exp, v_prep = (sem(n) for n in ("a_ln", "v_scan", "v_d3", "a_exp", "v_prep"))
        p_att, a_at, g_sel, a_ke = (sem(n) for n in ("p_att", "a_at", "g_sel", "a_ke"))
        p_u0, p_o0, v_sb, p_u1, p_o1, v_sa = (sem(n) for n in ("p_u0", "p_o0", "v_sb", "p_u1", "p_o1", "v_sa"))
        a_o, g_sq, v_ms, g_r, v_on, p_ot, a_ot = (sem(n) for n in ("a_o", "g_sq", "v_ms", "g_r", "v_on", "p_ot", "a_ot"))
        gate_act = sem("gate_act")
        gate_stored = sem("gate_stored")
        y_mul, y_hi, y_lo = sem("y_mul"), sem("y_hi"), sem("y_lo")
        qk_evac, qk_conv_s, qk_ready = sem("qk_evac"), sem("qk_conv"), sem("qk_ready")
        r_in, r_rows, r_e, r_cols, r_cols_sb, r_act = (sem(n) for n in ("r_in", "r_rows", "r_e", "r_cols", "r_cols_sb", "r_act"))
        b_kst, b_p1, b_d, b_dx, b_dm, b_sc, b_q, b_kw = (sem(n) for n in ("b_kst", "b_p1", "b_d", "b_dx", "b_dm", "b_sc", "b_q", "b_kw"))
        b_n0, b_cb, b_n1, b_ca = (sem(n) for n in ("b_n0", "b_cb", "b_n1", "b_ca"))
        b_h, b_sq, b_ms, b_r, b_hn, b_ot, b_otc = (sem(n) for n in ("b_h", "b_sq", "b_ms", "b_r", "b_hn", "b_ot", "b_otc"))
        mg_loaded = [sem(f"mg_loaded{s}") for s in range(2)]
        mg_used = sem("mg_used")
        up_evac = sem("up_evac")
        m_ready, m_hi, m_lo = sem("m_ready"), sem("m_hi"), sem("m_lo")
        o_tok_done = sem("o_tok_done")
        o_evac = sem("o_evac")
        o_sq = sem("o_sq")
        x2_loaded = [sem(f"x2_loaded{s}") for s in range(2)]
        wg_loaded, wg_split, mem_zero, lb_done, v_dec, v_red = (sem(n) for n in ("wg_loaded", "wg_split", "mem_zero", "lb_done", "v_dec", "v_red"))
        r_ms, r_pow, r_x1, r_x1v, r_sq2, r_ms2, r_pow2 = (sem(n) for n in ("r_ms", "r_pow", "r_x1", "r_x1v", "r_sq2", "r_ms2", "r_pow2"))
        gp_loaded = sem("gp_loaded")
        ff_gate = sem("ff_gate")
        ff_conv = sem("ff_conv")
        ff_gelu = sem("ff_gelu")
        ff_mul = sem("ff_mul")
        ff_hi = sem("ff_hi")
        ff_lo = sem("ff_lo")
        ff_chain = sem("ff_chain")
        dn_done = sem("dn_done")
        dn_evac = sem("dn_evac")
        gf_loaded = sem("gf_loaded")
        z_sq, z_ms, z_r, z_y, z_o, z_st = (sem(n) for n in ("z_sq", "z_ms", "z_r", "z_y", "z_o", "z_st"))
        z_free = sem("z_free")

        block = ctx.enter_context(nc.Block())

        @block.sync
        def _(sp):
            def load(u, s, src):
                sp.wait_ge(lo_ready, u + 1)
                j, n = src.shape[1], src.shape[2]
                sp.dma_start(raw[:, s, :].rearrange("p (j n) -> p j n", j=j), src).then_inc(raw_loaded[s], 16)
                assert j * n == U

            def columns(first, units, w, c0, width=P):
                with sp.Fori(0, units // 2) as i:
                    for s in range(2):
                        load(first + 2 * i + s, s, w[:, :, ds(c0 + width * (2 * i + s), width)])

            def blocks(first, n, w, c0):
                with sp.Fori(0, n) as i:
                    for q in range(4):
                        load(first + 4 * i + q, q % 2, w[:, 4 * q:4 * q + 4, ds(c0 + 512 * i, 512)])

            with sp.Fori(0, 2) as i:
                for s in range(2):
                    sp.wait_ge(xn_ready, 2 * i + s + 1)
                    sp.dma_start(n_x[:, s, :], x_d[ds((2 * i + s) * P, P), :]).then_inc(x_loaded[s], 16)
            columns(U_F, NU_F, w_in_d, C_F)
            columns(U_Q, NU_Q, w_in_d, C_Q)
            blocks(U_I, 2, w_in_d, C_I)
            columns(U_GA, NU_GA, w_in_d, C_GA)
            columns(U_G, NU_G, w_in_d, C_G)
            columns(U_QK, NU_QK, w_in_d, C_QK)
            blocks(U_V, 2, w_in_d, C_V)
            columns(U_GB, NU_GB, w_in_d, C_GB)
            columns(U_O, NU_O, w_in_d, C_O)
            with sp.Fori(0, 8) as i:
                load(U_UP + 2 * i, 0, up_a_d[:, :, ds(256 * i, 256)])
                load(U_UP + 2 * i + 1, 1, up_b_d[:, :, ds(256 * i, 256)])
            blocks(U_OUT, 4, w_out_d, 0)
            with sp.Fori(0, FF_STEPS) as i:
                for f in range(FG):
                    load(U_FF + FF_UNITS * i + 2 * f, 0, w_gate_d[:, :, ds((FG * i + f) * P, P)])
                    load(U_FF + FF_UNITS * i + 2 * f + 1, 1, w_up_d[:, :, ds((FG * i + f) * P, P)])
                for d in range(4):
                    load(U_FF + FF_UNITS * i + 2 * FG + d, d % 2, w_down_d[:, ds(FG * i, FG), 512 * d:512 * d + 512])

        @block.tensor
        def _(pe):
            pe.sem_inc(unit_done, RING)
            pe.sem_inc(turned, 8)
            for credit in (p_att, p_o1, b_p1):
                pe.sem_inc(credit, 1)

            def split_ready(u, part):
                if part == 0:
                    pe.wait_ge(hi_ready, u + 1)
                else:
                    pe.wait_ge(lo_ready, u + 1 + RING)

            def cm_unit(u, n, s, k_hi=h_hi, k_lo=h_lo):
                pe.wait_ge(cm_evac, n + 1)
                w = [t[:, s, :].rearrange("p (j n) -> p j n", j=KT) for t in (w_hi, w_lo)]
                split_ready(u, 0)
                for k in (k_hi, k_lo):
                    for j in range(KT):
                        pe.matmul(ps[:, 6 + s, :], w[0][:, j, :], k[:, j, :], start=(k is k_hi and j == 0), stop=False)
                split_ready(u, 1)
                for j in range(KT):
                    last = pe.matmul(ps[:, 6 + s, :], w[1][:, j, :], k_hi[:, j, :], start=False, stop=(j == KT - 1))
                last.then_inc(unit_done, 1)

            def cm_phase(first, n0, units):
                with pe.Fori(0, units // 2) as i:
                    for s in range(2):
                        cm_unit(first + 2 * i + s, n0 + 2 * i + s, s)

            def tm_products(b0, s, k_hi, k_lo, j0, nj, first, last, before, done):
                w = [t[:, s, :].rearrange("p (j n) -> p j n", j=nj) for t in (w_hi, w_lo)]
                for n in range(TT):
                    if first:
                        before(n)
                    for j in range(nj):
                        tok = slice(n * P, n * P + P)
                        pe.matmul(ps[:, b0 + n, :], k_hi[:, j0 + j, tok], w[0][:, j, :], start=(first and j == 0), stop=False)
                        pe.matmul(ps[:, b0 + n, :], k_hi[:, j0 + j, tok], w[1][:, j, :], start=False, stop=False)
                        mm = pe.matmul(ps[:, b0 + n, :], k_lo[:, j0 + j, tok], w[0][:, j, :], start=False,
                                       stop=(last and j == nj - 1))
                    if last:
                        mm.then_inc(done if n < TT - 1 else unit_done, 1)
                if not last:
                    mm.then_inc(unit_done, 1)

            def tm_block(u0, evac, e0, done):
                for q in range(4):
                    split_ready(u0 + q, 0)
                    split_ready(u0 + q, 1)
                    tm_products(0, q % 2, h_hi, h_lo, 4 * q, 4, q == 0, q == 3,
                                lambda n: pe.wait_ge(evac, e0 + n + 1), done)

            pe.wait_ge(consts, 2)
            pe.wait_ge(prm_loaded, 16 * 11)
            pe.transpose(ps[:, 5, 0:128], prow[:, 0, :], ident[:, :])
            pe.transpose(ps[:, 5, 128:248], prow[0:120, 1, :], ident[0:120, 0:120])
            pe.transpose(ps[:, 5, 256:344], prow[0:88, 2, :], ident[0:88, 0:88]).then_inc(prm_turned, 1)

            def turn_tokens(xn, t0, base_x, base_e):
                for s in range(2):
                    pe.wait_ge(xn_ready, base_x + t0 + s + 1 + 2)
                    for g in range(4):
                        pe.wait_ge(h_lo_ready, base_e + 4 * (t0 + s) + g + 1)
                        for k in range(4):
                            mm = pe.transpose(ps[:, g, k * P:(k + 1) * P], xn[:, s, (4 * g + k) * P:(4 * g + k + 1) * P],
                                              ident[:, :])
                        mm.then_inc(turned, 1)

            with pe.Fori(0, 2) as i:
                turn_tokens(n_xn, 2 * i, 0, 0)
            pe.wait_ge(h_lo_ready, 4 + 16)

            wg = (wg_hi, wg_lo)
            pe.wait_ge(wg_split, 1)
            for n in range(TT):
                tok = slice(n * P, n * P + P)
                for j in range(KT):
                    for a, b in ((h_hi, 0), (h_hi, 1), (h_lo, 0)):
                        mm = pe.matmul(ps[:, 4, 8 * n:8 * n + 8], a[:, j, tok], wg[b][:, j, :],
                                       start=(n == 0 and j == 0 and a is h_hi and b == 0), stop=(j == KT - 1 and a is h_lo),
                                       skip_group_check=True)
            mm.then_inc(gates_done, 1)

            cm_phase(U_F, N_F, NU_F)
            cm_phase(U_Q, N_Q, NU_Q)
            with pe.Fori(0, 2) as i:
                tm_block(U_I + 4 * i, tok_evac, 4 * i, tok_done)

            pe.wait_ge(tok_evac, 4 + 8)
            qd, ki, ke = heads(hg_e1), heads(hg_e2), heads(hg_e3)
            at_, ke0, ke1, sa, sb_, on = map(heads, (hg_at, hg_ke0, hg_ke1, hg_sa, hg_sb, hg_on))
            with pe.Fori(0, TT) as i:
                def unit(s):
                    cm_unit(U_GA + 4 * i + s, N_GA + 4 * i + s, s % 2)
                pe.wait_ge(v_prep, i + 1)
                pe.wait_ge(a_ot, i + 1)
                for h in range(HG_H):
                    pe.transpose(hT_[:, h, :], ke[:, h, :], ident[:, :])
                pe.wait_ge(v_sa, i + 1)
                for h in range(HG_H):
                    mm = pe.matmul(hA_[:, h, :], ki[:, h, :], qd[:, h, :], start=True, stop=True)
                mm.then_inc(p_att, 1)
                unit(0)
                pe.wait_ge(a_ke, 2 * i + 2)
                for h in range(HG_H):
                    mm = pe.matmul(hT_[:, h, :], ke0[:, h, :], v_hg[:, ds(i, 1), h * P:(h + 1) * P], start=True, stop=True)
                mm.then_inc(p_u0, 1)
                pe.wait_ge(g_sel, i + 1)
                pe.wait_ge(a_o, i + 1)
                for h in range(HG_H):
                    pe.matmul(hO_[:, h, :], at_[:, h, :], v_hg[:, ds(i, 1), h * P:(h + 1) * P],
                              start=(h % 4 == 0), stop=False, skip_group_check=True)
                for h in range(HG_H):
                    mm = pe.matmul(hO_[0:CHUNK, h, :], qd[:, h, 0:CHUNK], sa[:, h, :], start=False, stop=False,
                                   skip_group_check=True)
                mm.then_inc(p_o0, 1)
                for h in range(HG_H):
                    mm = pe.matmul(hA_[:, h, :], ke1[:, h, :], v_hg[:, ds(i, 1), h * P:(h + 1) * P], start=True, stop=True)
                mm.then_inc(p_u1, 1)
                unit(1)
                pe.wait_ge(v_sb, i + 1)
                for h in range(HG_H):
                    mm = pe.matmul(hO_[CHUNK:P, h, :], qd[:, h, CHUNK:P], sb_[:, h, :], start=False, stop=True,
                                   skip_group_check=True)
                mm.then_inc(p_o1, 1)
                unit(2)
                unit(3)
                pe.wait_ge(v_on, i + 1)
                for h in range(HG_H):
                    mm = pe.transpose(hT_[:, h, :], on[:, h, :], ident[:, :])
                mm.then_inc(p_ot, 1)

            cm_phase(U_G, N_G, NU_G)
            pe.wait_ge(r_in, 1)
            pe.wait_ge(a_ot, TT + 1)
            for k in range(2):
                for n in range(TT):
                    mm = pe.transpose(ps[0:ML_H, k, n * P:(n + 1) * P], gl[:, k, n, :], ident[:, :])
            mm.then_inc(r_rows, 1)
            cm_phase(U_QK, N_QK, NU_QK)
            pe.wait_ge(r_e, 1)
            for n in range(TT):
                for k, row in enumerate((row_a, row_w, row_r3)):
                    mm = pe.transpose(ps[:, 4, 12 * n + 4 * k:12 * n + 4 * k + 4], row[:, n * P:(n + 1) * P],
                                      ident[0:ML_H, 0:ML_H])
            mm.then_inc(r_cols, 1)
            with pe.Fori(0, 2) as i:
                tm_block(U_V + 4 * i, tok_evac, 8 + 4 * i, tok_done)
            pe.wait_ge(tok_evac, 4 + 16)

            kst, qst, sc, kw0, kw1 = (heads(t, ML_H) for t in (ml_k, ml_q, ml_d, ml_kw0, ml_kw1))
            ca, cb, hm = (heads(t, ML_H) for t in (ml_ca, ml_cb, ml_h))
            hm8 = heads(ml_h, 8)
            DEN, UN0, UN1 = (lambda h: slice(h, h + 1)), (lambda h: slice(4 + h, 5 + h)), (lambda h: slice(8 + h, 9 + h))
            with pe.Fori(0, TT) as i:
                def unit(s):
                    cm_unit(U_GB + 4 * i + s, N_GB + 4 * i + s, s % 2)
                pe.wait_ge(b_kst, i + 1)
                pe.wait_ge(b_otc, i + 1)
                for h in range(ML_H):
                    pe.matmul(mKQ[:, h, :], kst[:, h, :], qk_all[:, h, ds(i * P, P)], start=True, stop=True)
                for h in range(ML_H):
                    pe.transpose(mKT[:, h, :], kst[:, h, :], ident[:, :])
                pe.wait_ge(b_ca, i + 1)
                for h in range(ML_H):
                    pe.matmul(mM[:, h, :], ident[0:ML_H, h:h + 1].broadcast_to([ML_H, P]), row_m[:, ds(i * P, P)], start=True, stop=True)
                for h in range(ML_H):
                    mm = pe.matmul(mR[:, h, :], ident[0:ML_H, h:h + 1].broadcast_to([ML_H, P]), row_r2[:, ds(i * P, P)], start=True, stop=True)
                mm.then_inc(b_p1, 1)
                unit(0)
                pe.wait_ge(b_kw, i + 1)
                pe.wait_ge(b_sc, i + 1)
                pe.wait_ge(b_q, i + 1)
                for h in range(ML_H):
                    pe.matmul(mX[:, h, :], kw0[:, h, :], v_ml[:, ds(i, 1), h * ML_V:(h + 1) * ML_V], start=True, stop=True)
                pe.wait_ge(b_h, i + 1)
                for h in range(ML_H):
                    pe.matmul(mN[:, h, :], sc[:, h, :], v_ml[:, ds(i, 1), h * ML_V:(h + 1) * ML_V],
                              start=(h % 2 == 0), stop=False, skip_group_check=True)
                    pe.matmul(ps[:, 3, DEN(h)], sc[:, h, :], ones_col[:, 0:1], start=(h == 0), stop=False,
                              skip_group_check=True)
                for h in range(ML_H):
                    pe.matmul(ps[:, 3, UN0(h)], kw0[:, h, :], ones_col[:, 0:1], start=False, stop=False,
                              skip_group_check=True)
                for h in range(ML_H):
                    pe.matmul(mN[0:CHUNK, h, :], qst[:, h, 0:CHUNK], ca[:, h, :], start=False, stop=False,
                              skip_group_check=True)
                    mm = pe.matmul(ps[0:CHUNK, 3, DEN(h)], qst[:, h, 0:CHUNK], nstate[:, h:h + 1], start=False,
                                   stop=False, skip_group_check=True)
                mm.then_inc(b_n0, 1)
                unit(1)
                pe.wait_ge(b_cb, i + 1)
                for h in range(ML_H):
                    pe.matmul(mX[:, h, :], kw1[:, h, :], v_ml[:, ds(i, 1), h * ML_V:(h + 1) * ML_V], start=True, stop=True)
                    pe.matmul(ps[:, 3, UN1(h)], kw1[:, h, :], ones_col[:, 0:1], start=False, stop=False,
                              skip_group_check=True)
                for h in range(ML_H):
                    pe.matmul(mN[CHUNK:P, h, :], qst[:, h, CHUNK:P], cb[:, h, :], start=False, stop=True,
                              skip_group_check=True)
                    mm = pe.matmul(ps[CHUNK:P, 3, DEN(h)], qst[:, h, CHUNK:P], nstate[:, 4 + h:5 + h], start=False,
                                   stop=True, skip_group_check=True)
                mm.then_inc(b_n1, 1)
                unit(2)
                unit(3)
                pe.wait_ge(b_hn, i + 1)
                for h in range(8):
                    mm = pe.transpose(mOT[:, 4 * (h % 2) + h // 2, :], hm8[:, h, :], ident[:, :])
                mm.then_inc(b_ot, 1)

            cm_phase(U_O, N_O, NU_O)

            pe.wait_ge(b_otc, TT + 1)
            pe.wait_ge(cm_evac, N_O + NU_O + 2)
            pe.wait_ge(y_lo, 1 + 16)
            with pe.Fori(0, 4) as i:
                for h in range(2):
                    pe.wait_ge(up_evac, 2 * i + h + 1)
                    for s, (y_h, y_l) in enumerate(((ya_hi, ya_lo), (yb_hi, yb_lo))):
                        u = U_UP + 4 * i + 2 * h + s
                        split_ready(u, 0)
                        split_ready(u, 1)
                        w = [t[:, s, :].rearrange("p (j n) -> p j n", j=8) for t in (w_hi, w_lo)]
                        for d in range(2):
                            for a, (wk, yk) in enumerate(((0, y_h), (0, y_l), (1, y_h))):
                                for j in range(8):
                                    mm = pe.matmul(ps[:, 4 * h + 2 * s + d, :], w[wk][:, j, d * P:(d + 1) * P], yk[:, j, :],
                                                   start=(a == 0 and j == 0), stop=(a == 2 and j == 7))
                        mm.then_inc(unit_done, 1)

            pe.wait_ge(up_evac, 2 + 8)
            pe.wait_ge(m_lo, 1 + KT)
            with pe.Fori(0, 4) as i:
                tm_block(U_OUT + 4 * i, o_evac, 4 * i, o_tok_done)

            pe.wait_ge(o_evac, 4 + 16)
            with pe.Fori(0, 2) as i:
                turn_tokens(xn2, 2 * i, TT, 16)
            pe.wait_ge(h_lo_ready, 4 + 32)

            def mlp_step(i):
                u0 = U_FF + FF_UNITS * i
                for f in range(FG):
                    bank = (4, 6, 0, 2)[f]
                    pe.wait_ge(dn_evac, 16 * i + (12, 12, 16, 16)[f])
                    for s in range(2):
                        w = [t[:, s, :].rearrange("p (j n) -> p j n", j=KT) for t in (w_hi, w_lo)]
                        split_ready(u0 + 2 * f + s, 0)
                        for k in (h_hi, h_lo):
                            for j in range(KT):
                                pe.matmul(ps[:, bank + s, :], w[0][:, j, :], k[:, j, :], start=(k is h_hi and j == 0), stop=False)
                        split_ready(u0 + 2 * f + s, 1)
                        for j in range(KT):
                            mm = pe.matmul(ps[:, bank + s, :], w[1][:, j, :], h_hi[:, j, :], start=False, stop=(j == KT - 1))
                        mm.then_inc(unit_done, 1)
                for d in range(4):
                    u = u0 + 2 * FG + d
                    split_ready(u, 0)
                    split_ready(u, 1)
                    b0 = 4 if d % 2 == 0 else 0
                    w = [t[:, d % 2, :].rearrange("p (j n) -> p j n", j=FG) for t in (w_hi, w_lo)]
                    if d == 0:
                        pe.wait_ge(ff_mul, FG * i + 2)
                        for j in range(FG):
                            pe.wait_ge(ff_lo, FG * i + j + 1)
                            for n in range(TT):
                                tok = slice(n * P, n * P + P)
                                pe.matmul(ps[:, b0 + n, :], act_hi[:, j, tok], w[0][:, j, :], start=(j == 0), stop=False)
                                pe.matmul(ps[:, b0 + n, :], act_hi[:, j, tok], w[1][:, j, :], start=False, stop=False)
                                mm = pe.matmul(ps[:, b0 + n, :], act_lo[:, j, tok], w[0][:, j, :], start=False, stop=(j == FG - 1))
                                if j == FG - 1:
                                    mm.then_inc(dn_done if n < TT - 1 else unit_done, 1)
                    else:
                        tm_products(b0, d % 2, act_hi, act_lo, 0, FG, True, True,
                                    lambda n: pe.wait_ge(dn_evac, 16 * (i + 1) + 4 * (d - 2) + n + 1) if d >= 2 else None, dn_done)

            with pe.Fori(0, FF_STEPS - 1) as i:
                mlp_step(i)
            mlp_step(FF_STEPS - 1)

        def units_of(first, per):
            return lambda i, k: (first + per * i + k, first // 2 + (per // 2) * i + k // 2, k % 2)

        @block.scalar
        def _(act):
            for s_, n in ((cm_evac, 2), (a_o, 1), (a_ot, 1), (b_otc, 1), (o_evac, 4)):
                act.sem_inc(s_, n)
            act.sem_inc(gate_stored, 16)

            def split_hi(u, rnd, s):
                act.wait_ge(raw_loaded[s], 16 * rnd + 16)
                act.wait_ge(unit_done, u + 1)
                act.copy(w_hi[:, s, :], raw[:, s, :]).then_inc(hi_ready, 1)

            act.wait_ge(prm_ready, 2)
            act.activation(lb_t[:, 8:24], lb_t[:, 8:24], ACT.Exp).then_inc(achain, 1)

            def turned_hi(i, base):
                for s in range(2):
                    for g in range(4):
                        act.wait_ge(turned, 8 + 4 * (2 * i + s + base) + g + 1)
                        act.copy(h_hi[:, 4 * g:4 * g + 4, ds((2 * i + s) * P, P)],
                                 ps[:, g, :].rearrange("p (k t) -> p k t", k=4)).then_inc(h_hi_ready, 1)

            with act.Fori(0, 2) as i:
                for s in range(2):
                    act.wait_ge(x_loaded[s], 16 * i + 16)
                    act.wait_ge(ms_ready, 2 * i + s + 1)
                    act.activation(n_junk, n_x[:, s, :], ACT.Square, accum_out=ss[:, 0:1]).then_inc(sq_done, 1)
                turned_hi(i, 0)
            act.wait_ge(wg_loaded, 16)
            act.copy(wg_hi, wg_raw).then_inc(achain, 1)
            split_hi(0, 0, 0)

            def columns(first, units, evac):
                un = units_of(first, 2)
                with act.Fori(0, units // 2) as i:
                    for s in range(2):
                        split_hi(*un(i, s + 1))
                        act.wait_ge(unit_done, first + 2 * i + s + 1 + RING)
                        evac(2 * i + s, ps[:, 6 + s, :], s)

            def blocks(first, n):
                un = units_of(first, 4)
                with act.Fori(0, n) as i:
                    for q in range(4):
                        split_hi(*un(i, q + 1))

            def into(dst, func, col):
                def evac(m, bank, s):
                    act.activation(dst[:, ds(m, 1), :], bank, func, bias=prm[:, ds(col + m, 1)]).then_inc(cm_evac, 1)
                return evac

            columns(U_F, NU_F, into(f_all, ACT.Sigmoid, 8))
            columns(U_Q, NU_Q, into(q_all, ACT.Silu, 0))
            blocks(U_I, 2)

            def hg_prep(i):
                act.wait_ge(p_att, i + 1)
                act.wait_ge(v_ms, i + 1)
                act.activation(heads(hg_e3), f_all[:, :, ds(i * P, P)], ACT.Ln).then_inc(a_ln, 1)
                act.wait_ge(v_scan, i + 1)
                act.wait_ge(p_o1, i + 1)
                act.activation(hg_e1, hg_b, ACT.Exp).then_inc(a_exp, 1)
                act.activation(hg_e2, hg_b, ACT.Exp, scale=-1.0).then_inc(a_exp, 1)
                act.wait_ge(v_d3, i + 1)
                act.activation(hg_e3, hg_e3, ACT.Exp).then_inc(a_exp, 1)

            def gate_unit(i, k, u0, n0, tmp, which):
                m = 4 * i + k
                act.wait_ge(unit_done, u0 + m + 1 + RING)
                act.wait_ge(gate_stored, 16 * (KT * which + m) + 16)
                act.activation(tmp, ps[:, 6 + k % 2, :], ACT.Sigmoid,
                               bias=prm[:, ds(PB_GATES + KT * which + m, 1)]).then_inc(cm_evac, 1)
                act.wait_ge(cm_evac, n0 + m + 3)
                act.dma_start(gates_d[which, ds(m, 1), :, :].rearrange("a p t -> p (a t)"), tmp).then_inc(gate_stored, 16)

            act.wait_ge(f_ready, NU_F)
            hg_prep(0)
            un_ga = units_of(U_GA, 4)

            def hg_step(i, last):
                split_hi(*un_ga(i, 1))
                act.wait_ge(mem_zero, 2)
                act.wait_ge(p_att, i + 2)
                for a in (0, CHUNK):
                    act.copy(heads(hg_at)[a:a + CHUNK, :, a:a + CHUNK], hA_[a:a + CHUNK, :, a:a + CHUNK]).then_inc(a_at, 1)
                for a, dst in ((0, hg_ke0), (CHUNK, hg_ke1)):
                    act.copy(heads(dst)[a:a + CHUNK, :, :], hT_[a:a + CHUNK, :, :]).then_inc(a_ke, 1)
                gate_unit(i, 0, U_GA, N_GA, gate_a, 0)
                split_hi(*un_ga(i, 2))
                gate_unit(i, 1, U_GA, N_GA, gate_a, 0)
                split_hi(*un_ga(i, 3))
                act.wait_ge(p_o1, i + 2)
                act.copy(heads(hg_on), hO_).then_inc(a_o, 1)
                gate_unit(i, 2, U_GA, N_GA, gate_a, 0)
                split_hi(*un_ga(i, 4))
                if not last:
                    hg_prep(i + 1)
                gate_unit(i, 3, U_GA, N_GA, gate_a, 0)
                act.wait_ge(p_ot, i + 1)
                act.copy(q_all[:, :, ds(i * P, P)], hT_).then_inc(a_ot, 1)

            with act.Fori(0, TT - 1) as i:
                hg_step(i, False)
            hg_step(TT - 1, True)

            def gating(func, col, y_part, n0):
                def evac(h, bank, s):
                    act.wait_ge(y_mul, n0 + h + 1)
                    act.activation(g_act[:, s, :], bank, func, bias=prm[:, ds(col + h, 1)]).then_inc(cm_evac, 1)
                    act.wait_ge(y_mul, n0 + h + 3)
                    act.copy(y_part[:, ds(h, 1), :].rearrange("p a t -> p (a t)"), g_y).then_inc(y_hi, 1)
                return evac

            columns(U_G, NU_G, gating(ACT.Silu, 24, ya_hi, 0))

            act.wait_ge(r_act, 1)
            act.activation(gl[:, 2, :, :], gl[:, 2, :, :], ACT.Exp).then_inc(achain, 1)
            act.wait_ge(achain, 3)
            act.activation(gl[:, 2, :, :], gl[:, 2, :, :], ACT.Ln, bias=1.0).then_inc(achain, 1)
            act.wait_ge(r_act, 2)
            for row, sign in ((row_r2, 1.0), (row_w, 1.0), (row_r3, -1.0)):
                act.activation(row, row, ACT.Exp, scale=sign).then_inc(r_e, 1)

            def evac_qk(m, bank, s):
                act.wait_ge(qk_conv_s, m + 1)
                act.activation(qk_pre[:, 3:3 + T], bank, ACT.Identity, bias=prm[:, ds(32 + m, 1)]).then_inc(cm_evac, 1)
                act.wait_ge(qk_conv_s, m + 2)
                act.activation(qk_all[:, ds(m, 1), :].rearrange("p a t -> p (a t)"), qk_conv, ACT.Silu).then_inc(qk_ready, 1)

            columns(U_QK, NU_QK, evac_qk)
            blocks(U_V, 2)

            def ml_prep(i):
                act.wait_ge(b_p1, i + 1)
                act.wait_ge(b_ms, i + 1)
                act.activation(heads(ml_k, ML_H), qk_all[:, ML_H:2 * ML_H, ds(i * P, P)], ACT.Copy,
                               scale=SCALE).then_inc(b_kst, 1)

            ml_prep(0)
            un_gb = units_of(U_GB, 4)

            def ml_step(i, last):
                split_hi(*un_gb(i, 1))
                act.wait_ge(b_d, i + 1)
                act.activation(ml_d, ml_d, ACT.Exp, scale=-1.0).then_inc(b_dx, 1)
                gate_unit(i, 0, U_GB, N_GB, gate_b, 1)
                split_hi(*un_gb(i, 2))
                gate_unit(i, 1, U_GB, N_GB, gate_b, 1)
                split_hi(*un_gb(i, 3))
                gate_unit(i, 2, U_GB, N_GB, gate_b, 1)
                split_hi(*un_gb(i, 4))
                if not last:
                    ml_prep(i + 1)
                gate_unit(i, 3, U_GB, N_GB, gate_b, 1)
                act.wait_ge(b_ot, i + 1)
                act.copy(qk_all[:, :, ds(i * P, P)], mOT).then_inc(b_otc, 1)

            with act.Fori(0, TT - 1) as i:
                ml_step(i, False)
            ml_step(TT - 1, True)

            act.wait_ge(gate_stored, 16 + 16 * 2 * KT)
            columns(U_O, NU_O, gating(ACT.Sigmoid, 48, yb_hi, 8))

            un_up = units_of(U_UP, 2)
            with act.Fori(0, 8) as i:
                split_hi(*un_up(i, 1))
                split_hi(*un_up(i, 2))
                for d in range(2):
                    act.wait_ge(m_ready, 2 * i + d + 1)
                    act.copy(h_hi[:, ds(2 * i + d, 1), :].rearrange("p a t -> p (a t)"), m_sum[:, d, :]).then_inc(m_hi, 1)

            un_out = units_of(U_OUT, 4)
            with act.Fori(0, 4) as i:
                for q in range(4):
                    split_hi(*un_out(i, q + 1))
                for n in range(TT):
                    if n < TT - 1:
                        act.wait_ge(o_tok_done, 3 * i + n + 1)
                    else:
                        act.wait_ge(unit_done, U_OUT + 4 * i + 4 + RING)
                    act.wait_ge(o_evac, 4 * i + n + 4)
                    act.activation(junk2[:, 0:512], ps[:, n, :], ACT.Square, accum_out=ss[:, ds(4 * n + i, 1)]).then_inc(o_sq, 1)
                    act.copy(x1[:, n, ds(512 * i, 512)], ps[:, n, :]).then_inc(o_evac, 1)

            with act.Fori(0, 2) as i:
                for s in range(2):
                    act.wait_ge(r_x1, 2 * i + s + 1)
                    act.wait_ge(ms_ready, TT + 2 * i + s + 1)
                    act.activation(junk2, x1[:, ds(2 * i + s, 1), :].rearrange("p a d -> p (a d)"), ACT.Square,
                                   accum_out=ss[:, 0:1]).then_inc(sq_done, 1)
                turned_hi(i, TT)

            un_ff = units_of(U_FF, FF_UNITS)

            def mlp_step(i, last):
                u0 = U_FF + FF_UNITS * i
                for f in range(FG):
                    bank = (4, 6, 0, 2)[f]
                    split_hi(*un_ff(i, 2 * f + 1))
                    act.wait_ge(unit_done, u0 + 2 * f + 1 + RING)
                    act.wait_ge(ff_conv, FG * i + f + 1)
                    act.copy(ff_pad[:, 0, 2:2 + T], ps[:, bank, :]).then_inc(ff_gate, 1)
                    split_hi(*un_ff(i, 2 * f + 2))
                    act.wait_ge(ff_conv, FG * i + f + 2)
                    act.activation(ff_c, ff_c, ACT.Gelu_apprx_tanh).then_inc(ff_gelu, 1)
                    act.wait_ge(ff_mul, FG * i + f + 1)
                    act.copy(act_hi[:, f, :], ff_v).then_inc(ff_hi, 1)
                for d in range(4):
                    if not (last and d == 3):
                        split_hi(*un_ff(i, 2 * FG + d + 1))

            with act.Fori(0, FF_STEPS - 1) as i:
                mlp_step(i, False)
            mlp_step(FF_STEPS - 1, True)

            for n in range(TT):
                act.wait_ge(dn_evac, 16 * FF_STEPS + 12 + n + 1)
                if n:
                    act.wait_ge(z_sq, n)
                act.activation(z_junk, acc[:, n, :], ACT.Square, accum_out=ss[:, 8 + n:9 + n]).then_inc(z_sq, 1)

        @block.gpsimd
        def _(pool):
            pool.memset(ident[:, :], 0.0).then_inc(consts, 1)
            pool.memset(neg_half, -0.5).then_inc(mem_zero, 1)
            pool.wait_ge(consts, 1)
            pool.affine_select(out=ident[:, :], in_=ident[:, :], compare_op=ALU.not_equal, fill=1.0, base=0,
                               pattern=[[-1, P]], channel_multiplier=1).then_inc(consts, 1)

            def tile_rows(v):
                return v.rearrange("l (n p) -> (l n) p", p=P)

            taps = ffn_conv_w.rearrange("l k (n p) -> (l k) n p", p=P)
            rows = [(0, PB, tile_rows(b_in[:, 0:C_IG])), (0, PB_GATES, tile_rows(b_in[:, C_GA:C_GA + 2 * D])),
                    (0, PLB, tile_rows(hg_lb_logits)), (0, PHG, tile_rows(hg_norm)), (0, PML, tile_rows(ml_norm)),
                    (0, PCB, tile_rows(ml_conv_b)), (1, PCW - 128, ml_conv_w.rearrange("l k (n p) -> (l k n) p", p=P)),
                    (1, PFB - 128, tile_rows(ffn_conv_b)), (1, PFW0 - 128, taps[0, :, :]), (2, 0, taps[1, :, :]),
                    (2, FT, taps[2, :, :])]
            for t, r0, src in rows:
                pool.dma_start(prow[r0:r0 + src.shape[0], t, :], src).then_inc(prm_loaded, 16)
            pool.dma_start(n_gain, row_on_all(norm_mix_pre, 0, D)).then_inc(gain_loaded, 16)
            with nc.allow_non_contiguous_dma(reason="8 columns of the gates"):
                pool.dma_start(wg_raw, w_in_d[:, :, C_IG:C_IG + 8]).then_inc(wg_loaded, 16)
            pool.dma_start(gbias, row_on_all(b_in, C_IG, 8)).then_inc(vg_loaded, 16)

            def power(n, a=0):
                return pool.tensor_tensor(rstd[:, a:a + n], ms[:, a:a + n], neg_half[:, 0:n], ALU.pow)

            pool.wait_ge(mem_zero, 1)
            with pool.Fori(0, 2) as i:
                for s in range(2):
                    pool.wait_ge(ms_ready, 2 * i + s + 2)
                    pool.wait_ge(xn_ready, 2 * i + s + 2)
                    power(1).then_inc(rstd_ready, 1)

            pool.wait_ge(gates_done, 1)
            pool.memset(hg_ke0, 0.0)
            pool.memset(hg_ke1, 0.0)
            pool.memset(hg_mask, 1.0).then_inc(consts_v, 1)
            pool.wait_ge(consts_v, 1)
            pool.memset(hg_mask.rearrange("p (c k) -> p c k", k=CHUNK)[:, :, 0:1], 0.0).then_inc(consts_v, 1)
            pool.dma_start(hg_at, row_on_all(b_in, C_I, HG_W)).then_inc(vb_loaded, 16)
            pool.wait_ge(tok_evac, 4 + 8)
            pool.memset(hg_at, 0.0).then_inc(mem_zero, 1)

            for i in range(TT):
                pool.wait_ge(a_at, 2 * i + 2)
                pool.affine_select(out=heads(hg_at), in_=heads(hg_at), compare_op=ALU.is_ge, fill=0.0, base=0,
                                   pattern=[[0, HG_H], [1, P]], channel_multiplier=-1).then_inc(g_sel, 1)
                pool.wait_ge(a_o, i + 2)
                pool.tensor_tensor(hg_e3, hg_on, hg_on, ALU.mult).then_inc(g_sq, 1)
                pool.wait_ge(v_ms, i + 2)
                power(8).then_inc(g_r, 1)

            pool.wait_ge(y_lo, 1 + 8)
            pool.wait_ge(gate_stored, 16 + 16 * KT)
            pool.dma_start(vbias_ml, row_on_all(b_in, C_V, ML_W)).then_inc(vb_loaded, 16)

            for i in range(TT):
                pool.wait_ge(b_dx, i + 1)
                pool.affine_select(out=heads(ml_d, ML_H), in_=heads(ml_d, ML_H), compare_op=ALU.is_ge, fill=0.0, base=0,
                                   pattern=[[0, ML_H], [1, P]], channel_multiplier=-1).then_inc(b_dm, 1)
                pool.wait_ge(b_dm, 2 * i + 1)
                pool.memset(heads(ml_d, ML_H)[0:CHUNK, :, CHUNK:P], 0.0).then_inc(b_dm, 1)
                pool.wait_ge(b_h, i + 2)
                pool.tensor_tensor(ml_sq, ml_h, ml_h, ALU.mult).then_inc(b_sq, 1)
                pool.wait_ge(b_ms, i + 2)
                power(4).then_inc(b_r, 1)

            pool.wait_ge(gate_stored, 16 + 16 * 2 * KT)
            pool.wait_ge(y_lo, 1 + 16)
            with pool.Fori(0, 4) as i:
                for s in range(2):
                    pool.wait_ge(mg_used, 2 * i + s + 1)
                    for g in range(2):
                        pool.dma_start(m_gates[:, s, g, :, :], gates_d[g, ds(2 * (2 * i + s), 2), :, :]
                                       .rearrange("d p t -> p d t")).then_inc(mg_loaded[s], 16)
            pool.wait_ge(mg_used, 2 + 8)
            pool.wait_ge(m_lo, 1 + KT)
            pool.dma_start(g_post, row_on_all(norm_mix_post, 0, D)).then_inc(gp_loaded, 16)
            pool.dma_start(g_pre2, row_on_all(norm_ffn_pre, 0, D)).then_inc(gp_loaded, 16)
            for s in range(2):
                pool.dma_start(x_again[s], x_d[s * P:(s + 1) * P, :]).then_inc(x2_loaded[s], 16)
            pool.wait_ge(r_ms, 1)
            power(4).then_inc(r_pow, 1)

            def x1_step(i):
                for s in range(2):
                    pool.wait_ge(r_x1v, 2 * i + s + 1)
                    pool.wait_ge(x2_loaded[s], 16 * i + 16)
                    row = x1[:, 2 * i + s, :]
                    pool.tensor_tensor(row, row, x_again[s], ALU.add).then_inc(r_x1, 1)
                for s in range(2):
                    pool.wait_ge(r_x1, 2 * i + s + 1)
                    if i == 0:
                        pool.dma_start(x_again[s], x_d[(2 + s) * P:(3 + s) * P, :]).then_inc(x2_loaded[s], 16)
                    pool.wait_ge(ms_ready, 1 + TT + 2 * i + s + 1)
                    pool.wait_ge(xn_ready, 2 + TT + 2 * i + s)
                    power(1, 4).then_inc(rstd_ready, 1)

            for i in range(2):
                x1_step(i)
            pool.wait_ge(h_lo_ready, 4 + 32)
            pool.memset(arena[:, 32 * KB:64 * KB], 0.0).then_inc(z_free, 1)
            pool.memset(ff_pad[:, 0, 0:2], 0.0).then_inc(z_free, 1)

            pool.wait_ge(unit_done, UNITS + RING)
            pool.dma_start(z_gain, row_on_all(norm_ffn_post, 0, D)).then_inc(gf_loaded, 16)
            for n in range(TT):
                pool.wait_ge(z_ms, n + 1)
                power(1, n).then_inc(z_r, 1)
                pool.wait_ge(z_o, n + 1)
                pool.dma_start(out_d[n * P:(n + 1) * P, :], acc[:, n, :]).then_inc(z_st, 16)
            pool.wait_ge(z_st, 16 * TT)

        @block.vector
        def _(dve):
            for s_, n in ((lo_ready, RING), (xn_ready, 2), (h_lo_ready, 4), (tok_evac, 4), (ms_ready, 1), (v_ms, 1),
                          (y_mul, 2), (y_lo, 1), (qk_conv_s, 1), (b_ms, 1), (b_h, 1), (mg_used, 2), (up_evac, 2),
                          (ff_conv, 1), (dn_evac, 16)):
                dve.sem_inc(s_, n)

            def split_lo(u, rnd, s):
                dve.wait_ge(hi_ready, u + 1)
                dve.tensor_tensor(w_lo[:, s, :], raw[:, s, :], f32(w_hi[:, s, :]), ALU.subtract).then_inc(lo_ready, 1)

            made = [0]

            def then(ins):
                made[0] += 1
                ins.then_inc(vchain, 1)
                dve.wait_ge(vchain, made[0])

            dve.memset(ones_col, 1.0)
            dve.memset(m_prev[:, 0:1], 0.0)
            dve.memset(nstate, 0.0)
            dve.wait_ge(prm_turned, 1)
            then(dve.tensor_copy(prm[:, 0:248], ps[:, 5, 0:248]))
            dve.tensor_copy(prm[:, 256:344], ps[:, 5, 256:344]).then_inc(prm_ready, 1)
            then(dve.tensor_tensor(lb_t[:, 0:8], prm[:, PLB:PLB + 8], prm[:, PLB + 8:PLB + 16], ALU.max))
            then(dve.tensor_tensor(lb_t[:, 8:16], prm[:, PLB:PLB + 8], lb_t[:, 0:8], ALU.subtract))
            dve.tensor_tensor(lb_t[:, 16:24], prm[:, PLB + 8:PLB + 16], lb_t[:, 0:8], ALU.subtract).then_inc(prm_ready, 1)
            dve.wait_ge(achain, 1)
            then(dve.tensor_tensor(lb_t[:, 0:8], lb_t[:, 8:16], lb_t[:, 16:24], ALU.add))
            then(dve.reciprocal(lb_t[:, 0:8], lb_t[:, 0:8]))
            then(dve.tensor_tensor(lb, lb_t[:, 8:16], lb_t[:, 0:8], ALU.mult))
            then(dve.tensor_scalar(omlb, lb, -1.0, 1.0, ALU.mult, ALU.add))

            def norm_row(src, gain, xn, s, t, a):
                dve.wait_ge(sq_done, t + 1)
                dve.tensor_scalar(ms[:, a:a + 1], ss[:, 0:1], 1.0 / D, EPS, ALU.mult, ALU.add).then_inc(ms_ready, 1)
                dve.wait_ge(rstd_ready, t + 1)
                dve.wait_ge(turned, 4 * t + 4)
                dve.scalar_tensor_tensor(out=xn[:, s, :], in0=src, scalar=rstd[:, a:a + 1], in1=gain, op0=ALU.mult,
                                         op1=ALU.mult).then_inc(xn_ready, 1)

            def turned_lo(i, base):
                for s in range(2):
                    for g in range(4):
                        dve.wait_ge(h_hi_ready, 4 * (2 * i + s + base) + g + 1)
                        rows, tok = slice(4 * g, 4 * g + 4), ds((2 * i + s) * P, P)
                        dve.tensor_tensor(h_lo[:, rows, tok], ps[:, g, :].rearrange("p (k t) -> p k t", k=4),
                                          f32(h_hi[:, rows, tok]), ALU.subtract).then_inc(h_lo_ready, 1)

            dve.wait_ge(gain_loaded, 16)
            with dve.Fori(0, 2) as i:
                for s in range(2):
                    norm_row(n_x[:, s, :], n_gain, n_xn, s, 2 * i + s, 0)
                turned_lo(i, 0)
            dve.wait_ge(achain, 2)
            dve.tensor_tensor(wg_lo, wg_raw, f32(wg_hi), ALU.subtract).then_inc(wg_split, 1)
            split_lo(0, 0, 0)
            dve.wait_ge(gates_done, 1)
            dve.wait_ge(vg_loaded, 16)
            then(dve.tensor_tensor(G, ps[:, 4, 0:32].rearrange("p (n c) -> p n c", n=TT),
                                   gbias.unsqueeze(1).broadcast_to([P, TT, 8]), ALU.add))
            then(dve.tensor_scalar(gl[:, 1, :, :], G[:, :, 4:8], -1.0, None, ALU.mult))
            dve.tensor_tensor(gl[:, 2, :, :], G[:, :, 4:8], gl[:, 1, :, :], ALU.min).then_inc(r_act, 1)
            dve.tensor_copy(gl[:, 0, :, :], G[:, :, 0:4])

            def columns(first, units, work):
                un = units_of(first, 2)
                with dve.Fori(0, units // 2) as i:
                    for s in range(2):
                        split_lo(*un(i, s + 1))
                        if work:
                            work(2 * i + s, s, i)

            def flat(t, m):
                return t[:, ds(m, 1), :].rearrange("p a t -> p (a t)")

            def f_affine(h, s, i):
                dve.wait_ge(cm_evac, N_F + h + 3)
                dve.tensor_scalar(flat(f_all, h), flat(f_all, h), omlb[:, ds(h, 1)], lb[:, ds(h, 1)], ALU.mult,
                                  ALU.add).then_inc(f_ready, 1)

            def v_blocks(first, v_all, bias, b0, loaded):
                un = units_of(first, 4)
                dve.wait_ge(vb_loaded, loaded)
                with dve.Fori(0, 2) as i:
                    for q in range(4):
                        split_lo(*un(i, q + 1))
                    for n in range(TT):
                        if n < TT - 1:
                            dve.wait_ge(tok_done, 3 * (b0 + i) + n + 1)
                        else:
                            dve.wait_ge(unit_done, first + 4 * i + 4 + RING)
                        dve.tensor_tensor(v_all[:, n, ds(512 * i, 512)], ps[:, n, :], bias[:, ds(512 * i, 512)],
                                          ALU.add).then_inc(tok_evac, 1)

            columns(U_F, NU_F, f_affine)
            columns(U_Q, NU_Q, None)
            v_blocks(U_I, v_hg, vbias_hg, 0, 16)

            def chunks(t):
                return t.rearrange("p (c k) -> p c k", k=CHUNK)

            def hg_prep(i):
                dve.wait_ge(a_ln, i + 1)
                dve.tensor_tensor_scan(hg_b[:, 0:T], hg_mask, hg_e3[:, 0:T], 0.0, ALU.mult, ALU.add)
                dve.tensor_tensor_scan(hg_b[:, T:2 * T], hg_mask, hg_e3[:, T:2 * T], 0.0, ALU.mult,
                                       ALU.add).then_inc(v_scan, 1)
                dve.wait_ge(v_scan, i + 1)
                dve.tensor_tensor(chunks(hg_e3), chunks(hg_b)[:, :, CHUNK - 1:CHUNK].broadcast_to([P, 2 * HG_H, CHUNK]),
                                  chunks(hg_b), ALU.subtract).then_inc(v_d3, 1)
                dve.wait_ge(a_exp, 3 * i + 3)
                f_pair = f_all[:, :, ds(i * P, P)]
                dve.wait_ge(v_sa, i + 1)
                dve.tensor_copy(dec.rearrange("p h c -> p (h c)").unsqueeze(2), chunks(hg_e1)[:, :, CHUNK - 1:CHUNK])\
                    .then_inc(v_dec, 1)
                for e in (hg_e2, hg_e3):
                    dve.scalar_tensor_tensor(out=heads(e), in0=f_pair, scalar=1.0, in1=heads(e), op0=ALU.subtract,
                                             op1=ALU.mult)
                dve.wait_ge(v_dec, i + 1)
                dve.scalar_tensor_tensor(out=heads(hg_e1), in0=q_all[:, :, ds(i * P, P)], scalar=-SCALE,
                                         in1=heads(hg_e1), op0=ALU.mult, op1=ALU.mult).then_inc(v_prep, 1)

            dve.memset(hg_sa, 0.0).then_inc(v_sa, 1)
            dve.wait_ge(consts_v, 2)
            hg_prep(0)
            un_ga = units_of(U_GA, 4)

            def hg_state(new, old, c, update):
                for h in range(HG_H):
                    ins = dve.scalar_tensor_tensor(out=heads(new)[:, h, :], in0=heads(old)[:, h, :], scalar=dec[:, h, c:c + 1],
                                                   in1=update[:, h, :], op0=ALU.mult, op1=ALU.add)
                return ins

            def hg_step(i, last):
                split_lo(*un_ga(i, 1))
                split_lo(*un_ga(i, 2))
                dve.wait_ge(p_u0, i + 1)
                hg_state(hg_sb, hg_sa, 0, hT_).then_inc(v_sb, 1)
                split_lo(*un_ga(i, 3))
                dve.wait_ge(p_u1, i + 1)
                dve.wait_ge(v_sb, i + 1)
                hg_state(hg_sa, hg_sb, 1, hA_).then_inc(v_sa, 1)
                dve.wait_ge(g_sq, i + 1)
                dve.tensor_reduce(ss[:, 0:8], heads(hg_e3), AX.X, ALU.add).then_inc(v_red, 1)
                dve.wait_ge(v_red, i + 1)
                dve.tensor_scalar(ms[:, 0:8], ss[:, 0:8], 1.0 / P, EPS, ALU.mult, ALU.add).then_inc(v_ms, 1)
                dve.wait_ge(g_r, i + 1)
                dve.tensor_tensor(heads(hg_on), heads(hg_on), rstd[:, 0:8].unsqueeze(2).broadcast_to([P, HG_H, P]),
                                  ALU.mult).then_inc(v_on, 1)
                split_lo(*un_ga(i, 4))
                if not last:
                    hg_prep(i + 1)

            with dve.Fori(0, TT - 1) as i:
                hg_step(i, False)
            hg_step(TT - 1, True)

            def gating(src, gain0, y_h, y_l, n0, cm0, slot_of):
                def work(h, s, i):
                    dve.wait_ge(cm_evac, cm0 + h + 3)
                    dve.wait_ge(y_lo, n0 + h + 1)
                    dve.scalar_tensor_tensor(out=g_y, in0=flat(src, slot_of(s, i)), scalar=prm[:, ds(gain0 + h, 1)],
                                             in1=g_act[:, s, :], op0=ALU.mult, op1=ALU.mult).then_inc(y_mul, 1)
                    dve.wait_ge(y_hi, n0 + h + 1)
                    dve.tensor_tensor(flat(y_l, h), g_y, f32(flat(y_h, h)), ALU.subtract).then_inc(y_lo, 1)
                return work

            dve.wait_ge(a_ot, TT + 1)
            columns(U_G, NU_G, gating(q_all, PHG, ya_hi, ya_lo, 0, N_G, lambda s, i: 2 * i + s))

            dve.wait_ge(achain, 4)
            then(dve.tensor_scalar(gl[:, 1, :, :], G[:, :, 4:8], 0.0, None, ALU.min))
            dve.tensor_tensor(gl[:, 1, :, :], gl[:, 1, :, :], gl[:, 2, :, :], ALU.subtract).then_inc(r_in, 1)
            dve.wait_ge(y_lo, 1 + 8)
            then(dve.memset(mask_row, 1.0))
            then(dve.memset(chunks(mask_row)[:, :, 0:1], 0.0))
            dve.wait_ge(r_rows, 1)
            then(dve.tensor_tensor_scan(row_b, mask_row, ps[0:ML_H, 1, :], 0.0, ALU.mult, ALU.add))
            then(dve.tensor_tensor(row_a, ps[0:ML_H, 0, :], row_b, ALU.subtract))
            with dve.Fori(0, T // CHUNK) as c:
                span = ds(c * CHUNK, CHUNK)
                dve.tensor_tensor_scan(row_m[:, span], row_a[:, span], row_a[:, span], m_prev[:, ds(c, 1)], ALU.max,
                                       ALU.max).then_inc(v_row, 1)
                dve.wait_ge(v_row, 2 * c + 1)
                end = ds(c * CHUNK + CHUNK - 1, 1)
                dve.tensor_tensor(m_prev[:, ds(c + 1, 1)], row_b[:, end], row_m[:, end], ALU.add).then_inc(v_row, 1)
                dve.wait_ge(v_row, 2 * c + 2)
            NC = T // CHUNK
            dve.tensor_tensor(chunks(row_r2), m_prev[:, 0:NC].unsqueeze(2).broadcast_to([ML_H, NC, CHUNK]), chunks(row_m),
                              ALU.subtract)
            dve.tensor_tensor(chunks(row_w), chunks(row_a), chunks(row_m)[:, :, CHUNK - 1:CHUNK]
                              .broadcast_to([ML_H, NC, CHUNK]), ALU.subtract)
            dve.tensor_tensor(row_r3, row_b, row_m, ALU.add).then_inc(r_act, 1)
            then(dve.memset(qk_pre[:, 0:3], 0.0))

            def qk_conv_tile(m, s, i):
                dve.wait_ge(cm_evac, N_QK + m + 3)
                dve.wait_ge(qk_ready, m + 1)
                dve.tensor_scalar(qk_conv, qk_pre[:, 3:3 + T], prm[:, ds(PCW + 24 + m, 1)], prm[:, ds(PCB + m, 1)],
                                  ALU.mult, ALU.add).then_inc(v_conv, 1)
                for n, k in enumerate((2, 1, 0)):
                    dve.wait_ge(v_conv, 3 * m + n + 1)
                    dve.scalar_tensor_tensor(out=qk_conv, in0=qk_pre[:, k:k + T], scalar=prm[:, ds(PCW + 8 * k + m, 1)],
                                             in1=qk_conv, op0=ALU.mult, op1=ALU.add)\
                        .then_inc(qk_conv_s if k == 0 else v_conv, 1)

            dve.sem_inc(qk_ready, 1)
            columns(U_QK, NU_QK, qk_conv_tile)
            dve.wait_ge(r_cols, 1)
            dve.tensor_copy(cols.rearrange("p n k c -> p (n k c)"), ps[:, 4, 0:48]).then_inc(r_cols_sb, 1)
            v_blocks(U_V, v_ml, vbias_ml, 2, 32)

            hd, kq = heads(ml_d, ML_H), (heads(ml_kw0, ML_H), heads(ml_kw1, ML_H))
            dve.wait_ge(qk_ready, 1 + NU_QK)
            dve.memset(ml_ca, 0.0)
            dve.memset(ml_kw0, 0.0)
            dve.memset(ml_kw1, 0.0).then_inc(b_ca, 1)
            dve.wait_ge(b_ca, 1)
            un_gb = units_of(U_GB, 4)
            decm = mlm[:, 0:8].rearrange("p (h c) -> p h c", c=2)

            def ml_state(new, old, c, n_old, n_new, un0):
                for h in range(ML_H):
                    dve.scalar_tensor_tensor(out=heads(new, ML_H)[:, h, :], in0=heads(old, ML_H)[:, h, :],
                                             scalar=decm[:, h, c:c + 1], in1=mX[:, h, :], op0=ALU.mult, op1=ALU.add)
                for h in range(ML_H):
                    ins = dve.scalar_tensor_tensor(out=nstate[:, n_new + h:n_new + h + 1], in0=nstate[:, n_old + h:n_old + h + 1],
                                                   scalar=decm[:, h, c:c + 1], in1=ps[:, 3, un0 + h:un0 + h + 1],
                                                   op0=ALU.mult, op1=ALU.add)
                return ins

            def ml_step(i, last):
                split_lo(*un_gb(i, 1))
                dve.wait_ge(b_p1, i + 2)
                col = cols[:, ds(i, 1), :, :].rearrange("p n k c -> p (n k) c")
                for h in range(ML_H):
                    ins = dve.tensor_scalar(hd[:, h, :], mM[:, h, :], col[:, 0, h:h + 1], 0.0, ALU.subtract, ALU.max)
                ins.then_inc(b_d, 1)
                dve.tensor_copy(decm, mR.rearrange("p h (c k) -> p h c k", c=2)[:, :, :, CHUNK - 1:CHUNK]
                                .rearrange("p h c k -> p h (c k)"))
                dve.tensor_tensor(heads(ml_q, ML_H), qk_all[:, 0:ML_H, ds(i * P, P)], mR, ALU.mult).then_inc(b_q, 1)
                for c in range(2):
                    a, b = c * CHUNK, (c + 1) * CHUNK
                    ins = dve.tensor_tensor(kq[c][a:b, :, :], mKT[a:b, :, :],
                                            col[a:b, 1, :].unsqueeze(2).broadcast_to([CHUNK, ML_H, P]), ALU.mult)
                ins.then_inc(b_kw, 1)
                dve.wait_ge(b_dm, 2 * i + 2)
                dve.tensor_tensor(hd, mKQ, hd, ALU.mult).then_inc(b_sc, 1)
                split_lo(*un_gb(i, 2))
                dve.wait_ge(b_n0, i + 1)
                ml_state(ml_cb, ml_ca, 0, 0, 4, 4).then_inc(b_cb, 1)
                split_lo(*un_gb(i, 3))
                dve.wait_ge(b_n1, i + 1)
                dve.tensor_scalar(den[:, 0:4], ps[:, 3, 0:4], -1.0, None, ALU.mult).then_inc(b_den, 1)
                dve.wait_ge(b_den, 5 * i + 1)
                dve.tensor_tensor(den[:, 0:4], ps[:, 3, 0:4], den[:, 0:4], ALU.max).then_inc(b_den, 1)
                dve.wait_ge(b_den, 5 * i + 2)
                dve.tensor_tensor(den[:, 0:4], den[:, 0:4], col[:, 2, :], ALU.max).then_inc(b_den, 1)
                dve.wait_ge(b_den, 5 * i + 3)
                dve.reciprocal(den[:, 4:8], den[:, 0:4]).then_inc(b_den, 1)
                dve.wait_ge(b_den, 5 * i + 4)
                dve.tensor_tensor(heads(ml_h, ML_H), mN, den[:, 4:8].unsqueeze(2).broadcast_to([P, ML_H, ML_V]),
                                  ALU.mult).then_inc(b_h, 1)
                dve.wait_ge(b_cb, i + 1)
                ml_state(ml_ca, ml_cb, 1, 4, 0, 8).then_inc(b_ca, 1)
                dve.wait_ge(b_sq, i + 1)
                dve.tensor_reduce(ss[:, 0:4], heads(ml_sq, ML_H), AX.X, ALU.add).then_inc(b_den, 1)
                dve.wait_ge(b_den, 5 * i + 5)
                dve.tensor_scalar(ms[:, 0:4], ss[:, 0:4], 1.0 / ML_V, EPS, ALU.mult, ALU.add).then_inc(b_ms, 1)
                split_lo(*un_gb(i, 4))
                dve.wait_ge(b_r, i + 1)
                dve.tensor_tensor(heads(ml_h, ML_H), heads(ml_h, ML_H),
                                  rstd[:, 0:4].unsqueeze(2).broadcast_to([P, ML_H, ML_V]), ALU.mult).then_inc(b_hn, 1)
                dve.wait_ge(b_ca, i + 2)

            with dve.Fori(0, TT - 1) as i:
                ml_step(i, False)
            ml_step(TT - 1, True)

            dve.wait_ge(b_otc, TT + 1)
            columns(U_O, NU_O, gating(qk_all, PML, yb_hi, yb_lo, 8, N_O, lambda s, i: 4 * s + i))

            un_up = units_of(U_UP, 2)

            def merge(i, j, s):
                split_lo(U_UP + 2 * j + 1, U_UP // 2 + j, 1)
                split_lo(U_UP + 2 * j + 2, U_UP // 2 + j + 1, 0)
                dve.wait_ge(unit_done, U_UP + 2 * j + 2 + RING)
                dve.wait_ge(mg_loaded[s], 32 * i + 32)
                for d in range(2):
                    dve.wait_ge(m_lo, 2 * j + d + 1)
                    dve.tensor_tensor(m_a, ps[:, 4 * s + d, :], m_gates[:, s, 0, d, :], ALU.mult)
                    dve.tensor_tensor(m_b, ps[:, 4 * s + 2 + d, :], m_gates[:, s, 1, d, :], ALU.mult)\
                        .then_inc(v_merge if d == 0 else up_evac, 1)
                    if d == 0:
                        dve.wait_ge(v_merge, j + 1)
                    else:
                        dve.wait_ge(up_evac, j + 3)
                    dve.tensor_tensor(m_sum[:, d, :], m_a, m_b, ALU.add).then_inc(m_ready, 1)
                    dve.wait_ge(m_hi, 2 * j + d + 1)
                    dve.tensor_tensor(flat(h_lo, 2 * j + d), m_sum[:, d, :], f32(flat(h_hi, 2 * j + d)),
                                      ALU.subtract).then_inc(m_lo, 1)
                dve.sem_inc(mg_used, 1)

            dve.sem_inc(m_lo, 1)
            with dve.Fori(0, 4) as i:
                for s in range(2):
                    merge(i, 2 * i + s, s)

            un_out = units_of(U_OUT, 4)
            with dve.Fori(0, 4) as i:
                for q in range(4):
                    split_lo(*un_out(i, q + 1))

            dve.wait_ge(o_evac, 4 + 16)
            then(dve.tensor_reduce(ms[:, 0:4], ss.rearrange("p (n b) -> p n b", n=TT), AX.X, ALU.add))
            dve.tensor_scalar(ms[:, 0:4], ms[:, 0:4], 1.0 / D, EPS, ALU.mult, ALU.add).then_inc(r_ms, 1)
            dve.wait_ge(r_pow, 1)
            dve.wait_ge(gp_loaded, 32)

            def x1_rows(n):
                row = x1[:, n, :]
                dve.scalar_tensor_tensor(out=row, in0=row, scalar=rstd[:, n:n + 1], in1=g_post, op0=ALU.mult,
                                         op1=ALU.mult).then_inc(r_x1v, 1)

            x1_rows(0)
            x1_rows(1)
            for i in range(2):
                for s in range(2):
                    norm_row(x1[:, 2 * i + s, :], g_pre2, xn2, s, TT + 2 * i + s, 4)
                    if i == 0:
                        x1_rows(2 + s)
                turned_lo(i, TT)

            un_ff = units_of(U_FF, FF_UNITS)

            def mlp_step(i, last):
                u0 = U_FF + FF_UNITS * i
                for f in range(FG):
                    bank = (4, 6, 0, 2)[f]
                    t = FG * i + f
                    split_lo(*un_ff(i, 2 * f + 1))
                    split_lo(*un_ff(i, 2 * f + 2))
                    dve.wait_ge(ff_gate, t + 1)
                    dve.tensor_scalar(ff_c, ff_pad[:, 0, 2:2 + T], prm[:, ds(PFW1 + FT + t, 1)], prm[:, ds(PFB + t, 1)],
                                      ALU.mult, ALU.add).then_inc(ff_chain, 1)
                    dve.wait_ge(ff_chain, 2 * t + 1)
                    dve.scalar_tensor_tensor(out=ff_c, in0=ff_pad[:, 0, 1:1 + T], scalar=prm[:, ds(PFW1 + t, 1)], in1=ff_c,
                                             op0=ALU.mult, op1=ALU.add).then_inc(ff_chain, 1)
                    dve.wait_ge(ff_chain, 2 * t + 2)
                    dve.scalar_tensor_tensor(out=ff_c, in0=ff_pad[:, 0, 0:T], scalar=prm[:, ds(PFW0 + t, 1)], in1=ff_c,
                                             op0=ALU.mult, op1=ALU.add).then_inc(ff_conv, 1)
                    dve.wait_ge(ff_gelu, t + 1)
                    dve.wait_ge(unit_done, u0 + 2 * f + 2 + RING)
                    dve.tensor_tensor(ff_v, ps[:, bank + 1, :], ff_c, ALU.mult).then_inc(ff_mul, 1)
                    dve.wait_ge(ff_hi, t + 1)
                    dve.tensor_tensor(act_lo[:, f, :], ff_v, f32(act_hi[:, f, :]), ALU.subtract).then_inc(ff_lo, 1)
                    dve.wait_ge(ff_lo, t + 1)
                for d in range(4):
                    if not (last and d == 3):
                        split_lo(*un_ff(i, 2 * FG + d + 1))
                    b0 = 4 if d % 2 == 0 else 0
                    for n in range(TT):
                        if n < TT - 1:
                            dve.wait_ge(dn_done, 3 * (4 * i + d) + n + 1)
                        else:
                            dve.wait_ge(unit_done, u0 + 2 * FG + d + 1 + RING)
                        part = acc[:, n, 512 * d:512 * d + 512]
                        dve.tensor_tensor(part, part, ps[:, b0 + n, :], ALU.add).then_inc(dn_evac, 1)

            dve.wait_ge(z_free, 2)
            with dve.Fori(0, FF_STEPS - 1) as i:
                mlp_step(i, False)
                dve.wait_ge(dn_evac, 16 * (i + 2))
            mlp_step(FF_STEPS - 1, True)

            dve.wait_ge(gf_loaded, 16)
            for n in range(TT):
                dve.wait_ge(z_sq, n + 1)
                dve.tensor_scalar(ms[:, n:n + 1], ss[:, 8 + n:9 + n], 1.0 / D, EPS, ALU.mult, ALU.add).then_inc(z_ms, 1)
                dve.wait_ge(z_r, n + 1)
                dve.scalar_tensor_tensor(out=acc[:, n, :], in0=acc[:, n, :], scalar=rstd[:, n:n + 1], in1=z_gain,
                                         op0=ALU.mult, op1=ALU.mult).then_inc(z_y, 1)
                dve.wait_ge(z_y, n + 1)
                dve.tensor_tensor(acc[:, n, :], acc[:, n, :], x1[:, n, :], ALU.add).then_inc(z_o, 1)


_INS = ["x", "norm_mix_pre", "norm_mix_post", "norm_ffn_pre", "norm_ffn_post", "w_in", "b_in", "hg_lb_logits", "hg_norm",
        "ml_conv_w", "ml_conv_b", "ml_norm", "w_up_a", "w_up_b", "w_out", "ffn_w_gate", "ffn_w_up", "ffn_conv_w",
        "ffn_conv_b", "ffn_w_down"]
_OUT_SHAPE = (1, T, D)


def kernel(**inputs):
    import numpy as np
    import concourse.bacc as bacc
    from concourse.bass_utils import run_bass_kernel_spmd

    nc = bacc.Bacc("TRN2", target_bir_lowering=False, num_devices=1)
    arrays, args = {}, []
    for name in _INS:
        a = np.ascontiguousarray(inputs[name])
        arrays[f"in_{name}"] = a
        args.append(nc.dram_tensor(f"in_{name}", a.shape, mybir.dt.from_np(a.dtype), kind="ExternalInput").ap())
    args.append(nc.dram_tensor("out", _OUT_SHAPE, F32, kind="ExternalOutput").ap())
    build(nc, *args)
    r = run_bass_kernel_spmd(nc, [arrays], core_ids=[0])
    return r.results[0]["out"]
```

```python
from contextlib import ExitStack

import concourse.bass as bass
from concourse import mybir

ALU = mybir.AluOpType
ACT = mybir.ActivationFunctionType
AX = mybir.AxisListType
F32 = mybir.dt.float32
F32R = mybir.dt.float32r
ds = bass.ds

P = 128
D = 2048
T = 512
KT = D // P
TT = T // P
CHUNK = 64
HG_H, HG_W = 8, 1024
ML_H, ML_V, ML_W = 4, 256, 1024
FF = 5632
FT = FF // P
FG = 4
EPS = 1e-6
SCALE = float(P) ** -0.5

C_Q, C_F, C_I, C_G, C_QK, C_V, C_O, C_IG, C_GA, C_GB = 0, 1024, 2048, 3072, 4096, 5120, 6144, 7168, 7176, 9224

U = 2048
RING = 2
NU_F, NU_Q, NU_I, NU_GA, NU_G, NU_QK, NU_V, NU_GB, NU_O, NU_UP, NU_OUT = 8, 8, 8, 16, 8, 8, 8, 16, 8, 16, 16
U_I = 0
U_F = U_I + NU_I
U_Q = U_F + NU_F
U_GA = U_Q + NU_Q
U_G = U_GA + NU_GA
U_QK = U_G + NU_G
U_V = U_QK + NU_QK
U_GB = U_V + NU_V
U_O = U_GB + NU_GB
U_UP = U_O + NU_O
U_OUT = U_UP + NU_UP
U_FF = U_OUT + NU_OUT
FF_UNITS = 3 * FG
FF_STEPS = FT // FG
UNITS = U_FF + FF_UNITS * FF_STEPS

N_F, N_Q, N_GA, N_G, N_QK, N_GB, N_O = 0, 8, 16, 32, 40, 48, 64

PB = 0
PB_GATES = 56
PLB = 88
PHG = 104
PML = 112
PCB = 120
PCW = 128
PFB = 160
PFW0 = 204
PFW1 = 256


def build(nc, x, norm_mix_pre, norm_mix_post, norm_ffn_pre, norm_ffn_post, w_in, b_in, hg_lb_logits, hg_norm,
          ml_conv_w, ml_conv_b, ml_norm, w_up_a, w_up_b, w_out, ffn_w_gate, ffn_w_up, ffn_conv_w, ffn_conv_b,
          ffn_w_down, out):
    x_d = x.rearrange("b t d -> (b t) d")
    out_d = out.rearrange("b t d -> (b t) d")

    def ktiles(w):
        return w.rearrange("l (j p) n -> p (l j) n", p=P)

    w_in_d, w_out_d, w_gate_d, w_up_d, w_down_d = map(ktiles, (w_in, w_out, ffn_w_gate, ffn_w_up, ffn_w_down))
    up_a_d, up_b_d = ktiles(w_up_a), ktiles(w_up_b)

    def row_on_all(v, a, n):
        return v[0:1, a:a + n].broadcast_to([P, n])

    gates_d = nc.dram_tensor("merge_gates", (2, KT, P, T), F32).ap()

    with ExitStack() as ctx:
        def sb(name, shape, dt=F32):
            return ctx.enter_context(nc.sbuf_tensor(name, shape, dt))

        def sem(name):
            return ctx.enter_context(nc.semaphore(name))

        h_hi = sb("h_hi", [P, KT, T], F32R)
        h_lo = sb("h_lo", [P, KT, T], F32R)
        raw = sb("raw", [P, RING, U])
        w_hi = sb("w_hi", [P, RING, U], F32R)
        w_lo = sb("w_lo", [P, RING, U], F32R)
        prm = sb("prm", [P, 384])
        ident = sb("ident", [P, P])
        small = sb("small", [P, 264])
        KB = 256
        ARENA = 92 * KB + KB // 2
        with nc.sbuf_tensor("arena", [P, ARENA], F32) as t:
            arena = t
        with ExitStack() as over:
            def at(name, kb, dt=F32R):
                return over.enter_context(nc.sbuf_tensor(name, [P, kb * KB], dt))
            yb_hi, ya_hi, ya_lo, _, yb_lo = (at(n, 16) for n in ("yb_hi", "ya_hi", "ya_lo", "gap1", "yb_lo"))
        with ExitStack() as over:
            def at(name, kb, dt=F32R):
                return over.enter_context(nc.sbuf_tensor(name, [P, kb * KB], dt))
            at("gap2", 64)
            act_hi, act_lo = at("act_hi", 8), at("act_lo", 8)
        ctx.enter_context(nc.sbuf_tensor("arena_keep", [P, ARENA], F32))


        def tiles(t):
            return t[:, :].rearrange("p (j t) -> p j t", t=T)
        yb_lo_flat = yb_lo
        ya_hi, ya_lo, yb_hi, yb_lo, act_hi, act_lo = map(tiles, (ya_hi, ya_lo, yb_hi, yb_lo, act_hi, act_lo))

        def ar(kb, n):
            a = int(kb * KB)
            return arena[:, a:a + n]

        def f32(r):
            return r.bitcast(F32)

        n_x = ar(0, 2 * D).rearrange("p (s d) -> p s d", s=2)
        n_gain = ar(16, D)
        n_xn = ar(24, 2 * D).rearrange("p (s d) -> p s d", s=2)
        n_junk = ar(40, D)
        prow = ar(48, 3 * P).rearrange("p (s c) -> p s c", s=3)
        q_all = ar(0, HG_H * T).rearrange("p (h t) -> p h t", h=HG_H)
        f_all = ar(16, HG_H * T).rearrange("p (h t) -> p h t", h=HG_H)
        v_hg = ar(32, TT * HG_W).rearrange("p (n c) -> p n c", n=TT)
        W8 = HG_H * P
        hg_b, hg_on, hg_e1, hg_e2, hg_e3, hg_at, hg_ke0, hg_ke1, hg_sa, hg_sb = (
            ar(48 + 4 * i, W8) for i in range(10))
        hg_mask = ar(88, T)
        gate_a = ar(90, T)
        vbias_hg = hg_at

        def heads(t, h=HG_H):
            return t.rearrange("p (h c) -> p h c", h=h)
        qk_all = ar(48, 8 * T).rearrange("p (m t) -> p m t", m=8)
        v_ml = ar(64, TT * ML_W).rearrange("p (n c) -> p n c", n=TT)
        row_m, row_r2, row_b, row_a, row_w, row_r3, row_t = (arena[0:ML_H, i * T:(i + 1) * T] for i in range(7))
        ml_k, ml_q, ml_d, ml_kw0, ml_kw1 = (ar(4 + 2 * i, T) for i in range(5))
        ml_sq = ar(4, ML_W)
        ml_ca, ml_cb, ml_h = (ar(80 + 4 * i, ML_W) for i in range(3))
        mask_row = arena[0:ML_H, 14 * KB:14 * KB + T]
        vbias_ml = ml_h
        wg_raw = ar(48, KT * P).rearrange("p (j n) -> p j n", j=KT)
        wg_hi, wg_lo = (yb_lo_flat[:, s * KT * P:(s + 1) * KT * P].rearrange("p (j n) -> p j n", j=KT) for s in range(2))
        COLS_WG = ((0, 32, 0), (32, 32, ML_H), (64, 64, 2 * ML_H))
        qk_pre = ar(80, T + 3)
        qk_conv = ar(83, T)
        g_act = ar(80, 2 * T).rearrange("p (s t) -> p s t", s=2)
        g_y = ar(84, T)
        gate_b = ar(14, T)
        m_gates = ar(48, 8 * T).rearrange("p (s g d t) -> p s g d t", s=2, g=2, d=2)
        m_a = ar(80, T)
        m_b = ar(82, T)
        m_sum = ar(84, 2 * T).rearrange("p (s t) -> p s t", s=2)
        x1 = ar(0, TT * D).rearrange("p (n d) -> p n d", n=TT)
        acc = ar(32, TT * D).rearrange("p (n d) -> p n d", n=TT)
        g_pre2 = ar(32, D)
        x_rows = ar(40, TT * D).rearrange("p (n d) -> p n d", n=TT)
        g_post = ar(72, D)
        junk2 = ar(80, D)
        ff_pad = ar(80, 2 * (T + 2)).rearrange("p (s t) -> p s t", s=2)
        ff_c = ar(84.5, T)
        ff_v = ar(86.5, T)
        z_gain = raw[:, 0, :]
        z_junk = ar(80, 512)

        lb = small[:, 0:8]
        omlb = small[:, 8:16]
        lb_t = small[:, 16:40]
        gbias = small[:, 72:73]
        cols = small[:, 128:176].rearrange("p (n k c) -> p n k c", n=TT, k=3)
        ss = small[:, 176:192]
        ms = small[:, 192:200]
        rstd = small[:, 200:208]
        neg_half = small[:, 208:216]
        dec = small[:, 216:232].rearrange("p (h c) -> p h c", c=2)
        den = small[:, 232:240]
        ones_col = small[:, 240:242]
        nstate = small[:, 242:250]
        mlm = small[:, 250:260]
        ss2 = small[:, 260:264]
        m_prev = sb("m_prev", [ML_H, 9])

        ps = ctx.enter_context(nc.psum_tensor("ps", [P, 8, 512], F32))

        def bank2(b, h):
            return ps[:, b:b + 2, :].rearrange("p b c -> p (b c)").rearrange("p (h c) -> p h c", h=h)
        hT_, hA_, hO_ = bank2(0, HG_H), bank2(2, HG_H), bank2(4, HG_H)
        mX, mN = bank2(0, ML_H), bank2(4, ML_H)
        mKQ = ps[:, 0, :].rearrange("p (h c) -> p h c", h=ML_H)
        mKT = ps[:, 1, :].rearrange("p (h c) -> p h c", h=ML_H)
        mM = ps[:, 2, :].rearrange("p (h c) -> p h c", h=ML_H)
        mR = ps[:, 3, :].rearrange("p (h c) -> p h c", h=ML_H)
        mOT = bank2(0, 8)

        raw_loaded = [sem(f"raw_loaded{s}") for s in range(RING)]
        hi_ready = sem("hi_ready")
        lo_ready = sem("lo_ready")
        unit_done = sem("unit_done")
        cm_evac = sem("cm_evac")
        x_loaded = [sem(f"x_loaded{s}") for s in range(2)]
        gain_loaded = sem("gain_loaded")
        prm_loaded = sem("prm_loaded")
        prm_turned = sem("prm_turned")
        prm_ready = sem("prm_ready")
        consts = sem("consts")
        consts_v = sem("consts_v")
        sq_done = sem("sq_done")
        ms_ready = sem("ms_ready")
        rstd_ready = sem("rstd_ready")
        xn_ready = sem("xn_ready")
        turned = sem("turned")
        h_hi_ready = sem("h_hi_ready")
        h_lo_ready = sem("h_lo_ready")
        vg_loaded = sem("vg_loaded")
        gates_done = sem("gates_done")
        vchain = sem("vchain")
        achain = sem("achain")
        tok_done = sem("tok_done")
        tok_evac = sem("tok_evac")
        vb_loaded = sem("vb_loaded")
        v_q0 = sem("v_q0")
        f_ready = sem("f_ready")
        q_ready = sem("q_ready")
        v_row, v_conv, b_den, v_merge = (sem(n) for n in ("v_row", "v_conv", "b_den", "v_merge"))
        a_ln, v_scan, v_d3, a_exp, v_prep = (sem(n) for n in ("a_ln", "v_scan", "v_d3", "a_exp", "v_prep"))
        p_att, a_at, g_sel, a_ke = (sem(n) for n in ("p_att", "a_at", "g_sel", "a_ke"))
        p_u0, p_o0, v_sb, p_u1, p_o1, v_sa = (sem(n) for n in ("p_u0", "p_o0", "v_sb", "p_u1", "p_o1", "v_sa"))
        a_o, g_sq, v_ms, g_r, v_on, p_ot, a_ot = (sem(n) for n in ("a_o", "g_sq", "v_ms", "g_r", "v_on", "p_ot", "a_ot"))
        gate_act = sem("gate_act")
        gate_stored = sem("gate_stored")
        y_mul, y_hi, y_lo = sem("y_mul"), sem("y_hi"), sem("y_lo")
        qk_evac, qk_conv_s, qk_ready = sem("qk_evac"), sem("qk_conv"), sem("qk_ready")
        r_in, r_rows, r_e, r_cols, r_cols_sb, r_act = (sem(n) for n in ("r_in", "r_rows", "r_e", "r_cols", "r_cols_sb", "r_act"))
        b_kst, b_p1, b_d, b_dx, b_dm, b_sc, b_q, b_kw = (sem(n) for n in ("b_kst", "b_p1", "b_d", "b_dx", "b_dm", "b_sc", "b_q", "b_kw"))
        b_n0, b_cb, b_n1, b_ca = (sem(n) for n in ("b_n0", "b_cb", "b_n1", "b_ca"))
        b_h, b_sq, b_ms, b_r, b_hn, b_ot, b_otc = (sem(n) for n in ("b_h", "b_sq", "b_ms", "b_r", "b_hn", "b_ot", "b_otc"))
        mg_loaded = [sem(f"mg_loaded{s}") for s in range(2)]
        mg_used = sem("mg_used")
        up_evac = sem("up_evac")
        m_ready, m_hi, m_lo = sem("m_ready"), sem("m_hi"), sem("m_lo")
        o_tok_done = sem("o_tok_done")
        o_evac = sem("o_evac")
        o_sq = sem("o_sq")
        x2_loaded = sem("x2_loaded")
        wg_loaded, wg_split, mem_zero, lb_done, v_dec, v_red = (sem(n) for n in ("wg_loaded", "wg_split", "mem_zero", "lb_done", "v_dec", "v_red"))
        r_ms, r_pow, r_x1, r_x1v, r_sq2, r_ms2, r_pow2 = (sem(n) for n in ("r_ms", "r_pow", "r_x1", "r_x1v", "r_sq2", "r_ms2", "r_pow2"))
        gp_loaded = sem("gp_loaded")
        ff_gate = sem("ff_gate")
        ff_conv = sem("ff_conv")
        ff_gelu = sem("ff_gelu")
        ff_mul = sem("ff_mul")
        ff_hi = sem("ff_hi")
        ff_lo = sem("ff_lo")
        ff_chain = sem("ff_chain")
        dn_done = sem("dn_done")
        dn_evac = sem("dn_evac")
        gf_loaded = sem("gf_loaded")
        z_sq, z_ms, z_r, z_y, z_o, z_st = (sem(n) for n in ("z_sq", "z_ms", "z_r", "z_y", "z_o", "z_st"))
        z_free, z_o0, z_sc = sem("z_free"), sem("z_o0"), sem("z_sc")

        block = ctx.enter_context(nc.Block())

        ZQ = D // 4

        @block.sync
        def _(sp):
            def load(u, s, src):
                sp.wait_ge(lo_ready, u + 1)
                j, n = src.shape[1], src.shape[2]
                sp.dma_start(raw[:, s, :].rearrange("p (j n) -> p j n", j=j), src).then_inc(raw_loaded[s], 16)
                assert j * n == U

            def columns(first, units, w, c0, width=P):
                with sp.Fori(0, units // 2) as i:
                    for s in range(2):
                        load(first + 2 * i + s, s, w[:, :, ds(c0 + width * (2 * i + s), width)])

            def blocks(first, n, w, c0):
                with sp.Fori(0, n) as i:
                    for q in range(4):
                        load(first + 4 * i + q, q % 2, w[:, 4 * q:4 * q + 4, ds(c0 + 512 * i, 512)])

            def load_x(t):
                sp.wait_ge(xn_ready, t + 1)
                sp.dma_start(n_x[:, t % 2, :], x_d[t * P:(t + 1) * P, :]).then_inc(x_loaded[t % 2], 16)

            def load_i(i, q):
                load(U_I + 4 * i + q, q % 2, w_in_d[:, 4 * q:4 * q + 4, C_I + 512 * i:C_I + 512 * i + 512])

            load_x(0)
            sp.dma_start(n_gain, row_on_all(norm_mix_pre, 0, D)).then_inc(gain_loaded, 16)
            load_i(0, 0)
            load_x(1)
            load_i(0, 1)
            load_x(2)
            load_x(3)
            for i in range(2):
                for q in range(4):
                    if i or q > 1:
                        load_i(i, q)
            columns(U_F, NU_F, w_in_d, C_F)
            columns(U_Q, NU_Q, w_in_d, C_Q)
            columns(U_GA, NU_GA, w_in_d, C_GA)
            columns(U_G, NU_G, w_in_d, C_G)
            columns(U_QK, NU_QK, w_in_d, C_QK)
            blocks(U_V, 2, w_in_d, C_V)
            columns(U_GB, NU_GB, w_in_d, C_GB)
            columns(U_O, NU_O, w_in_d, C_O)
            with sp.Fori(0, 8) as i:
                load(U_UP + 2 * i, 0, up_a_d[:, :, ds(256 * i, 256)])
                load(U_UP + 2 * i + 1, 1, up_b_d[:, :, ds(256 * i, 256)])
            blocks(U_OUT, 4, w_out_d, 0)
            with sp.Fori(0, FF_STEPS) as i:
                for f in range(FG):
                    load(U_FF + FF_UNITS * i + 2 * f, 0, w_gate_d[:, :, ds((FG * i + f) * P, P)])
                    load(U_FF + FF_UNITS * i + 2 * f + 1, 1, w_up_d[:, :, ds((FG * i + f) * P, P)])
                for d in range(4):
                    load(U_FF + FF_UNITS * i + 2 * FG + d, d % 2, w_down_d[:, ds(FG * i, FG), 512 * d:512 * d + 512])
            sp.wait_ge(lo_ready, UNITS - 1 + RING)
            sp.dma_start(z_gain, row_on_all(norm_ffn_post, 0, D)).then_inc(gf_loaded, 16)
            for n in range(TT):
                for a, b, done in ((0, ZQ, z_o0), (ZQ, D, z_o)):
                    sp.wait_ge(done, n + 1)
                    sp.dma_start(out_d[n * P:(n + 1) * P, a:b], acc[:, n, a:b]).then_inc(z_st, 16)
            sp.wait_ge(z_st, 16 * 2 * TT)

        @block.tensor
        def _(pe):
            pe.sem_inc(unit_done, RING)
            pe.sem_inc(turned, 8)
            for credit in (p_att, p_o1, b_p1):
                pe.sem_inc(credit, 1)

            def split_ready(u, part):
                if part == 0:
                    pe.wait_ge(hi_ready, u + 1)
                else:
                    pe.wait_ge(lo_ready, u + 1 + RING)

            def cm_unit(u, n, s, k_hi=h_hi, k_lo=h_lo):
                pe.wait_ge(cm_evac, n + 1)
                w = [t[:, s, :].rearrange("p (j n) -> p j n", j=KT) for t in (w_hi, w_lo)]
                split_ready(u, 0)
                for k in (k_hi, k_lo):
                    for j in range(KT):
                        pe.matmul(ps[:, 6 + s, :], w[0][:, j, :], k[:, j, :], start=(k is k_hi and j == 0), stop=False)
                split_ready(u, 1)
                for j in range(KT):
                    last = pe.matmul(ps[:, 6 + s, :], w[1][:, j, :], k_hi[:, j, :], start=False, stop=(j == KT - 1))
                last.then_inc(unit_done, 1)

            def cm_phase(first, n0, units):
                with pe.Fori(0, units // 2) as i:
                    for s in range(2):
                        cm_unit(first + 2 * i + s, n0 + 2 * i + s, s)

            def tm_products(b0, s, k_hi, k_lo, j0, nj, first, last, before, done):
                w = [t[:, s, :].rearrange("p (j n) -> p j n", j=nj) for t in (w_hi, w_lo)]
                for n in range(TT):
                    if first:
                        before(n)
                    for j in range(nj):
                        tok = slice(n * P, n * P + P)
                        pe.matmul(ps[:, b0 + n, :], k_hi[:, j0 + j, tok], w[0][:, j, :], start=(first and j == 0), stop=False)
                        pe.matmul(ps[:, b0 + n, :], k_hi[:, j0 + j, tok], w[1][:, j, :], start=False, stop=False)
                        mm = pe.matmul(ps[:, b0 + n, :], k_lo[:, j0 + j, tok], w[0][:, j, :], start=False,
                                       stop=(last and j == nj - 1))
                    if last:
                        mm.then_inc(done if n < TT - 1 else unit_done, 1)
                if not last:
                    mm.then_inc(unit_done, 1)

            def tm_block(u0, evac, e0, done, between=None):
                for q in range(4):
                    if between:
                        between(q)
                    split_ready(u0 + q, 0)
                    split_ready(u0 + q, 1)
                    tm_products(0, q % 2, h_hi, h_lo, 4 * q, 4, q == 0, q == 3,
                                lambda n: pe.wait_ge(evac, e0 + n + 1), done)

            pe.wait_ge(consts, 2)

            def turn_tokens(rows, t, banks):
                pe.wait_ge(xn_ready, 2 + t + 1)
                for g in range(4):
                    pe.wait_ge(h_lo_ready, 4 * t + g + 1)
                    for k in range(4):
                        mm = pe.transpose(ps[:, banks[g], k * P:(k + 1) * P], rows[:, (4 * g + k) * P:(4 * g + k + 1) * P],
                                          ident[:, :])
                    mm.then_inc(turned, 1)

            def first_units(n, q):
                split_ready(q, 0)
                split_ready(q, 1)
                pe.wait_ge(h_lo_ready, 4 + 4 * n + 4)
                w = [t[:, q, :].rearrange("p (j n) -> p j n", j=4) for t in (w_hi, w_lo)]
                tok = slice(n * P, n * P + P)
                for j in range(4):
                    for a, b in ((h_hi, 0), (h_hi, 1), (h_lo, 0)):
                        mm = pe.matmul(ps[:, n, :], a[:, 4 * q + j, tok], w[b][:, j, :],
                                       start=(q == 0 and j == 0 and a is h_hi and b == 0), stop=False)
                if n == TT - 1:
                    mm.then_inc(unit_done, 1)

            for n in range(TT):
                turn_tokens(n_xn[:, n % 2, :], n, (4, 5, 6, 7))
                if n:
                    first_units(n - 1, 1)
                first_units(n, 0)
            first_units(TT - 1, 1)
            for q in (2, 3):
                split_ready(q, 0)
                split_ready(q, 1)
                tm_products(0, q % 2, h_hi, h_lo, 4 * q, 4, False, q == 3, None, tok_done)
            pe.wait_ge(h_lo_ready, 4 + 16)
            pe.wait_ge(prm_loaded, 16 * 11)
            pe.transpose(ps[:, 4, 0:128], prow[:, 0, :], ident[:, :])
            pe.transpose(ps[:, 4, 128:248], prow[0:120, 1, :], ident[0:120, 0:120])
            pe.transpose(ps[:, 4, 256:344], prow[0:88, 2, :], ident[0:88, 0:88]).then_inc(prm_turned, 1)
            tm_block(U_I + 4, tok_evac, 4, tok_done)

            cm_phase(U_F, N_F, NU_F)
            cm_phase(U_Q, N_Q, NU_Q)

            pe.wait_ge(tok_evac, 4 + 8)
            qd, ki, ke = heads(hg_e1), heads(hg_e2), heads(hg_e3)
            at_, ke0, ke1, sa, sb_, on = map(heads, (hg_at, hg_ke0, hg_ke1, hg_sa, hg_sb, hg_on))
            with pe.Fori(0, TT) as i:
                def unit(s):
                    cm_unit(U_GA + 4 * i + s, N_GA + 4 * i + s, s % 2)
                pe.wait_ge(v_prep, i + 1)
                pe.wait_ge(a_ot, i + 1)
                for h in range(HG_H):
                    pe.transpose(hT_[:, h, :], ke[:, h, :], ident[:, :])
                pe.wait_ge(v_sa, i + 1)
                for h in range(HG_H):
                    mm = pe.matmul(hA_[:, h, :], ki[:, h, :], qd[:, h, :], start=True, stop=True)
                mm.then_inc(p_att, 1)
                unit(0)
                pe.wait_ge(a_ke, 2 * i + 2)
                for h in range(HG_H):
                    mm = pe.matmul(hT_[:, h, :], ke0[:, h, :], v_hg[:, ds(i, 1), h * P:(h + 1) * P], start=True, stop=True)
                mm.then_inc(p_u0, 1)
                pe.wait_ge(g_sel, i + 1)
                pe.wait_ge(a_o, i + 1)
                for h in range(HG_H):
                    pe.matmul(hO_[:, h, :], at_[:, h, :], v_hg[:, ds(i, 1), h * P:(h + 1) * P],
                              start=(h % 4 == 0), stop=False, skip_group_check=True)
                for h in range(HG_H):
                    mm = pe.matmul(hO_[0:CHUNK, h, :], qd[:, h, 0:CHUNK], sa[:, h, :], start=False, stop=False,
                                   skip_group_check=True)
                mm.then_inc(p_o0, 1)
                for h in range(HG_H):
                    mm = pe.matmul(hA_[:, h, :], ke1[:, h, :], v_hg[:, ds(i, 1), h * P:(h + 1) * P], start=True, stop=True)
                mm.then_inc(p_u1, 1)
                unit(1)
                pe.wait_ge(v_sb, i + 1)
                for h in range(HG_H):
                    mm = pe.matmul(hO_[CHUNK:P, h, :], qd[:, h, CHUNK:P], sb_[:, h, :], start=False, stop=True,
                                   skip_group_check=True)
                mm.then_inc(p_o1, 1)
                unit(2)
                pe.wait_ge(v_on, i + 1)
                for h in range(HG_H):
                    mm = pe.transpose(hT_[:, h, :], on[:, h, :], ident[:, :])
                mm.then_inc(p_ot, 1)
                unit(3)

            cm_phase(U_G, N_G, NU_G)
            cm_phase(U_QK, N_QK, NU_QK)
            pe.wait_ge(wg_split, 1)
            pe.wait_ge(a_ot, TT + 1)
            for k, (a, b) in enumerate(((wg_hi, h_hi), (wg_hi, h_lo), (wg_lo, h_hi))):
                for j in range(KT):
                    mm = pe.matmul(ps[:, 4, :], a[:, j, :], b[:, j, :], start=(k == 0 and j == 0), stop=(k == 2 and j == KT - 1))
            mm.then_inc(gates_done, 1)
            tm_block(U_V, tok_evac, 8, tok_done)

            def cols_of_rows(q):
                if q == 1:
                    pe.wait_ge(r_e, 3)
                    for n in range(TT):
                        for k, row in enumerate((row_a, row_w, row_r3)):
                            mm = pe.transpose(ps[:, 4, 12 * n + 4 * k:12 * n + 4 * k + 4], row[:, n * P:(n + 1) * P],
                                              ident[0:ML_H, 0:ML_H])
                    mm.then_inc(r_cols, 1)

            tm_block(U_V + 4, tok_evac, 12, tok_done, cols_of_rows)
            pe.wait_ge(tok_evac, 4 + 16)

            kst, qst, sc, kw0, kw1 = (heads(t, ML_H) for t in (ml_k, ml_q, ml_d, ml_kw0, ml_kw1))
            ca, cb, hm = (heads(t, ML_H) for t in (ml_ca, ml_cb, ml_h))
            hm8 = heads(ml_h, 8)
            DEN, UN0, UN1 = (lambda h: slice(h, h + 1)), (lambda h: slice(4 + h, 5 + h)), (lambda h: slice(8 + h, 9 + h))
            with pe.Fori(0, TT) as i:
                def unit(s):
                    cm_unit(U_GB + 4 * i + s, N_GB + 4 * i + s, s % 2)
                pe.wait_ge(b_kst, i + 1)
                pe.wait_ge(b_otc, i + 1)
                for h in range(ML_H):
                    pe.matmul(mKQ[:, h, :], kst[:, h, :], qk_all[:, h, ds(i * P, P)], start=True, stop=True)
                for h in range(ML_H):
                    pe.transpose(mKT[:, h, :], kst[:, h, :], ident[:, :])
                pe.wait_ge(b_ca, i + 1)
                for h in range(ML_H):
                    pe.matmul(mM[:, h, :], ident[0:ML_H, h:h + 1].broadcast_to([ML_H, P]), row_m[:, ds(i * P, P)], start=True, stop=True)
                for h in range(ML_H):
                    mm = pe.matmul(mR[:, h, :], ident[0:ML_H, h:h + 1].broadcast_to([ML_H, P]), row_r2[:, ds(i * P, P)], start=True, stop=True)
                mm.then_inc(b_p1, 1)
                unit(0)
                pe.wait_ge(b_kw, i + 1)
                pe.wait_ge(b_sc, i + 1)
                pe.wait_ge(b_q, i + 1)
                for h in range(ML_H):
                    pe.matmul(mX[:, h, :], kw0[:, h, :], v_ml[:, ds(i, 1), h * ML_V:(h + 1) * ML_V], start=True, stop=True)
                pe.wait_ge(b_h, i + 1)
                for h in range(ML_H):
                    pe.matmul(mN[:, h, :], sc[:, h, :], v_ml[:, ds(i, 1), h * ML_V:(h + 1) * ML_V],
                              start=(h % 2 == 0), stop=False, skip_group_check=True)
                    pe.matmul(ps[:, 3, DEN(h)], sc[:, h, :], ones_col[:, 0:1], start=(h == 0), stop=False,
                              skip_group_check=True)
                for h in range(ML_H):
                    pe.matmul(ps[:, 3, UN0(h)], kw0[:, h, :], ones_col[:, 0:1], start=False, stop=False,
                              skip_group_check=True)
                for h in range(ML_H):
                    pe.matmul(mN[0:CHUNK, h, :], qst[:, h, 0:CHUNK], ca[:, h, :], start=False, stop=False,
                              skip_group_check=True)
                    mm = pe.matmul(ps[0:CHUNK, 3, DEN(h)], qst[:, h, 0:CHUNK], nstate[:, h:h + 1], start=False,
                                   stop=False, skip_group_check=True)
                mm.then_inc(b_n0, 1)
                unit(1)
                pe.wait_ge(b_cb, i + 1)
                for h in range(ML_H):
                    pe.matmul(mX[:, h, :], kw1[:, h, :], v_ml[:, ds(i, 1), h * ML_V:(h + 1) * ML_V], start=True, stop=True)
                    pe.matmul(ps[:, 3, UN1(h)], kw1[:, h, :], ones_col[:, 0:1], start=False, stop=False,
                              skip_group_check=True)
                for h in range(ML_H):
                    pe.matmul(mN[CHUNK:P, h, :], qst[:, h, CHUNK:P], cb[:, h, :], start=False, stop=True,
                              skip_group_check=True)
                    mm = pe.matmul(ps[CHUNK:P, 3, DEN(h)], qst[:, h, CHUNK:P], nstate[:, 4 + h:5 + h], start=False,
                                   stop=True, skip_group_check=True)
                mm.then_inc(b_n1, 1)
                unit(2)
                pe.wait_ge(b_hn, i + 1)
                for h in range(8):
                    mm = pe.transpose(mOT[:, 4 * (h % 2) + h // 2, :], hm8[:, h, :], ident[:, :])
                mm.then_inc(b_ot, 1)
                unit(3)

            cm_phase(U_O, N_O, NU_O)

            pe.wait_ge(b_otc, TT + 1)
            pe.wait_ge(y_lo, 1 + 8)
            with pe.Fori(0, 4) as i:
                for h in range(2):
                    pe.wait_ge(up_evac, 2 * i + h + 1)
                    for s, (y_h, y_l) in enumerate(((ya_hi, ya_lo), (yb_hi, yb_lo))):
                        if s == 1:
                            pe.wait_ge(y_lo, 1 + 16)
                            pe.wait_ge(cm_evac, N_O + NU_O + 2)
                        u = U_UP + 4 * i + 2 * h + s
                        w = [t[:, s, :].rearrange("p (j n) -> p j n", j=8) for t in (w_hi, w_lo)]
                        for a, (wk, yk) in enumerate(((0, y_h), (0, y_l), (1, y_h))):
                            if a != 1:
                                split_ready(u, wk)
                            for d in range(2):
                                for j in range(8):
                                    mm = pe.matmul(ps[:, 4 * h + 2 * s + d, :], w[wk][:, j, d * P:(d + 1) * P], yk[:, j, :],
                                                   start=(a == 0 and j == 0), stop=(a == 2 and j == 7))
                        mm.then_inc(unit_done, 1)

            pe.wait_ge(up_evac, 2 + 7)
            with pe.Fori(0, 4) as i:
                tm_block(U_OUT + 4 * i, o_evac, 4 * i, o_tok_done, lambda q: pe.wait_ge(m_lo, 1 + 4 * (q + 1)))

            def first_hidden(n, s):
                u = U_FF + s
                split_ready(u, 0)
                split_ready(u, 1)
                pe.wait_ge(h_lo_ready, 4 + 16 + 8 * n + 8)
                w = [t[:, s, :].rearrange("p (j n) -> p j n", j=KT) for t in (w_hi, w_lo)]
                tok = slice(n * 2 * P, (n + 1) * 2 * P)
                for a, b in ((0, h_hi), (0, h_lo), (1, h_hi)):
                    for j in range(KT):
                        mm = pe.matmul(ps[:, 4 + s, tok], w[a][:, j, :], b[:, j, tok],
                                       start=(n == 0 and j == 0 and a == 0 and b is h_hi), stop=False, skip_group_check=True)
                if n:
                    mm.then_inc(unit_done, 1)

            for n in range(TT):
                turn_tokens(x_rows[:, n, :], TT + n, (6, 7, 0, 1))
                if n % 2:
                    first_hidden(n // 2, 0)
                    first_hidden(n // 2, 1)

            def mlp_step(i, first=False):
                u0 = U_FF + FF_UNITS * i
                for f in range(1 if first else 0, FG):
                    bank = (4, 6, 0, 2)[f]
                    pe.wait_ge(dn_evac, 16 * i + (12, 12, 16, 16)[f])
                    for s in range(2):
                        w = [t[:, s, :].rearrange("p (j n) -> p j n", j=KT) for t in (w_hi, w_lo)]
                        split_ready(u0 + 2 * f + s, 0)
                        for k in (h_hi, h_lo):
                            for j in range(KT):
                                pe.matmul(ps[:, bank + s, :], w[0][:, j, :], k[:, j, :], start=(k is h_hi and j == 0), stop=False)
                        split_ready(u0 + 2 * f + s, 1)
                        for j in range(KT):
                            mm = pe.matmul(ps[:, bank + s, :], w[1][:, j, :], h_hi[:, j, :], start=False, stop=(j == KT - 1))
                        mm.then_inc(unit_done, 1)
                for d in range(4):
                    u = u0 + 2 * FG + d
                    split_ready(u, 0)
                    split_ready(u, 1)
                    b0 = 4 if d % 2 == 0 else 0
                    w = [t[:, d % 2, :].rearrange("p (j n) -> p j n", j=FG) for t in (w_hi, w_lo)]
                    if d == 0:
                        pe.wait_ge(ff_mul, FG * i + 2)
                        for j in range(FG):
                            pe.wait_ge(ff_lo, FG * i + j + 1)
                            for n in range(TT):
                                tok = slice(n * P, n * P + P)
                                pe.matmul(ps[:, b0 + n, :], act_hi[:, j, tok], w[0][:, j, :], start=(j == 0), stop=False)
                                pe.matmul(ps[:, b0 + n, :], act_hi[:, j, tok], w[1][:, j, :], start=False, stop=False)
                                mm = pe.matmul(ps[:, b0 + n, :], act_lo[:, j, tok], w[0][:, j, :], start=False, stop=(j == FG - 1))
                                if j == FG - 1:
                                    mm.then_inc(dn_done if n < TT - 1 else unit_done, 1)
                    else:
                        tm_products(b0, d % 2, act_hi, act_lo, 0, FG, True, True,
                                    lambda n: pe.wait_ge(dn_evac, 16 * (i + 1) + 4 * (d - 2) + n + 1) if d >= 2 else None, dn_done)

            mlp_step(0, True)
            with pe.Fori(1, FF_STEPS - 1) as i:
                mlp_step(i)
            mlp_step(FF_STEPS - 1)

        def units_of(first, per):
            return lambda i, k: (first + per * i + k, first // 2 + (per // 2) * i + k // 2, k % 2)

        @block.scalar
        def _(act):
            for s_, n in ((cm_evac, 2), (a_o, 1), (a_ot, 1), (b_otc, 1), (o_evac, 4)):
                act.sem_inc(s_, n)
            act.sem_inc(gate_stored, 16)

            def split_hi(u, rnd, s):
                act.wait_ge(raw_loaded[s], 16 * rnd + 16)
                act.wait_ge(unit_done, u + 1)
                act.copy(w_hi[:, s, :], raw[:, s, :]).then_inc(hi_ready, 1)

            def turned_hi(t, banks, groups=range(4)):
                for g in groups:
                    act.wait_ge(turned, 8 + 4 * t + g + 1)
                    n = t % TT
                    act.copy(h_hi[:, 4 * g:4 * g + 4, n * P:(n + 1) * P],
                             ps[:, banks[g], :].rearrange("p (k t) -> p k t", k=4)).then_inc(h_hi_ready, 1)

            for t in range(TT):
                act.wait_ge(x_loaded[t % 2], 16 * (t // 2) + 16)
                act.wait_ge(ms_ready, t + 1)
                act.activation(n_junk, n_x[:, t % 2, :], ACT.Square, accum_out=ss[:, 0:1]).then_inc(sq_done, 1)
                if t < 2:
                    split_hi(t, 0, t)
                turned_hi(t, (4, 5, 6, 7))
            un_i = units_of(U_I, 4)
            for i in range(2):
                for q in range(4):
                    if i or q:
                        split_hi(*un_i(i, q + 1))
                    if (i, q) == (1, 2):
                        act.wait_ge(prm_ready, 2)
                        act.activation(lb_t[:, 8:24], lb_t[:, 8:24], ACT.Exp).then_inc(achain, 1)

            def columns(first, units, evac):
                un = units_of(first, 2)
                with act.Fori(0, units // 2) as i:
                    for s in range(2):
                        split_hi(*un(i, s + 1))
                        act.wait_ge(unit_done, first + 2 * i + s + 1 + RING)
                        evac(2 * i + s, ps[:, 6 + s, :], s)

            def blocks(first, n):
                un = units_of(first, 4)
                with act.Fori(0, n) as i:
                    for q in range(4):
                        split_hi(*un(i, q + 1))

            def into(dst, func, col):
                def evac(m, bank, s):
                    act.activation(dst[:, ds(m, 1), :], bank, func, bias=prm[:, ds(col + m, 1)]).then_inc(cm_evac, 1)
                return evac

            columns(U_F, NU_F, into(f_all, ACT.Sigmoid, 8))
            def hg_prep(i):
                act.wait_ge(p_att, i + 1)
                act.activation(heads(hg_e3), f_all[:, :, ds(i * P, P)], ACT.Ln).then_inc(a_ln, 1)
                act.wait_ge(v_scan, i + 1)
                act.wait_ge(p_o1, i + 1)
                act.activation(hg_e1, hg_b, ACT.Exp).then_inc(a_exp, 1)
                act.activation(hg_e2, hg_b, ACT.Exp, scale=-1.0).then_inc(a_exp, 1)
                act.wait_ge(v_d3, i + 1)
                act.activation(hg_e3, hg_e3, ACT.Exp).then_inc(a_exp, 1)

            def gate_unit(i, k, u0, n0, tmp, which):
                m = 4 * i + k
                act.wait_ge(unit_done, u0 + m + 1 + RING)
                act.wait_ge(gate_stored, 16 * (KT * which + m) + 16)
                act.activation(tmp, ps[:, 6 + k % 2, :], ACT.Sigmoid,
                               bias=prm[:, ds(PB_GATES + KT * which + m, 1)]).then_inc(cm_evac, 1)
                act.wait_ge(cm_evac, n0 + m + 3)
                act.dma_start(gates_d[which, ds(m, 1), :, :].rearrange("a p t -> p (a t)"), tmp).then_inc(gate_stored, 16)

            act.wait_ge(f_ready, NU_F)
            hg_prep(0)
            columns(U_Q, NU_Q, into(q_all, ACT.Silu, 0))
            un_ga = units_of(U_GA, 4)

            def hg_step(i, last):
                split_hi(*un_ga(i, 1))
                act.wait_ge(mem_zero, 2)
                act.wait_ge(p_att, i + 2)
                for a in (0, CHUNK):
                    act.copy(heads(hg_at)[a:a + CHUNK, :, a:a + CHUNK], hA_[a:a + CHUNK, :, a:a + CHUNK]).then_inc(a_at, 1)
                for a, dst in ((0, hg_ke0), (CHUNK, hg_ke1)):
                    act.copy(heads(dst)[a:a + CHUNK, :, :], hT_[a:a + CHUNK, :, :]).then_inc(a_ke, 1)
                gate_unit(i, 0, U_GA, N_GA, gate_a, 0)
                split_hi(*un_ga(i, 2))
                gate_unit(i, 1, U_GA, N_GA, gate_a, 0)
                split_hi(*un_ga(i, 3))
                act.wait_ge(p_o1, i + 2)
                act.copy(heads(hg_on), hO_).then_inc(a_o, 1)
                act.wait_ge(v_sa, i + 2)
                act.wait_ge(a_o, i + 2)
                act.activation(hg_sb, hg_on, ACT.Square).then_inc(g_sq, 1)
                if not last:
                    hg_prep(i + 1)
                gate_unit(i, 2, U_GA, N_GA, gate_a, 0)
                split_hi(*un_ga(i, 4))
                act.wait_ge(p_ot, i + 1)
                act.copy(q_all[:, :, ds(i * P, P)], hT_).then_inc(a_ot, 1)
                gate_unit(i, 3, U_GA, N_GA, gate_a, 0)

            with act.Fori(0, TT - 1) as i:
                hg_step(i, False)
            hg_step(TT - 1, True)

            def gating(func, col, y_part, n0):
                def evac(h, bank, s):
                    act.wait_ge(y_mul, n0 + h + 1)
                    act.activation(g_act[:, s, :], bank, func, bias=prm[:, ds(col + h, 1)]).then_inc(cm_evac, 1)
                    act.wait_ge(y_mul, n0 + h + 3)
                    act.copy(y_part[:, ds(h, 1), :].rearrange("p a t -> p (a t)"), g_y).then_inc(y_hi, 1)
                return evac

            columns(U_G, NU_G, gating(ACT.Silu, 24, ya_hi, 0))

            def evac_qk(m, bank, s):
                act.wait_ge(qk_conv_s, m + 1)
                act.activation(qk_pre[:, 3:3 + T], bank, ACT.Identity, bias=prm[:, ds(32 + m, 1)]).then_inc(cm_evac, 1)
                act.wait_ge(qk_conv_s, m + 2)
                act.activation(qk_all[:, ds(m, 1), :].rearrange("p a t -> p (a t)"), qk_conv, ACT.Silu).then_inc(qk_ready, 1)

            act.wait_ge(wg_loaded, 16 * len(COLS_WG))
            act.copy(wg_hi, wg_raw).then_inc(achain, 1)
            columns(U_QK, NU_QK, evac_qk)
            un_v = units_of(U_V, 4)
            for i in range(2):
                for q in range(4):
                    split_hi(*un_v(i, q + 1))
                    if (i, q) == (0, 0):
                        act.wait_ge(r_act, 1)
                        act.activation(row_w, row_w, ACT.Exp).then_inc(achain, 1)
                        act.wait_ge(achain, 3)
                        act.activation(row_w, row_w, ACT.Ln, bias=1.0).then_inc(achain, 1)
                    if (i, q) == (1, 0):
                        act.wait_ge(r_act, 2)
                        for row, sign in ((row_r2, 1.0), (row_w, 1.0), (row_r3, -1.0)):
                            act.activation(row, row, ACT.Exp, scale=sign).then_inc(r_e, 1)

            def ml_prep(i):
                act.wait_ge(b_p1, i + 1)
                act.wait_ge(b_ms, i + 1)
                act.activation(heads(ml_k, ML_H), qk_all[:, ML_H:2 * ML_H, ds(i * P, P)], ACT.Copy,
                               scale=SCALE).then_inc(b_kst, 1)

            ml_prep(0)
            un_gb = units_of(U_GB, 4)

            def ml_step(i, last):
                split_hi(*un_gb(i, 1))
                act.wait_ge(b_d, i + 1)
                act.activation(ml_d, ml_d, ACT.Exp, scale=-1.0).then_inc(b_dx, 1)
                gate_unit(i, 0, U_GB, N_GB, gate_b, 1)
                split_hi(*un_gb(i, 2))
                gate_unit(i, 1, U_GB, N_GB, gate_b, 1)
                split_hi(*un_gb(i, 3))
                act.wait_ge(b_h, i + 2)
                act.activation(ml_sq, ml_h, ACT.Square).then_inc(b_sq, 1)
                gate_unit(i, 2, U_GB, N_GB, gate_b, 1)
                split_hi(*un_gb(i, 4))
                if not last:
                    ml_prep(i + 1)
                act.wait_ge(b_ot, i + 1)
                act.copy(qk_all[:, :, ds(i * P, P)], mOT).then_inc(b_otc, 1)
                gate_unit(i, 3, U_GB, N_GB, gate_b, 1)

            with act.Fori(0, TT - 1) as i:
                ml_step(i, False)
            ml_step(TT - 1, True)

            act.wait_ge(gate_stored, 16 + 16 * 2 * KT)
            columns(U_O, NU_O, gating(ACT.Sigmoid, 48, yb_hi, 8))

            un_up = units_of(U_UP, 2)
            with act.Fori(0, 8) as i:
                split_hi(*un_up(i, 1))
                split_hi(*un_up(i, 2))
                for d in range(2):
                    act.wait_ge(m_ready, 2 * i + d + 1)
                    act.copy(h_hi[:, ds(2 * i + d, 1), :].rearrange("p a t -> p (a t)"), m_sum[:, d, :]).then_inc(m_hi, 1)

            un_out = units_of(U_OUT, 4)
            def out_square(i, n):
                if n < TT - 1:
                    act.wait_ge(o_tok_done, 3 * i + n + 1)
                else:
                    act.wait_ge(unit_done, U_OUT + 4 * i + 4 + RING)
                act.wait_ge(o_evac, 4 * i + n + 4)
                act.activation(junk2[:, 0:512], ps[:, n, :], ACT.Square, accum_out=ss[:, ds(4 * n + i, 1)]).then_inc(o_sq, 1)

            with act.Fori(0, 3) as i:
                for q in range(4):
                    split_hi(*un_out(i, q + 1))
                for n in range(TT):
                    out_square(i, n)

            def x1_square(n):
                act.wait_ge(r_x1, n + 1)
                act.wait_ge(o_sq, 15 if n == 0 else 16)
                if n:
                    act.wait_ge(sq_done, TT + n)
                act.activation(junk2, x1[:, n, :], ACT.Square, accum_out=ss2[:, n:n + 1]).then_inc(sq_done, 1)

            for q in range(4):
                split_hi(*un_out(3, q + 1))
            t_banks = (6, 7, 0, 1)
            for n in range(TT - 1):
                out_square(3, n)
            x1_square(0)
            out_square(3, TT - 1)
            turned_hi(TT, t_banks, (0, 1))
            x1_square(1)
            turned_hi(TT, t_banks, (2, 3))
            turned_hi(TT + 1, t_banks)
            split_hi(U_FF + 1, U_FF // 2, 1)
            x1_square(2)
            x1_square(3)
            turned_hi(TT + 2, t_banks)
            turned_hi(TT + 3, t_banks)

            un_ff = units_of(U_FF, FF_UNITS)

            def final_scale(n):
                act.wait_ge(z_r, n + 1)
                act.wait_ge(z_y, 4)
                act.activation(acc[:, n, 0:ZQ], acc[:, n, 0:ZQ], ACT.Copy, scale=rstd[:, n:n + 1]).then_inc(z_sc, 1)

            def mlp_step(i, first=False, last=False):
                u0 = U_FF + FF_UNITS * i
                for f in range(FG):
                    bank = (4, 6, 0, 2)[f]
                    if not (first and f == 0):
                        split_hi(*un_ff(i, 2 * f + 1))
                    act.wait_ge(unit_done, u0 + 2 * f + 1 + RING)
                    act.wait_ge(ff_conv, FG * i + f + 1)
                    act.copy(ff_pad[:, 0, 2:2 + T], ps[:, bank, :]).then_inc(ff_gate, 1)
                    split_hi(*un_ff(i, 2 * f + 2))
                    act.wait_ge(ff_conv, FG * i + f + 2)
                    act.activation(ff_c, ff_c, ACT.Gelu_apprx_tanh).then_inc(ff_gelu, 1)
                    act.wait_ge(ff_mul, FG * i + f + 1)
                    act.copy(act_hi[:, f, :], ff_v).then_inc(ff_hi, 1)
                for d in range(4):
                    if not (last and d == 3):
                        split_hi(*un_ff(i, 2 * FG + d + 1))
                    if last:
                        for n in range(TT):
                            act.wait_ge(dn_evac, 16 + 16 * i + 4 * d + n + 1)
                            if d or n:
                                act.wait_ge(z_sq, 4 * d + n)
                            act.activation(z_junk, acc[:, n, 512 * d:512 * d + 512], ACT.Square,
                                           accum_out=ss[:, 4 * n + d:4 * n + d + 1]).then_inc(z_sq, 1)
                            if d == 3 and n:
                                final_scale(n - 1)

            mlp_step(0, first=True)
            with act.Fori(1, FF_STEPS - 1) as i:
                mlp_step(i)
            mlp_step(FF_STEPS - 1, last=True)
            final_scale(TT - 1)

        @block.gpsimd
        def _(pool):
            pool.memset(ident[:, :], 0.0).then_inc(consts, 1)
            pool.memset(neg_half, -0.5).then_inc(mem_zero, 1)
            pool.wait_ge(consts, 1)
            pool.affine_select(out=ident[:, :], in_=ident[:, :], compare_op=ALU.not_equal, fill=1.0, base=0,
                               pattern=[[-1, P]], channel_multiplier=1).then_inc(consts, 1)

            def tile_rows(v):
                return v.rearrange("l (n p) -> (l n) p", p=P)

            taps = ffn_conv_w.rearrange("l k (n p) -> (l k) n p", p=P)
            rows = [(0, PB, tile_rows(b_in[:, 0:C_IG])), (0, PB_GATES, tile_rows(b_in[:, C_GA:C_GA + 2 * D])),
                    (0, PLB, tile_rows(hg_lb_logits)), (0, PHG, tile_rows(hg_norm)), (0, PML, tile_rows(ml_norm)),
                    (0, PCB, tile_rows(ml_conv_b)), (1, PCW - 128, ml_conv_w.rearrange("l k (n p) -> (l k n) p", p=P)),
                    (1, PFB - 128, tile_rows(ffn_conv_b)), (1, PFW0 - 128, taps[0, :, :]), (2, 0, taps[1, :, :]),
                    (2, FT, taps[2, :, :])]
            def power(n, a=0):
                return pool.tensor_tensor(rstd[:, a:a + n], ms[:, a:a + n], neg_half[:, 0:n], ALU.pow)

            pool.wait_ge(mem_zero, 1)
            for t in range(TT):
                pool.wait_ge(ms_ready, t + 2)
                pool.wait_ge(xn_ready, t + 2)
                power(1).then_inc(rstd_ready, 1)
                if t == 0:
                    for tile, r0, src in rows:
                        pool.dma_start(prow[r0:r0 + src.shape[0], tile, :], src).then_inc(prm_loaded, 16)
                    for k in range(2):
                        pool.dma_start(gbias[32 * k:32 * k + ML_H, :],
                                       b_in[0, C_IG + ML_H * k:C_IG + ML_H * (k + 1)].unsqueeze(1)).then_inc(vg_loaded, 16)
                    pool.dma_start(vbias_hg, row_on_all(b_in, C_I, HG_W)).then_inc(vb_loaded, 16)

            pool.memset(hg_ke0, 0.0)
            pool.memset(hg_ke1, 0.0)
            pool.memset(hg_mask, 1.0).then_inc(consts_v, 1)
            pool.wait_ge(consts_v, 1)
            pool.memset(hg_mask.rearrange("p (c k) -> p c k", k=CHUNK)[:, :, 0:1], 0.0).then_inc(consts_v, 1)
            pool.wait_ge(tok_evac, 4 + 8)
            pool.memset(hg_at, 0.0).then_inc(mem_zero, 1)

            for i in range(TT):
                pool.wait_ge(a_at, 2 * i + 2)
                pool.affine_select(out=heads(hg_at), in_=heads(hg_at), compare_op=ALU.is_ge, fill=0.0, base=0,
                                   pattern=[[0, HG_H], [1, P]], channel_multiplier=-1).then_inc(g_sel, 1)
                pool.wait_ge(v_ms, i + 2)
                power(8).then_inc(g_r, 1)

            pool.wait_ge(p_ot, TT)
            with nc.allow_non_contiguous_dma(reason="few columns of the gates"):
                for a, n, c in COLS_WG:
                    pool.dma_start(wg_raw[:, :, a:a + n], w_in_d[:, :, C_IG + c:C_IG + c + n]).then_inc(wg_loaded, 16)

            pool.wait_ge(y_lo, 1 + 8)
            pool.wait_ge(gate_stored, 16 + 16 * KT)
            pool.dma_start(vbias_ml, row_on_all(b_in, C_V, ML_W)).then_inc(vb_loaded, 16)

            for i in range(TT):
                pool.wait_ge(b_dx, i + 1)
                pool.affine_select(out=heads(ml_d, ML_H), in_=heads(ml_d, ML_H), compare_op=ALU.is_ge, fill=0.0, base=0,
                                   pattern=[[0, ML_H], [1, P]], channel_multiplier=-1).then_inc(b_dm, 1)
                pool.wait_ge(b_dm, 2 * i + 1)
                pool.memset(heads(ml_d, ML_H)[0:CHUNK, :, CHUNK:P], 0.0).then_inc(b_dm, 1)
                pool.wait_ge(b_ms, i + 2)
                power(4).then_inc(b_r, 1)

            pool.wait_ge(gate_stored, 16 + 16 * 2 * KT)
            pool.wait_ge(y_lo, 1 + 16)
            with pool.Fori(0, 4) as i:
                for s in range(2):
                    pool.wait_ge(mg_used, 2 * i + s + 1)
                    for g in range(2):
                        pool.dma_start(m_gates[:, s, g, :, :], gates_d[g, ds(2 * (2 * i + s), 2), :, :]
                                       .rearrange("d p t -> p d t")).then_inc(mg_loaded[s], 16)
            pool.wait_ge(mg_used, 2 + 8)
            pool.wait_ge(m_lo, 1 + KT)
            pool.dma_start(g_post, row_on_all(norm_mix_post, 0, D)).then_inc(gp_loaded, 16)
            for n in range(TT):
                pool.wait_ge(o_evac, 4 + 2 * n + 1)
                pool.dma_start(x_rows[:, n, :], x_d[n * P:(n + 1) * P, :]).then_inc(x2_loaded, 16)
            pool.dma_start(g_pre2, row_on_all(norm_ffn_pre, 0, D)).then_inc(x2_loaded, 16)
            for what, n in (("mix", 0), ("mix", 1), ("x1", 0), ("mix", 2), ("mix", 3), ("x1", 1), ("x1", 2), ("x1", 3)):
                if what == "mix":
                    pool.wait_ge(r_ms, n + 1)
                    power(1, n).then_inc(r_pow, 1)
                else:
                    pool.wait_ge(ms_ready, 1 + TT + n + 1)
                    power(1, 4 + n).then_inc(rstd_ready, 1)
            pool.wait_ge(sq_done, 2 * TT)
            pool.memset(ff_pad[:, 0, 0:2], 0.0).then_inc(z_free, 1)

            def final_add(n):
                pool.wait_ge(z_sc, n + 1)
                pool.tensor_tensor(acc[:, n, 0:ZQ], acc[:, n, 0:ZQ], x1[:, n, 0:ZQ], ALU.add).then_inc(z_o0, 1)

            for n in range(TT):
                pool.wait_ge(z_ms, n + 1)
                power(1, n).then_inc(z_r, 1)
                if n:
                    final_add(n - 1)
            final_add(TT - 1)

        @block.vector
        def _(dve):
            for s_, n in ((lo_ready, RING), (xn_ready, 2), (h_lo_ready, 4), (tok_evac, 4), (ms_ready, 1), (v_ms, 1),
                          (y_mul, 2), (y_lo, 1), (qk_conv_s, 1), (b_ms, 1), (b_h, 1), (mg_used, 2), (up_evac, 2),
                          (ff_conv, 1), (dn_evac, 16)):
                dve.sem_inc(s_, n)

            def split_lo(u, rnd, s):
                dve.wait_ge(hi_ready, u + 1)
                dve.tensor_tensor(w_lo[:, s, :], raw[:, s, :], f32(w_hi[:, s, :]), ALU.subtract).then_inc(lo_ready, 1)

            made = [0]

            def then(ins):
                made[0] += 1
                ins.then_inc(vchain, 1)
                dve.wait_ge(vchain, made[0])

            dve.memset(ones_col, 1.0)
            dve.memset(m_prev[:, 0:1], 0.0)
            dve.memset(nstate, 0.0)

            def row_ms(t, total, a):
                dve.wait_ge(sq_done, t + 1)
                dve.tensor_scalar(ms[:, a:a + 1], total, 1.0 / D, EPS, ALU.mult, ALU.add).then_inc(ms_ready, 1)

            def row_scale(t, src, gain, to, a):
                dve.wait_ge(rstd_ready, t + 1)
                dve.scalar_tensor_tensor(out=to, in0=src, scalar=rstd[:, a:a + 1], in1=gain, op0=ALU.mult,
                                         op1=ALU.mult).then_inc(xn_ready, 1)

            def turned_lo(t, banks):
                n = t % TT
                for g in range(4):
                    dve.wait_ge(h_hi_ready, 4 * t + g + 1)
                    rows, tok = slice(4 * g, 4 * g + 4), slice(n * P, (n + 1) * P)
                    dve.tensor_tensor(h_lo[:, rows, tok], ps[:, banks[g], :].rearrange("p (k t) -> p k t", k=4),
                                      f32(h_hi[:, rows, tok]), ALU.subtract).then_inc(h_lo_ready, 1)

            dve.wait_ge(gain_loaded, 16)
            for t in range(TT):
                row_ms(t, ss[:, 0:1], 0)
                if t > 1:
                    dve.wait_ge(turned, 4 * t + 4)
                row_scale(t, n_x[:, t % 2, :], n_gain, n_xn[:, t % 2, :], 0)
                if t < 2:
                    split_lo(t, 0, t)
                turned_lo(t, (4, 5, 6, 7))
            def columns(first, units, work):
                un = units_of(first, 2)
                with dve.Fori(0, units // 2) as i:
                    for s in range(2):
                        split_lo(*un(i, s + 1))
                        if work:
                            work(2 * i + s, s, i)

            def flat(t, m):
                return t[:, ds(m, 1), :].rearrange("p a t -> p (a t)")

            def f_affine(h, s, i):
                dve.wait_ge(cm_evac, N_F + h + 3)
                dve.tensor_scalar(flat(f_all, h), flat(f_all, h), omlb[:, ds(h, 1)], lb[:, ds(h, 1)], ALU.mult,
                                  ALU.add).then_inc(f_ready, 1)

            def v_block(i, first, v_all, bias, b0, between=None, q0=0):
                un = units_of(first, 4)
                for q in range(q0, 4):
                    split_lo(*un(i, q + 1))
                    if between:
                        between(q)
                for n in range(TT):
                    if n < TT - 1:
                        dve.wait_ge(tok_done, 3 * (b0 + i) + n + 1)
                    else:
                        dve.wait_ge(unit_done, first + 4 * i + 4 + RING)
                    dve.tensor_tensor(v_all[:, n, ds(512 * i, 512)], ps[:, n, :], bias[:, ds(512 * i, 512)],
                                      ALU.add).then_inc(tok_evac, 1)

            def parameters(q):
                if q == 1:
                    dve.wait_ge(prm_turned, 1)
                    then(dve.tensor_copy(prm[:, 0:248], ps[:, 4, 0:248]))
                    dve.tensor_copy(prm[:, 256:344], ps[:, 4, 256:344]).then_inc(prm_ready, 1)
                    then(dve.tensor_tensor(lb_t[:, 0:8], prm[:, PLB:PLB + 8], prm[:, PLB + 8:PLB + 16], ALU.max))
                    then(dve.tensor_tensor(lb_t[:, 8:16], prm[:, PLB:PLB + 8], lb_t[:, 0:8], ALU.subtract))
                    dve.tensor_tensor(lb_t[:, 16:24], prm[:, PLB + 8:PLB + 16], lb_t[:, 0:8], ALU.subtract).then_inc(prm_ready, 1)
                elif q == 3:
                    dve.wait_ge(achain, 1)
                    then(dve.tensor_tensor(lb_t[:, 0:8], lb_t[:, 8:16], lb_t[:, 16:24], ALU.add))
                    then(dve.reciprocal(lb_t[:, 0:8], lb_t[:, 0:8]))
                    then(dve.tensor_tensor(lb, lb_t[:, 8:16], lb_t[:, 0:8], ALU.mult))
                    then(dve.tensor_scalar(omlb, lb, -1.0, 1.0, ALU.mult, ALU.add))

            dve.wait_ge(vb_loaded, 16)
            v_block(0, U_I, v_hg, vbias_hg, 0, q0=1)
            v_block(1, U_I, v_hg, vbias_hg, 0, parameters)
            columns(U_F, NU_F, f_affine)
            def chunks(t):
                return t.rearrange("p (c k) -> p c k", k=CHUNK)

            def hg_prep_b(i):
                dve.wait_ge(a_ln, i + 1)
                dve.tensor_tensor_scan(hg_b[:, 0:T], hg_mask, hg_e3[:, 0:T], 0.0, ALU.mult, ALU.add)
                dve.tensor_tensor_scan(hg_b[:, T:2 * T], hg_mask, hg_e3[:, T:2 * T], 0.0, ALU.mult,
                                       ALU.add).then_inc(v_scan, 1)
                dve.wait_ge(v_scan, i + 1)
                dve.tensor_tensor(chunks(hg_e3), chunks(hg_b)[:, :, CHUNK - 1:CHUNK].broadcast_to([P, 2 * HG_H, CHUNK]),
                                  chunks(hg_b), ALU.subtract).then_inc(v_d3, 1)

            def hg_prep(i, with_q=True):
                dve.wait_ge(a_exp, 3 * i + 3)
                f_pair = f_all[:, :, ds(i * P, P)]
                dve.wait_ge(v_sa, i + 1)
                dve.tensor_copy(dec.rearrange("p h c -> p (h c)").unsqueeze(2), chunks(hg_e1)[:, :, CHUNK - 1:CHUNK])\
                    .then_inc(v_dec, 1)
                for e in (hg_e2, hg_e3):
                    dve.scalar_tensor_tensor(out=heads(e), in0=f_pair, scalar=1.0, in1=heads(e), op0=ALU.subtract,
                                             op1=ALU.mult)
                dve.wait_ge(v_dec, i + 1)
                if with_q:
                    dve.scalar_tensor_tensor(out=heads(hg_e1), in0=q_all[:, :, ds(i * P, P)], scalar=-SCALE,
                                             in1=heads(hg_e1), op0=ALU.mult, op1=ALU.mult).then_inc(v_prep, 1)

            def first_q_dec(h, s, i):
                dve.wait_ge(cm_evac, N_Q + h + 3)
                dve.scalar_tensor_tensor(out=hg_e1[:, ds(h * P, P)], in0=flat(q_all, h)[:, 0:P], scalar=-SCALE,
                                         in1=hg_e1[:, ds(h * P, P)], op0=ALU.mult, op1=ALU.mult).then_inc(v_q0, 1)

            dve.memset(hg_sa, 0.0).then_inc(v_sa, 1)
            dve.wait_ge(consts_v, 2)
            hg_prep_b(0)
            hg_prep(0, False)
            columns(U_Q, NU_Q, first_q_dec)
            dve.wait_ge(v_q0, NU_Q)
            dve.sem_inc(v_prep, 1)
            un_ga = units_of(U_GA, 4)

            def hg_state(new, old, c, update):
                for h in range(HG_H):
                    ins = dve.scalar_tensor_tensor(out=heads(new)[:, h, :], in0=heads(old)[:, h, :], scalar=dec[:, h, c:c + 1],
                                                   in1=update[:, h, :], op0=ALU.mult, op1=ALU.add)
                return ins

            def hg_step(i, last):
                split_lo(*un_ga(i, 1))
                split_lo(*un_ga(i, 2))
                dve.wait_ge(p_u0, i + 1)
                hg_state(hg_sb, hg_sa, 0, hT_).then_inc(v_sb, 1)
                dve.wait_ge(p_u1, i + 1)
                dve.wait_ge(v_sb, i + 1)
                hg_state(hg_sa, hg_sb, 1, hA_).then_inc(v_sa, 1)
                split_lo(*un_ga(i, 3))
                dve.wait_ge(g_sq, i + 1)
                dve.tensor_reduce(ss[:, 0:8], heads(hg_sb), AX.X, ALU.add).then_inc(v_red, 1)
                dve.wait_ge(v_red, i + 1)
                dve.tensor_scalar(ms[:, 0:8], ss[:, 0:8], 1.0 / P, EPS, ALU.mult, ALU.add).then_inc(v_ms, 1)
                if not last:
                    hg_prep_b(i + 1)
                dve.wait_ge(g_r, i + 1)
                dve.tensor_tensor(heads(hg_on), heads(hg_on), rstd[:, 0:8].unsqueeze(2).broadcast_to([P, HG_H, P]),
                                  ALU.mult).then_inc(v_on, 1)
                split_lo(*un_ga(i, 4))
                if not last:
                    hg_prep(i + 1)

            with dve.Fori(0, TT - 1) as i:
                hg_step(i, False)
            hg_step(TT - 1, True)

            def gating(src, gain0, y_h, y_l, n0, cm0, slot_of):
                def work(h, s, i):
                    dve.wait_ge(cm_evac, cm0 + h + 3)
                    dve.wait_ge(y_lo, n0 + h + 1)
                    dve.scalar_tensor_tensor(out=g_y, in0=flat(src, slot_of(s, i)), scalar=prm[:, ds(gain0 + h, 1)],
                                             in1=g_act[:, s, :], op0=ALU.mult, op1=ALU.mult).then_inc(y_mul, 1)
                    dve.wait_ge(y_hi, n0 + h + 1)
                    dve.tensor_tensor(flat(y_l, h), g_y, f32(flat(y_h, h)), ALU.subtract).then_inc(y_lo, 1)
                return work

            dve.wait_ge(a_ot, TT + 1)
            columns(U_G, NU_G, gating(q_all, PHG, ya_hi, ya_lo, 0, N_G, lambda s, i: 2 * i + s))

            then(dve.memset(qk_pre[:, 0:3], 0.0))

            def qk_conv_tile(m, s, i):
                dve.wait_ge(cm_evac, N_QK + m + 3)
                dve.wait_ge(qk_ready, m + 1)
                dve.tensor_scalar(qk_conv, qk_pre[:, 3:3 + T], prm[:, ds(PCW + 24 + m, 1)], prm[:, ds(PCB + m, 1)],
                                  ALU.mult, ALU.add).then_inc(v_conv, 1)
                for n, k in enumerate((2, 1, 0)):
                    dve.wait_ge(v_conv, 3 * m + n + 1)
                    dve.scalar_tensor_tensor(out=qk_conv, in0=qk_pre[:, k:k + T], scalar=prm[:, ds(PCW + 8 * k + m, 1)],
                                             in1=qk_conv, op0=ALU.mult, op1=ALU.add)\
                        .then_inc(qk_conv_s if k == 0 else v_conv, 1)

            dve.sem_inc(qk_ready, 1)
            dve.wait_ge(achain, 2)
            dve.tensor_tensor(wg_lo, wg_raw, f32(wg_hi), ALU.subtract).then_inc(wg_split, 1)
            columns(U_QK, NU_QK, qk_conv_tile)

            NC = T // CHUNK

            def rows_max(c):
                span, end = slice(c * CHUNK, (c + 1) * CHUNK), slice((c + 1) * CHUNK - 1, (c + 1) * CHUNK)
                then(dve.tensor_tensor_scan(row_m[:, span], row_a[:, span], row_a[:, span], m_prev[:, c:c + 1], ALU.max,
                                            ALU.max))
                then(dve.tensor_tensor(m_prev[:, c + 1:c + 2], row_b[:, end], row_m[:, end], ALU.add))

            def rows_step(q):
                if q == 0:
                    then(dve.memset(mask_row, 1.0))
                    then(dve.memset(chunks(mask_row)[:, :, 0:1], 0.0))
                    dve.wait_ge(gates_done, 1)
                    dve.wait_ge(vg_loaded, 32)
                    then(dve.tensor_scalar(row_a, ps[0:ML_H, 4, :], gbias[0:ML_H, :], None, ALU.add))
                    then(dve.tensor_scalar(row_t, ps[32:32 + ML_H, 4, :], gbias[32:32 + ML_H, :], None, ALU.add))
                    dve.scalar_tensor_tensor(out=row_w, in0=row_t, scalar=-1.0, in1=row_t, op0=ALU.mult,
                                             op1=ALU.min).then_inc(r_act, 1)
                elif q == 1:
                    dve.wait_ge(achain, 4)
                    then(dve.scalar_tensor_tensor(out=row_t, in0=row_t, scalar=0.0, in1=row_w, op0=ALU.min,
                                                  op1=ALU.subtract))
                    then(dve.tensor_tensor_scan(row_b, mask_row, row_t, 0.0, ALU.mult, ALU.add))
                    then(dve.tensor_tensor(row_a, row_a, row_b, ALU.subtract))
                elif q == 2:
                    for c in range(NC):
                        rows_max(c)
                else:
                    dve.tensor_tensor(chunks(row_r2), m_prev[:, 0:NC].unsqueeze(2).broadcast_to([ML_H, NC, CHUNK]),
                                      chunks(row_m), ALU.subtract)
                    dve.tensor_tensor(chunks(row_w), chunks(row_a), chunks(row_m)[:, :, CHUNK - 1:CHUNK]
                                      .broadcast_to([ML_H, NC, CHUNK]), ALU.subtract)
                    dve.tensor_tensor(row_r3, row_b, row_m, ALU.add).then_inc(r_act, 1)

            def cols_step(q):
                if q == 3:
                    dve.wait_ge(r_cols, 1)
                    dve.tensor_copy(cols.rearrange("p n k c -> p (n k c)"), ps[:, 4, 0:48]).then_inc(r_cols_sb, 1)

            dve.wait_ge(vb_loaded, 32)
            v_block(0, U_V, v_ml, vbias_ml, 2, rows_step)
            v_block(1, U_V, v_ml, vbias_ml, 2, cols_step)

            hd, kq = heads(ml_d, ML_H), (heads(ml_kw0, ML_H), heads(ml_kw1, ML_H))
            dve.wait_ge(qk_ready, 1 + NU_QK)
            dve.memset(ml_ca, 0.0)
            dve.memset(ml_kw0, 0.0)
            dve.memset(ml_kw1, 0.0).then_inc(b_ca, 1)
            dve.wait_ge(b_ca, 1)
            un_gb = units_of(U_GB, 4)
            decm = mlm[:, 0:8].rearrange("p (h c) -> p h c", c=2)

            def ml_state(new, old, c, n_old, n_new, un0):
                for h in range(ML_H):
                    dve.scalar_tensor_tensor(out=heads(new, ML_H)[:, h, :], in0=heads(old, ML_H)[:, h, :],
                                             scalar=decm[:, h, c:c + 1], in1=mX[:, h, :], op0=ALU.mult, op1=ALU.add)
                for h in range(ML_H):
                    ins = dve.scalar_tensor_tensor(out=nstate[:, n_new + h:n_new + h + 1], in0=nstate[:, n_old + h:n_old + h + 1],
                                                   scalar=decm[:, h, c:c + 1], in1=ps[:, 3, un0 + h:un0 + h + 1],
                                                   op0=ALU.mult, op1=ALU.add)
                return ins

            def ml_step(i, last):
                split_lo(*un_gb(i, 1))
                dve.wait_ge(b_p1, i + 2)
                col = cols[:, ds(i, 1), :, :].rearrange("p n k c -> p (n k) c")
                for h in range(ML_H):
                    ins = dve.tensor_scalar(hd[:, h, :], mM[:, h, :], col[:, 0, h:h + 1], 0.0, ALU.subtract, ALU.max)
                ins.then_inc(b_d, 1)
                dve.tensor_copy(decm, mR.rearrange("p h (c k) -> p h c k", c=2)[:, :, :, CHUNK - 1:CHUNK]
                                .rearrange("p h c k -> p h (c k)"))
                dve.tensor_tensor(heads(ml_q, ML_H), qk_all[:, 0:ML_H, ds(i * P, P)], mR, ALU.mult).then_inc(b_q, 1)
                for c in range(2):
                    a, b = c * CHUNK, (c + 1) * CHUNK
                    ins = dve.tensor_tensor(kq[c][a:b, :, :], mKT[a:b, :, :],
                                            col[a:b, 1, :].unsqueeze(2).broadcast_to([CHUNK, ML_H, P]), ALU.mult)
                ins.then_inc(b_kw, 1)
                dve.wait_ge(b_dm, 2 * i + 2)
                dve.tensor_tensor(hd, mKQ, hd, ALU.mult).then_inc(b_sc, 1)
                split_lo(*un_gb(i, 2))
                dve.wait_ge(b_n0, i + 1)
                ml_state(ml_cb, ml_ca, 0, 0, 4, 4).then_inc(b_cb, 1)
                split_lo(*un_gb(i, 3))
                dve.wait_ge(b_n1, i + 1)
                dve.tensor_scalar(den[:, 0:4], ps[:, 3, 0:4], -1.0, None, ALU.mult).then_inc(b_den, 1)
                dve.wait_ge(b_den, 5 * i + 1)
                dve.tensor_tensor(den[:, 0:4], ps[:, 3, 0:4], den[:, 0:4], ALU.max).then_inc(b_den, 1)
                dve.wait_ge(b_den, 5 * i + 2)
                dve.tensor_tensor(den[:, 0:4], den[:, 0:4], col[:, 2, :], ALU.max).then_inc(b_den, 1)
                dve.wait_ge(b_den, 5 * i + 3)
                dve.reciprocal(den[:, 4:8], den[:, 0:4]).then_inc(b_den, 1)
                dve.wait_ge(b_den, 5 * i + 4)
                dve.tensor_tensor(heads(ml_h, ML_H), mN, den[:, 4:8].unsqueeze(2).broadcast_to([P, ML_H, ML_V]),
                                  ALU.mult).then_inc(b_h, 1)
                dve.wait_ge(b_cb, i + 1)
                ml_state(ml_ca, ml_cb, 1, 4, 0, 8).then_inc(b_ca, 1)
                dve.wait_ge(b_sq, i + 1)
                dve.tensor_reduce(ss[:, 0:4], heads(ml_sq, ML_H), AX.X, ALU.add).then_inc(b_den, 1)
                dve.wait_ge(b_den, 5 * i + 5)
                dve.tensor_scalar(ms[:, 0:4], ss[:, 0:4], 1.0 / ML_V, EPS, ALU.mult, ALU.add).then_inc(b_ms, 1)
                dve.wait_ge(b_r, i + 1)
                dve.tensor_tensor(heads(ml_h, ML_H), heads(ml_h, ML_H),
                                  rstd[:, 0:4].unsqueeze(2).broadcast_to([P, ML_H, ML_V]), ALU.mult).then_inc(b_hn, 1)
                split_lo(*un_gb(i, 4))
                dve.wait_ge(b_ca, i + 2)

            with dve.Fori(0, TT - 1) as i:
                ml_step(i, False)
            ml_step(TT - 1, True)

            dve.wait_ge(b_otc, TT + 1)
            columns(U_O, NU_O, gating(qk_all, PML, yb_hi, yb_lo, 8, N_O, lambda s, i: 4 * s + i))

            un_up = units_of(U_UP, 2)

            def merge(i, j, s):
                split_lo(U_UP + 2 * j + 1, U_UP // 2 + j, 1)
                split_lo(U_UP + 2 * j + 2, U_UP // 2 + j + 1, 0)
                dve.wait_ge(unit_done, U_UP + 2 * j + 2 + RING)
                dve.wait_ge(mg_loaded[s], 32 * i + 32)
                for d in range(2):
                    dve.wait_ge(m_lo, 2 * j + d + 1)
                    dve.tensor_tensor(m_a, ps[:, 4 * s + d, :], m_gates[:, s, 0, d, :], ALU.mult)
                    dve.tensor_tensor(m_b, ps[:, 4 * s + 2 + d, :], m_gates[:, s, 1, d, :], ALU.mult)\
                        .then_inc(v_merge if d == 0 else up_evac, 1)
                    if d == 0:
                        dve.wait_ge(v_merge, j + 1)
                    else:
                        dve.wait_ge(up_evac, j + 3)
                    dve.tensor_tensor(m_sum[:, d, :], m_a, m_b, ALU.add).then_inc(m_ready, 1)
                    dve.wait_ge(m_hi, 2 * j + d + 1)
                    dve.tensor_tensor(flat(h_lo, 2 * j + d), m_sum[:, d, :], f32(flat(h_hi, 2 * j + d)),
                                      ALU.subtract).then_inc(m_lo, 1)
                dve.sem_inc(mg_used, 1)

            dve.sem_inc(m_lo, 1)
            with dve.Fori(0, 4) as i:
                for s in range(2):
                    merge(i, 2 * i + s, s)

            un_out = units_of(U_OUT, 4)
            def out_evac(i, n):
                dve.wait_ge(o_sq, 4 * i + n + 1)
                dve.tensor_tensor(x1[:, n, ds(512 * i, 512)], ps[:, n, :], g_post[:, ds(512 * i, 512)], ALU.mult)\
                    .then_inc(o_evac, 1)

            with dve.Fori(0, 3) as i:
                for q in range(4):
                    split_lo(*un_out(i, q + 1))
                dve.wait_ge(gp_loaded, 16)
                for n in range(TT):
                    out_evac(i, n)
            for q in range(4):
                split_lo(*un_out(3, q + 1))

            def mix_ms(n):
                out_evac(3, n)
                then(dve.tensor_reduce(ms[:, n:n + 1], ss[:, 4 * n:4 * n + 4], AX.X, ALU.add))
                dve.tensor_scalar(ms[:, n:n + 1], ms[:, n:n + 1], 1.0 / D, EPS, ALU.mult, ALU.add).then_inc(r_ms, 1)

            def x1_rows(n):
                dve.wait_ge(r_pow, n + 1)
                dve.wait_ge(o_evac, 4 + 12 + n + 1)
                dve.scalar_tensor_tensor(out=x1[:, n, :], in0=x1[:, n, :], scalar=rstd[:, n:n + 1], in1=x_rows[:, n, :],
                                         op0=ALU.mult, op1=ALU.add).then_inc(r_x1, 1)

            def x1_norm(n):
                row_ms(TT + n, ss2[:, n:n + 1], 4 + n)
                row_scale(TT + n, x1[:, n, :], g_pre2, x_rows[:, n, :], 4 + n)

            t_banks = (6, 7, 0, 1)
            dve.wait_ge(x2_loaded, 16 * (TT + 1))
            mix_ms(0)
            x1_rows(0)
            mix_ms(1)
            x1_norm(0)
            x1_rows(1)
            mix_ms(2)
            mix_ms(3)
            x1_norm(1)
            turned_lo(TT, t_banks)
            turned_lo(TT + 1, t_banks)
            x1_rows(2)
            split_lo(U_FF + 1, U_FF // 2, 1)
            x1_norm(2)
            x1_rows(3)
            x1_norm(3)
            turned_lo(TT + 2, t_banks)
            turned_lo(TT + 3, t_banks)

            un_ff = units_of(U_FF, FF_UNITS)

            def mlp_step(i, first=False, last=False):
                u0 = U_FF + FF_UNITS * i
                for f in range(FG):
                    bank = (4, 6, 0, 2)[f]
                    t = FG * i + f
                    if not (first and f == 0):
                        split_lo(*un_ff(i, 2 * f + 1))
                    split_lo(*un_ff(i, 2 * f + 2))
                    dve.wait_ge(ff_gate, t + 1)
                    dve.tensor_scalar(ff_c, ff_pad[:, 0, 2:2 + T], prm[:, ds(PFW1 + FT + t, 1)], prm[:, ds(PFB + t, 1)],
                                      ALU.mult, ALU.add).then_inc(ff_chain, 1)
                    dve.wait_ge(ff_chain, 2 * t + 1)
                    dve.scalar_tensor_tensor(out=ff_c, in0=ff_pad[:, 0, 1:1 + T], scalar=prm[:, ds(PFW1 + t, 1)], in1=ff_c,
                                             op0=ALU.mult, op1=ALU.add).then_inc(ff_chain, 1)
                    dve.wait_ge(ff_chain, 2 * t + 2)
                    dve.scalar_tensor_tensor(out=ff_c, in0=ff_pad[:, 0, 0:T], scalar=prm[:, ds(PFW0 + t, 1)], in1=ff_c,
                                             op0=ALU.mult, op1=ALU.add).then_inc(ff_conv, 1)
                    dve.wait_ge(ff_gelu, t + 1)
                    dve.wait_ge(unit_done, u0 + 2 * f + 2 + RING)
                    dve.tensor_tensor(ff_v, ps[:, bank + 1, :], ff_c, ALU.mult).then_inc(ff_mul, 1)
                    dve.wait_ge(ff_hi, t + 1)
                    dve.tensor_tensor(act_lo[:, f, :], ff_v, f32(act_hi[:, f, :]), ALU.subtract).then_inc(ff_lo, 1)
                    dve.wait_ge(ff_lo, t + 1)
                for d in range(4):
                    if not (last and d == 3):
                        split_lo(*un_ff(i, 2 * FG + d + 1))
                    b0 = 4 if d % 2 == 0 else 0
                    for n in range(TT):
                        if n < TT - 1:
                            dve.wait_ge(dn_done, 3 * (4 * i + d) + n + 1)
                        else:
                            dve.wait_ge(unit_done, u0 + 2 * FG + d + 1 + RING)
                        part = acc[:, n, 512 * d:512 * d + 512]
                        if first:
                            dve.tensor_copy(part, ps[:, b0 + n, :]).then_inc(dn_evac, 1)
                        else:
                            dve.tensor_tensor(part, part, ps[:, b0 + n, :], ALU.add).then_inc(dn_evac, 1)
                        if last and d == 3 and n:
                            final_rows(n - 1)
                    if last and d == 1:
                        final_gain(0)
                    if last and d == 2:
                        final_gain(1)
                        final_gain(2)

            def final_gain(d, tiles=range(TT)):
                for n in tiles:
                    dve.wait_ge(z_sq, 4 * d + n + 1)
                    dve.wait_ge(gf_loaded, 16)
                    part = acc[:, n, 512 * d:512 * d + 512]
                    dve.tensor_tensor(part, part, z_gain[:, 512 * d:512 * d + 512], ALU.mult).then_inc(z_y, 1)

            def final_rows(n):
                dve.wait_ge(z_sq, 12 + n + 1)
                then(dve.tensor_reduce(ms[:, n:n + 1], ss[:, 4 * n:4 * n + 4], AX.X, ALU.add))
                dve.tensor_scalar(ms[:, n:n + 1], ms[:, n:n + 1], 1.0 / D, EPS, ALU.mult, ALU.add).then_inc(z_ms, 1)
                final_gain(3, (n,))
                dve.wait_ge(z_r, n + 1)
                dve.wait_ge(z_y, 12 + n + 1)
                dve.scalar_tensor_tensor(out=acc[:, n, ZQ:D], in0=acc[:, n, ZQ:D], scalar=rstd[:, n:n + 1],
                                         in1=x1[:, n, ZQ:D], op0=ALU.mult, op1=ALU.add).then_inc(z_o, 1)

            dve.wait_ge(z_free, 1)
            mlp_step(0, first=True)
            dve.wait_ge(dn_evac, 16 * 2)
            with dve.Fori(1, FF_STEPS - 1) as i:
                mlp_step(i)
                dve.wait_ge(dn_evac, 16 * (i + 2))
            mlp_step(FF_STEPS - 1, last=True)
            final_rows(TT - 1)


_INS = ["x", "norm_mix_pre", "norm_mix_post", "norm_ffn_pre", "norm_ffn_post", "w_in", "b_in", "hg_lb_logits", "hg_norm",
        "ml_conv_w", "ml_conv_b", "ml_norm", "w_up_a", "w_up_b", "w_out", "ffn_w_gate", "ffn_w_up", "ffn_conv_w",
        "ffn_conv_b", "ffn_w_down"]
_OUT_SHAPE = (1, T, D)


def kernel(**inputs):
    import numpy as np
    import concourse.bacc as bacc
    from concourse.bass_utils import run_bass_kernel_spmd

    nc = bacc.Bacc("TRN2", target_bir_lowering=False, num_devices=1)
    arrays, args = {}, []
    for name in _INS:
        a = np.ascontiguousarray(inputs[name])
        arrays[f"in_{name}"] = a
        args.append(nc.dram_tensor(f"in_{name}", a.shape, mybir.dt.from_np(a.dtype), kind="ExternalInput").ap())
    args.append(nc.dram_tensor("out", _OUT_SHAPE, F32, kind="ExternalOutput").ap())
    build(nc, *args)
    r = run_bass_kernel_spmd(nc, [arrays], core_ids=[0])
    return r.results[0]["out"]
```

```python
from contextlib import ExitStack

import concourse.bass as bass
from concourse import mybir

ALU = mybir.AluOpType
ACT = mybir.ActivationFunctionType
AX = mybir.AxisListType
F32 = mybir.dt.float32
F32R = mybir.dt.float32r
ds = bass.ds


P = 128
D = 2048
T = 512
KT = D // P
TT = T // P
CHUNK = 64
HG_H, HG_W = 8, 1024
ML_H, ML_V, ML_W = 4, 256, 1024
FF = 5632
FT = FF // P
FG = 4
EPS = 1e-6
SCALE = float(P) ** -0.5

C_Q, C_F, C_I, C_G, C_QK, C_V, C_O, C_IG, C_GA, C_GB = 0, 1024, 2048, 3072, 4096, 5120, 6144, 7168, 7176, 9224

U = 2048
RING = 2
NU_F, NU_Q, NU_I, NU_GA, NU_G, NU_QK, NU_V, NU_GB, NU_O, NU_UP, NU_OUT = 8, 8, 8, 16, 8, 8, 8, 16, 8, 16, 20
U_I = 0
U_F = U_I + NU_I
U_Q = U_F + NU_F
U_GA = U_Q + NU_Q
U_G = U_GA + NU_GA
U_QK = U_G + NU_G
U_V = U_QK + NU_QK
U_GB = U_V + NU_V
U_O = U_GB + NU_GB
U_UP = U_O + NU_O
U_OUT = U_UP + NU_UP
U_FF = U_OUT + NU_OUT
FF_UNITS = 3 * FG
FF_STEPS = FT // FG
UNITS = U_FF + FF_UNITS * FF_STEPS + 4
HALVES = ((0, 1), (2, 3))

N_F, N_Q, N_GA, N_G, N_QK, N_GB, N_O = 0, 8, 16, 32, 40, 48, 64

PB = 0
PB_GATES = 56
PLB = 88
PHG = 104
PML = 112
PCB = 120
PCW = 128
PFB = 160
PFW0 = 204
PFW1 = 256


def build(nc, x, norm_mix_pre, norm_mix_post, norm_ffn_pre, norm_ffn_post, w_in, b_in, hg_lb_logits, hg_norm,
          ml_conv_w, ml_conv_b, ml_norm, w_up_a, w_up_b, w_out, ffn_w_gate, ffn_w_up, ffn_conv_w, ffn_conv_b,
          ffn_w_down, out):
    x_d = x.rearrange("b t d -> (b t) d")
    out_d = out.rearrange("b t d -> (b t) d")

    def ktiles(w):
        return w.rearrange("l (j p) n -> p (l j) n", p=P)

    w_in_d, w_out_d, w_gate_d, w_up_d, w_down_d = map(ktiles, (w_in, w_out, ffn_w_gate, ffn_w_up, ffn_w_down))
    up_a_d, up_b_d = ktiles(w_up_a), ktiles(w_up_b)

    def row_on_all(v, a, n):
        return v[0:1, a:a + n].broadcast_to([P, n])

    gates_d = nc.dram_tensor("merge_gates", (2, KT, P, T), F32).ap()

    with ExitStack() as ctx:
        def sb(name, shape, dt=F32):
            return ctx.enter_context(nc.sbuf_tensor(name, shape, dt))

        def sem(name):
            return ctx.enter_context(nc.semaphore(name))

        h_hi = sb("h_hi", [P, KT, T], F32R)
        h_lo = sb("h_lo", [P, KT, T], F32R)
        raw = sb("raw", [P, RING, U])
        w_hi = sb("w_hi", [P, RING, U], F32R)
        w_lo = sb("w_lo", [P, RING, U], F32R)
        prm = sb("prm", [P, 384])
        ident = sb("ident", [P, P])
        small = sb("small", [P, 264])
        KB = 256
        ARENA = 92 * KB + KB // 2
        with nc.sbuf_tensor("arena", [P, ARENA], F32) as t:
            arena = t
        with ExitStack() as over:
            def at(name, kb):
                return over.enter_context(nc.sbuf_tensor(name, [P, kb * KB], F32R))
            yb_hi, ya_hi, ya_lo = (at(n, 16) for n in ("yb_hi", "ya_hi", "ya_lo"))
            at("gap1", 16)
            yb_lo = at("yb_lo", 16)
        with ExitStack() as over:
            def at(name, kb):
                return over.enter_context(nc.sbuf_tensor(name, [P, kb * KB], F32R))
            at("gap2", 64)
            act_hi, act_lo = at("act_hi", 8), at("act_lo", 8)
        ctx.enter_context(nc.sbuf_tensor("arena_keep", [P, ARENA], F32))

        def tiles(t):
            return t[:, :].rearrange("p (j t) -> p j t", t=T)
        yb_lo_flat = yb_lo
        ya_hi, ya_lo, yb_hi, yb_lo, act_hi, act_lo = map(tiles, (ya_hi, ya_lo, yb_hi, yb_lo, act_hi, act_lo))

        def ar(kb, n):
            a = int(kb * KB)
            return arena[:, a:a + n]

        def f32(r):
            return r.bitcast(F32)

        n_x = ar(0, 2 * D).rearrange("p (s d) -> p s d", s=2)
        n_gain = ar(16, D)
        n_xn = ar(24, 2 * D).rearrange("p (s d) -> p s d", s=2)
        n_junk = ar(40, D)
        prow = ar(48, 3 * P).rearrange("p (s c) -> p s c", s=3)
        q_all = ar(0, HG_H * T).rearrange("p (h t) -> p h t", h=HG_H)
        f_all = ar(16, HG_H * T).rearrange("p (h t) -> p h t", h=HG_H)
        v_hg = ar(32, TT * HG_W).rearrange("p (n c) -> p n c", n=TT)
        W8 = HG_H * P
        hg_b, hg_on, hg_e1, hg_e2, hg_e3, hg_at, hg_ke0, hg_ke1, hg_sa, hg_sb = (
            ar(48 + 4 * i, W8) for i in range(10))
        hg_mask = ar(88, T)
        gate_a = ar(90, T)
        vbias_hg = hg_at

        def heads(t, h=HG_H):
            return t.rearrange("p (h c) -> p h c", h=h)
        qk_all = ar(48, 8 * T).rearrange("p (m t) -> p m t", m=8)
        v_ml = ar(64, TT * ML_W).rearrange("p (n c) -> p n c", n=TT)
        row_m, row_r2, row_b, row_a, row_w, row_r3, row_t = (arena[0:ML_H, i * T:(i + 1) * T] for i in range(7))
        ml_k, ml_q, ml_d, ml_kw = (ar(4 + 2 * i, T) for i in range(4))
        ml_sq = ar(4, ML_W)
        ml_c, ml_h = ar(80, ML_W), ar(88, ML_W)
        mask_row = arena[0:ML_H, 14 * KB:14 * KB + T]
        vbias_ml = ml_h
        wg_raw = ar(48, KT * P).rearrange("p (j n) -> p j n", j=KT)
        wg_hi, wg_lo = (yb_lo_flat[:, s * KT * P:(s + 1) * KT * P].rearrange("p (j n) -> p j n", j=KT) for s in range(2))
        COLS_WG = ((0, 32, 0), (32, 32, ML_H), (64, 64, 2 * ML_H))
        qk_pre = ar(80, T + 3)
        qk_conv = ar(83, T)
        g_act = ar(80, 2 * T).rearrange("p (s t) -> p s t", s=2)
        g_y = ar(84, T)
        gate_b = ar(14, T)
        m_gates = ar(48, 8 * T).rearrange("p (s g d t) -> p s g d t", s=2, g=2, d=2)
        m_a = ar(80, T)
        m_b = ar(82, T)
        m_sum = ar(84, 2 * T).rearrange("p (s t) -> p s t", s=2)
        x1 = ar(0, TT * D).rearrange("p (n d) -> p n d", n=TT)
        acc = ar(32, TT * D).rearrange("p (n d) -> p n d", n=TT)
        g_pre2 = ar(32, D)
        x_rows = ar(40, TT * D).rearrange("p (n d) -> p n d", n=TT)
        g_post = ar(72, D)
        junk2 = ar(80, D)
        ff_pad = ar(80, 2 * (T + 2)).rearrange("p (s t) -> p s t", s=2)
        ff_c = ar(84.5, T)
        ff_v = ar(86.5, T)
        z_gain = ar(80, D)
        z_junk = ar(88.5, 512)

        lb = small[:, 0:8]
        omlb = small[:, 8:16]
        lb_t = small[:, 16:40]
        gbias = small[:, 72:73]
        cols = small[:, 128:176].rearrange("p (n k c) -> p n k c", n=TT, k=3)
        ss = small[:, 176:192]
        ms = small[:, 192:200]
        rstd = small[:, 200:208]
        neg_half = small[:, 208:216]
        dec = small[:, 216:232].rearrange("p (h c) -> p h c", c=2)
        den = small[:, 232:240]
        ones_col = small[:, 240:242]
        nstate = small[:, 242:246]
        decm = small[:, 250:254]
        ss2 = small[:, 260:264]
        m_prev = sb("m_prev", [ML_H, TT + 1])

        ps = ctx.enter_context(nc.psum_tensor("ps", [P, 8, 512], F32))

        def bank2(b, h):
            return ps[:, b:b + 2, :].rearrange("p b c -> p (b c)").rearrange("p (h c) -> p h c", h=h)
        hT_, hA_, hO_ = bank2(0, HG_H), bank2(2, HG_H), bank2(4, HG_H)
        mX, mN = bank2(0, ML_H), bank2(4, ML_H)
        mKQ = ps[:, 0, :].rearrange("p (h c) -> p h c", h=ML_H)
        mKT = ps[:, 1, :].rearrange("p (h c) -> p h c", h=ML_H)
        mM = ps[:, 2, :].rearrange("p (h c) -> p h c", h=ML_H)
        mR = ps[:, 3, :].rearrange("p (h c) -> p h c", h=ML_H)
        mOT = bank2(0, 8)

        def sems(names):
            return [sem(name) for name in names.split()]

        raw_loaded = sems("raw_loaded0 raw_loaded1")
        hi_ready, lo_ready, unit_done = sems("hi_ready lo_ready unit_done")
        cm_evac, = sems("cm_evac")
        tok_done, tok_evac = sems("tok_done tok_evac")
        act_step, dve_step = sems("act_step dve_step")
        gain_loaded, prm_loaded, gbias_loaded, vbias_loaded = sems("gain_loaded prm_loaded gbias_loaded vbias_loaded")
        consts, mem_zero, hg_mask_ready = sems("consts mem_zero hg_mask_ready")
        prm_turned, prm_ready = sems("prm_turned prm_ready")
        x_loaded = sems("x_loaded0 x_loaded1")
        sq_done, ms_ready, rstd_ready = sems("sq_done ms_ready rstd_ready")
        xn_ready, turned = sems("xn_ready turned")
        h_hi_ready, h_lo_ready = sems("h_hi_ready h_lo_ready")
        f_ready, q_dec_first = sems("f_ready q_dec_first")
        logf_ready, logf_sums, logf_to_end, exp_ready, hg_prepared, decay_kept = sems(
            "logf_ready logf_sums logf_to_end exp_ready hg_prepared decay_kept")
        hg_scores_done, hg_scores_copied, hg_scores_masked, k_end_copied = sems(
            "hg_scores_done hg_scores_copied hg_scores_masked k_end_copied")
        hg_update0, hg_mid_state, hg_update1, hg_out_done, hg_new_state = sems(
            "hg_update0 hg_mid_state hg_update1 hg_out_done hg_new_state")
        hg_out_copied, hg_squares, hg_sums, hg_ms_ready, hg_rstd_ready = sems(
            "hg_out_copied hg_squares hg_sums hg_ms_ready hg_rstd_ready")
        hg_normed, hg_out_turned, hg_out_kept = sems("hg_normed hg_out_turned hg_out_kept")
        gate_stored, = sems("gate_stored")
        y_mul, y_hi, y_lo = sems("y_mul y_hi y_lo")
        conv_tap, qk_conv_done, qk_ready = sems("conv_tap qk_conv_done qk_ready")
        wg_loaded, wg_split, gates_done, rows_ready, rows_exp, cols_turned = sems(
            "wg_loaded wg_split gates_done rows_ready rows_exp cols_turned")
        ml_keys_ready, ml_scores_done, ml_exponents, ml_weights_ready, ml_weights_masked = sems(
            "ml_keys_ready ml_scores_done ml_exponents ml_weights_ready ml_weights_masked")
        ml_scores_ready, ml_queries_ready, ml_weighted_keys = sems("ml_scores_ready ml_queries_ready ml_weighted_keys")
        ml_out_done, den_step, ml_sums_decayed, ml_new_state = sems("ml_out_done den_step ml_sums_decayed ml_new_state")
        ml_h_ready, ml_squares, ml_ms_ready, ml_rstd_ready = sems(
            "ml_h_ready ml_squares ml_ms_ready ml_rstd_ready")
        ml_normed, ml_out_turned, ml_out_kept = sems("ml_normed ml_out_turned ml_out_kept")
        mg_loaded = sems("mg_loaded0 mg_loaded1")
        mg_used, up_evac, merge_mul = sems("mg_used up_evac merge_mul")
        m_ready, m_hi, m_lo = sems("m_ready m_hi m_lo")
        o_tok_done, o_sq, o_evac = sems("o_tok_done o_sq o_evac")
        g_post_loaded, x2_loaded = sems("g_post_loaded x2_loaded")
        mix_ms_ready, mix_rstd_ready, x1_ready = sems("mix_ms_ready mix_rstd_ready x1_ready")
        ff_gate, ff_chain, ff_conv, ff_gelu, ff_mul, ff_hi, ff_lo = sems(
            "ff_gate ff_chain ff_conv ff_gelu ff_mul ff_hi ff_lo")
        pad_zero, = sems("pad_zero")
        down_done, down_evac = sems("down_done down_evac")
        z_gain_loaded, fin_squares, fin_ms_ready, fin_rstd_ready = sems(
            "z_gain_loaded fin_squares fin_ms_ready fin_rstd_ready")
        fin_gain_pool, fin_gain_dve, fin_scaled, fin_done_pool, fin_done_dve, out_stored = sems(
            "fin_gain_pool fin_gain_dve fin_scaled fin_done_pool fin_done_dve out_stored")

        block = ctx.enter_context(nc.Block())

        ZQ, ZM = D // 4, 5 * D // 8

        @block.sync
        def _(sp):
            def load(u, s, src):
                sp.wait_ge(lo_ready, u + 1)
                j, n = src.shape[1], src.shape[2]
                sp.dma_start(raw[:, s, :].rearrange("p (j n) -> p j n", j=j), src).then_inc(raw_loaded[s], 16)
                assert j * n == U

            def columns(first, units, w, c0, width=P):
                with sp.Fori(0, units // 2) as i:
                    for s in range(2):
                        load(first + 2 * i + s, s, w[:, :, ds(c0 + width * (2 * i + s), width)])

            def blocks(first, n, w, c0):
                with sp.Fori(0, n) as i:
                    for q in range(4):
                        load(first + 4 * i + q, q % 2, w[:, 4 * q:4 * q + 4, ds(c0 + 512 * i, 512)])

            def load_x(t):
                sp.wait_ge(xn_ready, t + 1)
                sp.dma_start(n_x[:, t % 2, :], x_d[t * P:(t + 1) * P, :]).then_inc(x_loaded[t % 2], 16)

            def load_i(i, q):
                load(U_I + 4 * i + q, q % 2, w_in_d[:, 4 * q:4 * q + 4, C_I + 512 * i:C_I + 512 * i + 512])

            load_x(0)
            sp.dma_start(n_gain, row_on_all(norm_mix_pre, 0, D)).then_inc(gain_loaded, 16)
            load_i(0, 0)
            load_x(1)
            load_i(0, 1)
            load_x(2)
            load_x(3)
            for i in range(2):
                for q in range(4):
                    if i or q > 1:
                        load_i(i, q)
            columns(U_F, NU_F, w_in_d, C_F)
            columns(U_Q, NU_Q, w_in_d, C_Q)
            columns(U_GA, NU_GA, w_in_d, C_GA)
            columns(U_G, NU_G, w_in_d, C_G)
            columns(U_QK, NU_QK, w_in_d, C_QK)
            blocks(U_V, 2, w_in_d, C_V)
            columns(U_GB, NU_GB, w_in_d, C_GB)
            columns(U_O, NU_O, w_in_d, C_O)
            with sp.Fori(0, 8) as i:
                load(U_UP + 2 * i, 0, up_a_d[:, :, ds(256 * i, 256)])
                load(U_UP + 2 * i + 1, 1, up_b_d[:, :, ds(256 * i, 256)])
            blocks(U_OUT, 4, w_out_d, 0)
            for q in range(4):
                load(U_OUT + 16 + q, q % 2, w_out_d[:, 4 * q:4 * q + 4, 3 * 512:D])
            with sp.Fori(0, FF_STEPS) as i:
                for f in range(FG):
                    load(U_FF + FF_UNITS * i + 2 * f, 0, w_gate_d[:, :, ds((FG * i + f) * P, P)])
                    load(U_FF + FF_UNITS * i + 2 * f + 1, 1, w_up_d[:, :, ds((FG * i + f) * P, P)])
                for d in range(4):
                    load(U_FF + FF_UNITS * i + 2 * FG + d, d % 2, w_down_d[:, ds(FG * i, FG), 512 * d:512 * d + 512])
            sp.wait_ge(ff_lo, FT)
            sp.dma_start(z_gain, row_on_all(norm_ffn_post, 0, D)).then_inc(z_gain_loaded, 16)
            for d in range(4):
                load(UNITS - 4 + d, d % 2, w_down_d[:, FT - FG:FT, 512 * d:512 * d + 512])
            for n in range(TT):
                for a, b, done, count in ((ZQ, ZM, fin_done_dve, 2 * n + 1), (0, ZQ, fin_done_pool, n + 1),
                                          (ZM, D, fin_done_dve, 2 * n + 2)):
                    sp.wait_ge(done, count)
                    sp.dma_start(out_d[n * P:(n + 1) * P, a:b], acc[:, n, a:b]).then_inc(out_stored, 16)
            sp.wait_ge(out_stored, 16 * 3 * TT)

        @block.tensor
        def _(pe):
            pe.sem_inc(unit_done, RING)
            pe.sem_inc(turned, 8)
            for credit in (hg_scores_done, hg_out_done, ml_scores_done):
                pe.sem_inc(credit, 1)

            def split_ready(u, part):
                if part == 0:
                    pe.wait_ge(hi_ready, u + 1)
                else:
                    pe.wait_ge(lo_ready, u + 1 + RING)

            def cm_unit(u, n, s, k_hi=h_hi, k_lo=h_lo):
                pe.wait_ge(cm_evac, n + 1)
                w = [t[:, s, :].rearrange("p (j n) -> p j n", j=KT) for t in (w_hi, w_lo)]
                split_ready(u, 0)
                for k in (k_hi, k_lo):
                    for j in range(KT):
                        pe.matmul(ps[:, 6 + s, :], w[0][:, j, :], k[:, j, :], start=(k is k_hi and j == 0), stop=False)
                split_ready(u, 1)
                for j in range(KT):
                    last = pe.matmul(ps[:, 6 + s, :], w[1][:, j, :], k_hi[:, j, :], start=False, stop=(j == KT - 1))
                last.then_inc(unit_done, 1)

            def cm_phase(first, n0, units):
                with pe.Fori(0, units // 2) as i:
                    for s in range(2):
                        cm_unit(first + 2 * i + s, n0 + 2 * i + s, s)

            def tm_products(b0, s, k_hi, k_lo, j0, nj, first, last, before, done, tiles=range(TT)):
                w = [t[:, s, :].rearrange("p (j n) -> p j n", j=nj) for t in (w_hi, w_lo)]
                for n in tiles:
                    if first:
                        before(n)
                    for j in range(nj):
                        tok = slice(n * P, n * P + P)
                        pe.matmul(ps[:, b0 + n, :], k_hi[:, j0 + j, tok], w[0][:, j, :], start=(first and j == 0), stop=False)
                        pe.matmul(ps[:, b0 + n, :], k_hi[:, j0 + j, tok], w[1][:, j, :], start=False, stop=False)
                        mm = pe.matmul(ps[:, b0 + n, :], k_lo[:, j0 + j, tok], w[0][:, j, :], start=False,
                                       stop=(last and j == nj - 1))
                    if last:
                        mm.then_inc(done if n != tiles[-1] else unit_done, 1)
                if not last:
                    mm.then_inc(unit_done, 1)

            def tm_block(u0, evac, e0, done, between=None):
                for q in range(4):
                    if between:
                        between(q)
                    split_ready(u0 + q, 0)
                    split_ready(u0 + q, 1)
                    tm_products(0, q % 2, h_hi, h_lo, 4 * q, 4, q == 0, q == 3,
                                lambda n: pe.wait_ge(evac, e0 + n + 1), done)

            pe.wait_ge(consts, 2)

            def turn_tokens(rows, t, banks):
                pe.wait_ge(xn_ready, 2 + t + 1)
                for g in range(4):
                    pe.wait_ge(h_lo_ready, 4 * t + g + 1)
                    for k in range(4):
                        mm = pe.transpose(ps[:, banks[g], k * P:(k + 1) * P], rows[:, (4 * g + k) * P:(4 * g + k + 1) * P],
                                          ident[:, :])
                    mm.then_inc(turned, 1)

            def first_units(n, q):
                split_ready(q, 0)
                split_ready(q, 1)
                pe.wait_ge(h_lo_ready, 4 + 4 * n + 4)
                w = [t[:, q, :].rearrange("p (j n) -> p j n", j=4) for t in (w_hi, w_lo)]
                tok = slice(n * P, n * P + P)
                for j in range(4):
                    for a, b in ((h_hi, 0), (h_hi, 1), (h_lo, 0)):
                        mm = pe.matmul(ps[:, n, :], a[:, 4 * q + j, tok], w[b][:, j, :],
                                       start=(q == 0 and j == 0 and a is h_hi and b == 0), stop=False)
                if n == TT - 1:
                    mm.then_inc(unit_done, 1)

            for n in range(TT):
                turn_tokens(n_xn[:, n % 2, :], n, (4, 5, 6, 7))
                if n:
                    first_units(n - 1, 1)
                first_units(n, 0)
            first_units(TT - 1, 1)
            for q in (2, 3):
                split_ready(q, 0)
                split_ready(q, 1)
                tm_products(0, q % 2, h_hi, h_lo, 4 * q, 4, False, q == 3, None, tok_done)
            pe.wait_ge(h_lo_ready, 4 + 16)
            pe.wait_ge(prm_loaded, 16 * 11)
            pe.transpose(ps[:, 4, 0:128], prow[:, 0, :], ident[:, :])
            pe.transpose(ps[:, 4, 128:248], prow[0:120, 1, :], ident[0:120, 0:120])
            pe.transpose(ps[:, 4, 256:344], prow[0:88, 2, :], ident[0:88, 0:88]).then_inc(prm_turned, 1)
            tm_block(U_I + 4, tok_evac, 4, tok_done)

            cm_phase(U_F, N_F, NU_F)
            cm_phase(U_Q, N_Q, NU_Q)

            pe.wait_ge(tok_evac, 4 + 8)
            qd, ki, ke = heads(hg_e1), heads(hg_e2), heads(hg_e3)
            at_, ke0, ke1, sa, sb_, on = map(heads, (hg_at, hg_ke0, hg_ke1, hg_sa, hg_sb, hg_on))
            with pe.Fori(0, TT) as i:
                def unit(s):
                    cm_unit(U_GA + 4 * i + s, N_GA + 4 * i + s, s % 2)
                pe.wait_ge(hg_prepared, i + 1)
                pe.wait_ge(hg_out_kept, i + 1)
                for h in range(HG_H):
                    pe.transpose(hT_[:, h, :], ke[:, h, :], ident[:, :])
                pe.wait_ge(hg_new_state, i + 1)
                for h in range(HG_H):
                    mm = pe.matmul(hA_[:, h, :], ki[:, h, :], qd[:, h, :], start=True, stop=True)
                mm.then_inc(hg_scores_done, 1)
                unit(0)
                pe.wait_ge(k_end_copied, 2 * i + 2)
                for h in range(HG_H):
                    mm = pe.matmul(hT_[:, h, :], ke0[:, h, :], v_hg[:, ds(i, 1), h * P:(h + 1) * P], start=True, stop=True)
                mm.then_inc(hg_update0, 1)
                pe.wait_ge(hg_scores_masked, i + 1)
                pe.wait_ge(hg_out_copied, i + 1)
                for h in range(HG_H):
                    pe.matmul(hO_[:, h, :], at_[:, h, :], v_hg[:, ds(i, 1), h * P:(h + 1) * P],
                              start=(h % 4 == 0), stop=False, skip_group_check=True)
                for h in range(HG_H):
                    pe.matmul(hO_[0:CHUNK, h, :], qd[:, h, 0:CHUNK], sa[:, h, :], start=False, stop=False,
                                   skip_group_check=True)
                for h in range(HG_H):
                    mm = pe.matmul(hA_[:, h, :], ke1[:, h, :], v_hg[:, ds(i, 1), h * P:(h + 1) * P], start=True, stop=True)
                mm.then_inc(hg_update1, 1)
                unit(1)
                pe.wait_ge(hg_mid_state, i + 1)
                for h in range(HG_H):
                    mm = pe.matmul(hO_[CHUNK:P, h, :], qd[:, h, CHUNK:P], sb_[:, h, :], start=False, stop=True,
                                   skip_group_check=True)
                mm.then_inc(hg_out_done, 1)
                unit(2)
                pe.wait_ge(hg_normed, i + 1)
                for h in range(HG_H):
                    mm = pe.transpose(hT_[:, h, :], on[:, h, :], ident[:, :])
                mm.then_inc(hg_out_turned, 1)
                unit(3)

            cm_phase(U_G, N_G, NU_G)
            cm_phase(U_QK, N_QK, NU_QK)
            pe.wait_ge(wg_split, 1)
            pe.wait_ge(hg_out_kept, TT + 1)
            for k, (a, b) in enumerate(((wg_hi, h_hi), (wg_hi, h_lo), (wg_lo, h_hi))):
                for j in range(KT):
                    mm = pe.matmul(ps[:, 4, :], a[:, j, :], b[:, j, :], start=(k == 0 and j == 0), stop=(k == 2 and j == KT - 1))
            mm.then_inc(gates_done, 1)
            tm_block(U_V, tok_evac, 8, tok_done)

            def cols_of_rows(q):
                if q == 1:
                    pe.wait_ge(rows_exp, 3)
                    for n in range(TT):
                        for k, row in enumerate((row_a, row_w, row_r3)):
                            mm = pe.transpose(ps[:, 4, 12 * n + 4 * k:12 * n + 4 * k + 4], row[:, n * P:(n + 1) * P],
                                              ident[0:ML_H, 0:ML_H])
                    mm.then_inc(cols_turned, 1)

            tm_block(U_V + 4, tok_evac, 12, tok_done, cols_of_rows)
            pe.wait_ge(tok_evac, 4 + 16)

            kst, qst, sc, kw, c_old = (heads(t, ML_H) for t in (ml_k, ml_q, ml_d, ml_kw, ml_c))
            hm8 = heads(ml_h, 8)
            DEN, UN = (lambda h: slice(h, h + 1)), (lambda h: slice(4 + h, 5 + h))
            with pe.Fori(0, TT) as i:
                def unit(s):
                    cm_unit(U_GB + 4 * i + s, N_GB + 4 * i + s, s % 2)
                pe.wait_ge(ml_keys_ready, i + 1)
                pe.wait_ge(ml_out_kept, i + 1)
                for h in range(ML_H):
                    pe.matmul(mKQ[:, h, :], kst[:, h, :], qk_all[:, h, ds(i * P, P)], start=True, stop=True)
                for h in range(ML_H):
                    pe.transpose(mKT[:, h, :], kst[:, h, :], ident[:, :])
                pe.wait_ge(ml_new_state, i + 1)
                for h in range(ML_H):
                    pe.matmul(mM[:, h, :], ident[0:ML_H, h:h + 1].broadcast_to([ML_H, P]), row_m[:, ds(i * P, P)],
                              start=True, stop=True)
                for h in range(ML_H):
                    mm = pe.matmul(mR[:, h, :], ident[0:ML_H, h:h + 1].broadcast_to([ML_H, P]), row_r2[:, ds(i * P, P)],
                                   start=True, stop=True)
                mm.then_inc(ml_scores_done, 1)
                unit(0)
                pe.wait_ge(ml_weighted_keys, i + 1)
                pe.wait_ge(ml_scores_ready, i + 1)
                pe.wait_ge(ml_queries_ready, i + 1)
                for h in range(ML_H):
                    pe.matmul(mX[:, h, :], kw[:, h, :], v_ml[:, ds(i, 1), h * ML_V:(h + 1) * ML_V], start=True, stop=True)
                    pe.matmul(ps[:, 3, UN(h)], kw[:, h, :], ones_col[:, 0:1], start=(h == 0), stop=True,
                              skip_group_check=True)
                pe.wait_ge(ml_h_ready, i + 1)
                for h in range(ML_H):
                    pe.matmul(mN[:, h, :], sc[:, h, :], v_ml[:, ds(i, 1), h * ML_V:(h + 1) * ML_V],
                              start=(h % 2 == 0), stop=False, skip_group_check=True)
                    pe.matmul(ps[:, 3, DEN(h)], sc[:, h, :], ones_col[:, 0:1], start=False, stop=False,
                              skip_group_check=True)
                    pe.matmul(mN[:, h, :], qst[:, h, :], c_old[:, h, :], start=False, stop=True, skip_group_check=True)
                    mm = pe.matmul(ps[:, 3, DEN(h)], qst[:, h, :], nstate[:, h:h + 1], start=False, stop=True,
                                   skip_group_check=True)
                mm.then_inc(ml_out_done, 1)
                unit(1)
                unit(2)
                pe.wait_ge(ml_normed, i + 1)
                for h in range(8):
                    mm = pe.transpose(mOT[:, 4 * (h % 2) + h // 2, :], hm8[:, h, :], ident[:, :])
                mm.then_inc(ml_out_turned, 1)
                unit(3)

            cm_phase(U_O, N_O, NU_O)

            pe.wait_ge(ml_out_kept, TT + 1)
            pe.wait_ge(y_lo, 1 + 8)
            with pe.Fori(0, 4) as i:
                for h in range(2):
                    pe.wait_ge(up_evac, 2 * i + h + 1)
                    for s, (y_h, y_l) in enumerate(((ya_hi, ya_lo), (yb_hi, yb_lo))):
                        if s == 1:
                            pe.wait_ge(y_lo, 1 + 16)
                            pe.wait_ge(cm_evac, N_O + NU_O + 2)
                        u = U_UP + 4 * i + 2 * h + s
                        w = [t[:, s, :].rearrange("p (j n) -> p j n", j=8) for t in (w_hi, w_lo)]
                        for a, (wk, yk) in enumerate(((0, y_h), (0, y_l), (1, y_h))):
                            if a != 1:
                                split_ready(u, wk)
                            for d in range(2):
                                for j in range(8):
                                    mm = pe.matmul(ps[:, 4 * h + 2 * s + d, :], w[wk][:, j, d * P:(d + 1) * P], yk[:, j, :],
                                                   start=(a == 0 and j == 0), stop=(a == 2 and j == 7))
                        mm.then_inc(unit_done, 1)

            pe.wait_ge(up_evac, 2 + 7)
            with pe.Fori(0, 3) as i:
                tm_block(U_OUT + 4 * i, o_evac, 4 * i, o_tok_done, lambda q: pe.wait_ge(m_lo, 1 + 4 * (q + 1)))

            def first_hidden(n, s):
                u = U_FF + s
                split_ready(u, 0)
                split_ready(u, 1)
                pe.wait_ge(h_lo_ready, 4 + 16 + 8 * n + 8)
                w = [t[:, s, :].rearrange("p (j n) -> p j n", j=KT) for t in (w_hi, w_lo)]
                tok = slice(n * 2 * P, (n + 1) * 2 * P)
                for a, b in ((0, h_hi), (0, h_lo), (1, h_hi)):
                    for j in range(KT):
                        mm = pe.matmul(ps[:, 4 + s, tok], w[a][:, j, :], b[:, j, tok],
                                       start=(n == 0 and j == 0 and a == 0 and b is h_hi), stop=False, skip_group_check=True)
                if n:
                    mm.then_inc(unit_done, 1)

            for half, tiles in enumerate(HALVES):
                for q in range(4):
                    u = U_OUT + 12 + 4 * half + q
                    split_ready(u, 0)
                    split_ready(u, 1)
                    tm_products(0, q % 2, h_hi, h_lo, 4 * q, 4, q == 0, q == 3,
                                lambda n: pe.wait_ge(o_evac, 12 + n + 1), o_tok_done, tiles)
                    if half == 1 and q == 2:
                        for n in HALVES[0]:
                            turn_tokens(x_rows[:, n, :], TT + n, (6, 7, 0, 1))
            first_hidden(0, 0)
            first_hidden(0, 1)
            for n in HALVES[1]:
                turn_tokens(x_rows[:, n, :], TT + n, (6, 7, 0, 1))
            first_hidden(1, 0)
            first_hidden(1, 1)

            def mlp_step(i, first=False, halves=None):
                u0 = U_FF + FF_UNITS * i
                for f in range(1 if first else 0, FG):
                    bank = (4, 6, 0, 2)[f]
                    pe.wait_ge(down_evac, 16 * i + (12, 12, 16, 16)[f])
                    for s in range(2):
                        w = [t[:, s, :].rearrange("p (j n) -> p j n", j=KT) for t in (w_hi, w_lo)]
                        split_ready(u0 + 2 * f + s, 0)
                        for k in (h_hi, h_lo):
                            for j in range(KT):
                                pe.matmul(ps[:, bank + s, :], w[0][:, j, :], k[:, j, :], start=(k is h_hi and j == 0), stop=False)
                        split_ready(u0 + 2 * f + s, 1)
                        for j in range(KT):
                            mm = pe.matmul(ps[:, bank + s, :], w[1][:, j, :], h_hi[:, j, :], start=False, stop=(j == KT - 1))
                        mm.then_inc(unit_done, 1)
                parts = halves or (tuple(range(TT)),)
                for part, d in ((part, d) for part in range(len(parts)) for d in range(4)):
                    u = u0 + 2 * FG + 4 * part + d
                    tiles = parts[part]
                    split_ready(u, 0)
                    split_ready(u, 1)
                    b0 = 4 if d % 2 == 0 else 0
                    w = [t[:, d % 2, :].rearrange("p (j n) -> p j n", j=FG) for t in (w_hi, w_lo)]
                    if d == 0:
                        pe.wait_ge(ff_mul, FG * i + 2)
                        for j in range(FG):
                            pe.wait_ge(ff_lo, FG * i + j + 1)
                            for n in tiles:
                                tok = slice(n * P, n * P + P)
                                pe.matmul(ps[:, b0 + n, :], act_hi[:, j, tok], w[0][:, j, :], start=(j == 0), stop=False)
                                pe.matmul(ps[:, b0 + n, :], act_hi[:, j, tok], w[1][:, j, :], start=False, stop=False)
                                mm = pe.matmul(ps[:, b0 + n, :], act_lo[:, j, tok], w[0][:, j, :], start=False, stop=(j == FG - 1))
                                if j == FG - 1:
                                    mm.then_inc(down_done if n != tiles[-1] else unit_done, 1)
                    else:
                        tm_products(b0, d % 2, act_hi, act_lo, 0, FG, True, True,
                                    lambda n: pe.wait_ge(down_evac, 16 * (i + 1) + len(tiles) * (4 * part + d - 2)
                                                         + n - tiles[0] + 1) if d >= 2 else None, down_done, tiles)

            mlp_step(0, True)
            with pe.Fori(1, FF_STEPS - 1) as i:
                mlp_step(i)
            mlp_step(FF_STEPS - 1, halves=HALVES)

        def units_of(first, per):
            return lambda i, k: (first + per * i + k, first // 2 + (per // 2) * i + k // 2, k % 2)

        @block.scalar
        def _(act):
            for s_, n in ((cm_evac, 2), (hg_out_copied, 1), (hg_out_kept, 1), (ml_out_kept, 1), (o_evac, 4)):
                act.sem_inc(s_, n)
            act.sem_inc(gate_stored, 16)

            def split_hi(u, rnd, s):
                act.wait_ge(raw_loaded[s], 16 * rnd + 16)
                act.wait_ge(unit_done, u + 1)
                act.copy(w_hi[:, s, :], raw[:, s, :]).then_inc(hi_ready, 1)

            def turned_hi(t, banks, groups=range(4)):
                for g in groups:
                    act.wait_ge(turned, 8 + 4 * t + g + 1)
                    n = t % TT
                    act.copy(h_hi[:, 4 * g:4 * g + 4, n * P:(n + 1) * P],
                             ps[:, banks[g], :].rearrange("p (k t) -> p k t", k=4)).then_inc(h_hi_ready, 1)

            for t in range(TT):
                act.wait_ge(x_loaded[t % 2], 16 * (t // 2) + 16)
                act.wait_ge(ms_ready, t + 1)
                act.activation(n_junk, n_x[:, t % 2, :], ACT.Square, accum_out=ss[:, 0:1]).then_inc(sq_done, 1)
                if t < 2:
                    split_hi(t, 0, t)
                turned_hi(t, (4, 5, 6, 7))
            un_i = units_of(U_I, 4)
            for i in range(2):
                for q in range(4):
                    if i or q:
                        split_hi(*un_i(i, q + 1))
                    if (i, q) == (1, 2):
                        act.wait_ge(prm_ready, 2)
                        act.activation(lb_t[:, 8:24], lb_t[:, 8:24], ACT.Exp).then_inc(act_step, 1)

            def columns(first, units, evac):
                un = units_of(first, 2)
                with act.Fori(0, units // 2) as i:
                    for s in range(2):
                        split_hi(*un(i, s + 1))
                        act.wait_ge(unit_done, first + 2 * i + s + 1 + RING)
                        evac(2 * i + s, ps[:, 6 + s, :], s)

            def blocks(first, n):
                un = units_of(first, 4)
                with act.Fori(0, n) as i:
                    for q in range(4):
                        split_hi(*un(i, q + 1))

            def into(dst, func, col):
                def evac(m, bank, s):
                    act.activation(dst[:, ds(m, 1), :], bank, func, bias=prm[:, ds(col + m, 1)]).then_inc(cm_evac, 1)
                return evac

            columns(U_F, NU_F, into(f_all, ACT.Sigmoid, 8))
            def hg_prep(i):
                act.wait_ge(hg_scores_done, i + 1)
                act.activation(heads(hg_e3), f_all[:, :, ds(i * P, P)], ACT.Ln).then_inc(logf_ready, 1)
                act.wait_ge(logf_sums, i + 1)
                act.wait_ge(hg_out_done, i + 1)
                act.activation(hg_e1, hg_b, ACT.Exp).then_inc(exp_ready, 1)
                act.activation(hg_e2, hg_b, ACT.Exp, scale=-1.0).then_inc(exp_ready, 1)
                act.wait_ge(logf_to_end, i + 1)
                act.activation(hg_e3, hg_e3, ACT.Exp).then_inc(exp_ready, 1)

            def gate_unit(i, k, u0, n0, tmp, which):
                m = 4 * i + k
                act.wait_ge(unit_done, u0 + m + 1 + RING)
                act.wait_ge(gate_stored, 16 * (KT * which + m) + 16)
                act.activation(tmp, ps[:, 6 + k % 2, :], ACT.Sigmoid,
                               bias=prm[:, ds(PB_GATES + KT * which + m, 1)]).then_inc(cm_evac, 1)
                act.wait_ge(cm_evac, n0 + m + 3)
                act.dma_start(gates_d[which, ds(m, 1), :, :].rearrange("a p t -> p (a t)"), tmp).then_inc(gate_stored, 16)

            act.wait_ge(f_ready, NU_F)
            hg_prep(0)
            columns(U_Q, NU_Q, into(q_all, ACT.Silu, 0))
            un_ga = units_of(U_GA, 4)

            def hg_step(i, last):
                split_hi(*un_ga(i, 1))
                act.wait_ge(mem_zero, 2)
                act.wait_ge(hg_scores_done, i + 2)
                for a in (0, CHUNK):
                    act.copy(heads(hg_at)[a:a + CHUNK, :, a:a + CHUNK], hA_[a:a + CHUNK, :, a:a + CHUNK])\
                        .then_inc(hg_scores_copied, 1)
                for a, dst in ((0, hg_ke0), (CHUNK, hg_ke1)):
                    act.copy(heads(dst)[a:a + CHUNK, :, :], hT_[a:a + CHUNK, :, :]).then_inc(k_end_copied, 1)
                gate_unit(i, 0, U_GA, N_GA, gate_a, 0)
                split_hi(*un_ga(i, 2))
                gate_unit(i, 1, U_GA, N_GA, gate_a, 0)
                split_hi(*un_ga(i, 3))
                act.wait_ge(hg_out_done, i + 2)
                act.copy(heads(hg_on), hO_).then_inc(hg_out_copied, 1)
                act.wait_ge(hg_new_state, i + 2)
                act.wait_ge(hg_out_copied, i + 2)
                act.activation(hg_sb, hg_on, ACT.Square).then_inc(hg_squares, 1)
                if not last:
                    hg_prep(i + 1)
                gate_unit(i, 2, U_GA, N_GA, gate_a, 0)
                split_hi(*un_ga(i, 4))
                act.wait_ge(hg_out_turned, i + 1)
                act.copy(q_all[:, :, ds(i * P, P)], hT_).then_inc(hg_out_kept, 1)
                gate_unit(i, 3, U_GA, N_GA, gate_a, 0)

            with act.Fori(0, TT - 1) as i:
                hg_step(i, False)
            hg_step(TT - 1, True)

            def gating(func, col, y_part, n0):
                def evac(h, bank, s):
                    act.wait_ge(y_mul, n0 + h + 1)
                    act.activation(g_act[:, s, :], bank, func, bias=prm[:, ds(col + h, 1)]).then_inc(cm_evac, 1)
                    act.wait_ge(y_mul, n0 + h + 3)
                    act.copy(y_part[:, ds(h, 1), :].rearrange("p a t -> p (a t)"), g_y).then_inc(y_hi, 1)
                return evac

            columns(U_G, NU_G, gating(ACT.Silu, 24, ya_hi, 0))

            def evac_qk(m, bank, s):
                act.wait_ge(qk_conv_done, m + 1)
                act.activation(qk_pre[:, 3:3 + T], bank, ACT.Identity, bias=prm[:, ds(32 + m, 1)]).then_inc(cm_evac, 1)
                act.wait_ge(qk_conv_done, m + 2)
                act.activation(qk_all[:, ds(m, 1), :].rearrange("p a t -> p (a t)"), qk_conv, ACT.Silu).then_inc(qk_ready, 1)

            act.wait_ge(wg_loaded, 16 * len(COLS_WG))
            act.copy(wg_hi, wg_raw).then_inc(act_step, 1)
            columns(U_QK, NU_QK, evac_qk)
            un_v = units_of(U_V, 4)
            for i in range(2):
                for q in range(4):
                    split_hi(*un_v(i, q + 1))
                    if (i, q) == (0, 0):
                        act.wait_ge(rows_ready, 1)
                        act.activation(row_w, row_w, ACT.Exp).then_inc(act_step, 1)
                        act.wait_ge(act_step, 3)
                        act.activation(row_w, row_w, ACT.Ln, bias=1.0).then_inc(act_step, 1)
                    if (i, q) == (1, 0):
                        act.wait_ge(rows_ready, 2)
                        for row, sign in ((row_r2, 1.0), (row_w, 1.0), (row_r3, -1.0)):
                            act.activation(row, row, ACT.Exp, scale=sign).then_inc(rows_exp, 1)

            def ml_prep(i):
                act.wait_ge(ml_scores_done, i + 1)
                act.wait_ge(ml_ms_ready, i + 1)
                act.activation(heads(ml_k, ML_H), qk_all[:, ML_H:2 * ML_H, ds(i * P, P)], ACT.Copy,
                               scale=SCALE).then_inc(ml_keys_ready, 1)

            ml_prep(0)
            un_gb = units_of(U_GB, 4)

            def ml_step(i, last):
                split_hi(*un_gb(i, 1))
                act.wait_ge(ml_exponents, i + 1)
                act.activation(ml_d, ml_d, ACT.Exp, scale=-1.0).then_inc(ml_weights_ready, 1)
                gate_unit(i, 0, U_GB, N_GB, gate_b, 1)
                split_hi(*un_gb(i, 2))
                act.wait_ge(ml_h_ready, i + 2)
                act.activation(ml_sq, ml_h, ACT.Square).then_inc(ml_squares, 1)
                gate_unit(i, 1, U_GB, N_GB, gate_b, 1)
                split_hi(*un_gb(i, 3))
                gate_unit(i, 2, U_GB, N_GB, gate_b, 1)
                split_hi(*un_gb(i, 4))
                if not last:
                    ml_prep(i + 1)
                act.wait_ge(ml_out_turned, i + 1)
                act.copy(qk_all[:, :, ds(i * P, P)], mOT).then_inc(ml_out_kept, 1)
                gate_unit(i, 3, U_GB, N_GB, gate_b, 1)

            with act.Fori(0, TT - 1) as i:
                ml_step(i, False)
            ml_step(TT - 1, True)

            act.wait_ge(gate_stored, 16 + 16 * 2 * KT)
            columns(U_O, NU_O, gating(ACT.Sigmoid, 48, yb_hi, 8))

            un_up = units_of(U_UP, 2)
            with act.Fori(0, 8) as i:
                split_hi(*un_up(i, 1))
                split_hi(*un_up(i, 2))
                for d in range(2):
                    act.wait_ge(m_ready, 2 * i + d + 1)
                    act.copy(h_hi[:, ds(2 * i + d, 1), :].rearrange("p a t -> p (a t)"), m_sum[:, d, :]).then_inc(m_hi, 1)

            un_out = units_of(U_OUT, 4)
            def out_square(i, n, halves=False):
                if halves:
                    if n % 2 == 0:
                        act.wait_ge(o_tok_done, 9 + n // 2 + 1)
                    else:
                        act.wait_ge(unit_done, U_OUT + 12 + 4 * (n // 2 + 1) + RING)
                elif n < TT - 1:
                    act.wait_ge(o_tok_done, 3 * i + n + 1)
                else:
                    act.wait_ge(unit_done, U_OUT + 4 * i + 4 + RING)
                act.wait_ge(o_sq, 4 * i + n + 1)
                act.activation(junk2[:, 0:512], ps[:, n, :], ACT.Square, accum_out=ss[:, ds(4 * n + i, 1)]).then_inc(o_sq, 1)

            act.sem_inc(o_sq, 1)
            with act.Fori(0, 3) as i:
                for q in range(4):
                    split_hi(*un_out(i, q + 1))
                for n in range(TT):
                    out_square(i, n)

            def x1_square(n):
                act.wait_ge(x1_ready, n + 1)
                act.wait_ge(o_sq, 1 + 12 + 2 * (n // 2) + 2)
                if n:
                    act.wait_ge(sq_done, TT + n)
                act.activation(junk2, x1[:, n, :], ACT.Square, accum_out=ss2[:, n:n + 1]).then_inc(sq_done, 1)

            for q in range(4):
                split_hi(*un_out(3, q + 1))
            t_banks = (6, 7, 0, 1)
            out_square(3, 0, True)
            out_square(3, 1, True)
            split_hi(*un_out(4, 1))
            x1_square(0)
            split_hi(*un_out(4, 2))
            split_hi(*un_out(4, 3))
            x1_square(1)
            turned_hi(TT, t_banks)
            turned_hi(TT + 1, t_banks)
            split_hi(*un_out(4, 4))
            out_square(3, 2, True)
            out_square(3, 3, True)
            split_hi(*un_out(4, 5))
            x1_square(2)
            x1_square(3)
            turned_hi(TT + 2, t_banks)
            turned_hi(TT + 3, t_banks)

            un_ff = units_of(U_FF, FF_UNITS)

            def final_squares(e, tiles=(0, 1)):
                half, d = e // 4, e % 4
                for k in tiles:
                    n = HALVES[half][k]
                    count = 2 * e + k
                    act.wait_ge(down_evac, 16 * FF_STEPS + count + 1)
                    if count:
                        act.wait_ge(fin_squares, count)
                    act.activation(z_junk, acc[:, n, 512 * d:512 * d + 512], ACT.Square,
                                   accum_out=ss[:, 4 * n + d:4 * n + d + 1]).then_inc(fin_squares, 1)

            def final_scale(n):
                act.wait_ge(fin_rstd_ready, n + 1)
                act.wait_ge(fin_gain_pool, 6 * (n // 2) + 2)
                act.activation(acc[:, n, 0:ZQ], acc[:, n, 0:ZQ], ACT.Copy, scale=rstd[:, n:n + 1]).then_inc(fin_scaled, 1)

            def mlp_step(i, first=False, last=False):
                u0 = U_FF + FF_UNITS * i
                for f in range(FG):
                    bank = (4, 6, 0, 2)[f]
                    if not (first and f == 0):
                        split_hi(*un_ff(i, 2 * f + 1))
                    act.wait_ge(unit_done, u0 + 2 * f + 1 + RING)
                    act.wait_ge(ff_conv, FG * i + f + 1)
                    act.copy(ff_pad[:, 0, 2:2 + T], ps[:, bank, :]).then_inc(ff_gate, 1)
                    split_hi(*un_ff(i, 2 * f + 2))
                    act.wait_ge(ff_conv, FG * i + f + 2)
                    act.activation(ff_c, ff_c, ACT.Gelu_apprx_tanh).then_inc(ff_gelu, 1)
                    act.wait_ge(ff_mul, FG * i + f + 1)
                    act.copy(act_hi[:, f, :], ff_v).then_inc(ff_hi, 1)
                for d in range(4):
                    if last:
                        break
                    split_hi(*un_ff(i, 2 * FG + d + 1))

            mlp_step(0, first=True)
            with act.Fori(1, FF_STEPS - 1) as i:
                mlp_step(i)
            mlp_step(FF_STEPS - 1, last=True)
            split_hi(*un_ff(FF_STEPS - 1, 2 * FG + 1))
            for e in range(7):
                if e < 6:
                    split_hi(*un_ff(FF_STEPS - 1, 2 * FG + e + 2))
                final_squares(e)
                if e in (4, 5):
                    final_scale(e - 4)
            final_squares(7)
            final_scale(2)
            final_scale(3)

        @block.gpsimd
        def _(pool):
            pool.memset(ident[:, :], 0.0).then_inc(consts, 1)
            pool.memset(neg_half, -0.5).then_inc(mem_zero, 1)
            pool.wait_ge(consts, 1)
            pool.affine_select(out=ident[:, :], in_=ident[:, :], compare_op=ALU.not_equal, fill=1.0, base=0,
                               pattern=[[-1, P]], channel_multiplier=1).then_inc(consts, 1)

            def tile_rows(v):
                return v.rearrange("l (n p) -> (l n) p", p=P)

            taps = ffn_conv_w.rearrange("l k (n p) -> (l k) n p", p=P)
            rows = [(0, PB, tile_rows(b_in[:, 0:C_IG])), (0, PB_GATES, tile_rows(b_in[:, C_GA:C_GA + 2 * D])),
                    (0, PLB, tile_rows(hg_lb_logits)), (0, PHG, tile_rows(hg_norm)), (0, PML, tile_rows(ml_norm)),
                    (0, PCB, tile_rows(ml_conv_b)), (1, PCW - 128, ml_conv_w.rearrange("l k (n p) -> (l k n) p", p=P)),
                    (1, PFB - 128, tile_rows(ffn_conv_b)), (1, PFW0 - 128, taps[0, :, :]), (2, 0, taps[1, :, :]),
                    (2, FT, taps[2, :, :])]
            def power(n, a=0):
                return pool.tensor_tensor(rstd[:, a:a + n], ms[:, a:a + n], neg_half[:, 0:n], ALU.pow)

            pool.wait_ge(mem_zero, 1)
            for t in range(TT):
                pool.wait_ge(ms_ready, t + 2)
                pool.wait_ge(xn_ready, t + 2)
                power(1).then_inc(rstd_ready, 1)
                if t in (1, 2):
                    for tile, r0, src in rows[:6] if t == 1 else rows[6:]:
                        pool.dma_start(prow[r0:r0 + src.shape[0], tile, :], src).then_inc(prm_loaded, 16)
                if t == 3:
                    pool.dma_start(vbias_hg, row_on_all(b_in, C_I, HG_W)).then_inc(vbias_loaded, 16)
                    for k in range(2):
                        pool.dma_start(gbias[32 * k:32 * k + ML_H, :],
                                       b_in[0, C_IG + ML_H * k:C_IG + ML_H * (k + 1)].unsqueeze(1)).then_inc(gbias_loaded, 16)

            pool.memset(hg_ke0, 0.0)
            pool.memset(hg_ke1, 0.0)
            pool.memset(hg_mask, 1.0).then_inc(hg_mask_ready, 1)
            pool.wait_ge(hg_mask_ready, 1)
            pool.memset(hg_mask.rearrange("p (c k) -> p c k", k=CHUNK)[:, :, 0:1], 0.0).then_inc(hg_mask_ready, 1)
            pool.wait_ge(tok_evac, 4 + 8)
            pool.memset(hg_at, 0.0).then_inc(mem_zero, 1)

            for i in range(TT):
                pool.wait_ge(hg_scores_copied, 2 * i + 2)
                pool.affine_select(out=heads(hg_at), in_=heads(hg_at), compare_op=ALU.is_ge, fill=0.0, base=0,
                                   pattern=[[0, HG_H], [1, P]], channel_multiplier=-1).then_inc(hg_scores_masked, 1)
                pool.wait_ge(hg_ms_ready, i + 2)
                power(8).then_inc(hg_rstd_ready, 1)

            pool.wait_ge(hg_out_turned, TT)
            with nc.allow_non_contiguous_dma(reason="few columns of the gates"):
                for a, n, c in COLS_WG:
                    pool.dma_start(wg_raw[:, :, a:a + n], w_in_d[:, :, C_IG + c:C_IG + c + n]).then_inc(wg_loaded, 16)

            pool.wait_ge(y_lo, 1 + 8)
            pool.wait_ge(gate_stored, 16 + 16 * KT)
            pool.dma_start(vbias_ml, row_on_all(b_in, C_V, ML_W)).then_inc(vbias_loaded, 16)

            for i in range(TT):
                pool.wait_ge(ml_weights_ready, i + 1)
                pool.affine_select(out=heads(ml_d, ML_H), in_=heads(ml_d, ML_H), compare_op=ALU.is_ge, fill=0.0, base=0,
                                   pattern=[[0, ML_H], [1, P]], channel_multiplier=-1).then_inc(ml_weights_masked, 1)
                pool.wait_ge(ml_ms_ready, i + 2)
                power(4).then_inc(ml_rstd_ready, 1)

            pool.wait_ge(gate_stored, 16 + 16 * 2 * KT)
            pool.wait_ge(y_lo, 1 + 16)
            with pool.Fori(0, 4) as i:
                for s in range(2):
                    pool.wait_ge(mg_used, 2 * i + s + 1)
                    for g in range(2):
                        pool.dma_start(m_gates[:, s, g, :, :], gates_d[g, ds(2 * (2 * i + s), 2), :, :]
                                       .rearrange("d p t -> p d t")).then_inc(mg_loaded[s], 16)
            pool.wait_ge(mg_used, 2 + 8)
            pool.wait_ge(m_lo, 1 + KT)
            pool.dma_start(g_post, row_on_all(norm_mix_post, 0, D)).then_inc(g_post_loaded, 16)
            for n in range(TT):
                pool.wait_ge(o_evac, 4 + 2 * n + 1)
                pool.dma_start(x_rows[:, n, :], x_d[n * P:(n + 1) * P, :]).then_inc(x2_loaded, 16)
            pool.dma_start(g_pre2, row_on_all(norm_ffn_pre, 0, D)).then_inc(x2_loaded, 16)
            for what, n in (("mix", 0), ("mix", 1), ("x1", 0), ("x1", 1), ("mix", 2), ("mix", 3), ("x1", 2), ("x1", 3)):
                if what == "mix":
                    pool.wait_ge(mix_ms_ready, n + 1)
                    power(1, n).then_inc(mix_rstd_ready, 1)
                else:
                    pool.wait_ge(ms_ready, 1 + TT + n + 1)
                    power(1, 4 + n).then_inc(rstd_ready, 1)
            pool.wait_ge(sq_done, 2 * TT)
            pool.memset(ff_pad[:, 0, 0:2], 0.0).then_inc(pad_zero, 1)

            def final_add(n):
                pool.wait_ge(fin_scaled, n + 1)
                pool.tensor_tensor(acc[:, n, 0:ZQ], acc[:, n, 0:ZQ], x1[:, n, 0:ZQ], ALU.add).then_inc(fin_done_pool, 1)

            def final_gain(half, d):
                for k, n in enumerate(HALVES[half]):
                    pool.wait_ge(fin_squares, 8 * half + 2 * d + k + 1)
                    part = slice(512 * d, 512 * d + 512)
                    pool.tensor_tensor(acc[:, n, part], acc[:, n, part], z_gain[:, part], ALU.mult).then_inc(fin_gain_pool, 1)

            def final_power(n):
                pool.wait_ge(fin_ms_ready, n + 1)
                power(1, n).then_inc(fin_rstd_ready, 1)

            pool.wait_ge(z_gain_loaded, 16)
            for d in range(3):
                final_gain(0, d)
            for n in range(2):
                final_power(n)
                final_add(n)
                final_gain(1, n)
            for n in HALVES[1]:
                final_power(n)
                final_add(n)

        @block.vector
        def _(dve):
            for s_, n in ((lo_ready, RING), (xn_ready, 2), (h_lo_ready, 4), (tok_evac, 4), (ms_ready, 1), (hg_ms_ready, 1),
                          (y_mul, 2), (y_lo, 1), (qk_conv_done, 1), (ml_ms_ready, 1), (ml_h_ready, 1), (mg_used, 2), (up_evac, 2),
                          (ff_conv, 1), (down_evac, 16)):
                dve.sem_inc(s_, n)

            def split_lo(u, rnd, s):
                dve.wait_ge(hi_ready, u + 1)
                dve.tensor_tensor(w_lo[:, s, :], raw[:, s, :], f32(w_hi[:, s, :]), ALU.subtract).then_inc(lo_ready, 1)

            made = [0]

            def then(ins):
                made[0] += 1
                ins.then_inc(dve_step, 1)
                dve.wait_ge(dve_step, made[0])

            dve.memset(ones_col, 1.0)
            dve.memset(m_prev[:, 0:1], 0.0)
            dve.memset(nstate, 0.0)

            def row_ms(t, total, a):
                dve.wait_ge(sq_done, t + 1)
                dve.tensor_scalar(ms[:, a:a + 1], total, 1.0 / D, EPS, ALU.mult, ALU.add).then_inc(ms_ready, 1)

            def row_scale(t, src, gain, to, a):
                dve.wait_ge(rstd_ready, t + 1)
                dve.scalar_tensor_tensor(out=to, in0=src, scalar=rstd[:, a:a + 1], in1=gain, op0=ALU.mult,
                                         op1=ALU.mult).then_inc(xn_ready, 1)

            def turned_lo(t, banks):
                n = t % TT
                for g in range(4):
                    dve.wait_ge(h_hi_ready, 4 * t + g + 1)
                    rows, tok = slice(4 * g, 4 * g + 4), slice(n * P, (n + 1) * P)
                    dve.tensor_tensor(h_lo[:, rows, tok], ps[:, banks[g], :].rearrange("p (k t) -> p k t", k=4),
                                      f32(h_hi[:, rows, tok]), ALU.subtract).then_inc(h_lo_ready, 1)

            for t in range(TT):
                row_ms(t, ss[:, 0:1], 0)
                dve.wait_ge(gain_loaded, 16)
                if t > 1:
                    dve.wait_ge(turned, 4 * t + 4)
                row_scale(t, n_x[:, t % 2, :], n_gain, n_xn[:, t % 2, :], 0)
                if t < 2:
                    split_lo(t, 0, t)
                turned_lo(t, (4, 5, 6, 7))
            def columns(first, units, work):
                un = units_of(first, 2)
                with dve.Fori(0, units // 2) as i:
                    for s in range(2):
                        split_lo(*un(i, s + 1))
                        if work:
                            work(2 * i + s, s, i)

            def flat(t, m):
                return t[:, ds(m, 1), :].rearrange("p a t -> p (a t)")

            def f_affine(h, s, i):
                dve.wait_ge(cm_evac, N_F + h + 3)
                dve.tensor_scalar(flat(f_all, h), flat(f_all, h), omlb[:, ds(h, 1)], lb[:, ds(h, 1)], ALU.mult,
                                  ALU.add).then_inc(f_ready, 1)

            def v_block(i, first, v_all, bias, b0, between=None, q0=0):
                un = units_of(first, 4)
                for q in range(q0, 4):
                    split_lo(*un(i, q + 1))
                    if between:
                        between(q)
                for n in range(TT):
                    if n < TT - 1:
                        dve.wait_ge(tok_done, 3 * (b0 + i) + n + 1)
                    else:
                        dve.wait_ge(unit_done, first + 4 * i + 4 + RING)
                    dve.tensor_tensor(v_all[:, n, ds(512 * i, 512)], ps[:, n, :], bias[:, ds(512 * i, 512)],
                                      ALU.add).then_inc(tok_evac, 1)

            def parameters(q):
                if q == 1:
                    dve.wait_ge(prm_turned, 1)
                    then(dve.tensor_copy(prm[:, 0:248], ps[:, 4, 0:248]))
                    dve.tensor_copy(prm[:, 256:344], ps[:, 4, 256:344]).then_inc(prm_ready, 1)
                    then(dve.tensor_tensor(lb_t[:, 0:8], prm[:, PLB:PLB + 8], prm[:, PLB + 8:PLB + 16], ALU.max))
                    then(dve.tensor_tensor(lb_t[:, 8:16], prm[:, PLB:PLB + 8], lb_t[:, 0:8], ALU.subtract))
                    dve.tensor_tensor(lb_t[:, 16:24], prm[:, PLB + 8:PLB + 16], lb_t[:, 0:8], ALU.subtract).then_inc(prm_ready, 1)
                elif q == 3:
                    dve.wait_ge(act_step, 1)
                    then(dve.tensor_tensor(lb_t[:, 0:8], lb_t[:, 8:16], lb_t[:, 16:24], ALU.add))
                    then(dve.reciprocal(lb_t[:, 0:8], lb_t[:, 0:8]))
                    then(dve.tensor_tensor(lb, lb_t[:, 8:16], lb_t[:, 0:8], ALU.mult))
                    then(dve.tensor_scalar(omlb, lb, -1.0, 1.0, ALU.mult, ALU.add))

            dve.wait_ge(vbias_loaded, 16)
            v_block(0, U_I, v_hg, vbias_hg, 0, q0=1)
            v_block(1, U_I, v_hg, vbias_hg, 0, parameters)
            columns(U_F, NU_F, f_affine)
            def chunks(t):
                return t.rearrange("p (c k) -> p c k", k=CHUNK)

            def hg_prep_b(i):
                dve.wait_ge(logf_ready, i + 1)
                dve.tensor_tensor_scan(hg_b[:, 0:T], hg_mask, hg_e3[:, 0:T], 0.0, ALU.mult, ALU.add)
                dve.tensor_tensor_scan(hg_b[:, T:2 * T], hg_mask, hg_e3[:, T:2 * T], 0.0, ALU.mult,
                                       ALU.add).then_inc(logf_sums, 1)
                dve.wait_ge(logf_sums, i + 1)
                dve.tensor_tensor(chunks(hg_e3), chunks(hg_b)[:, :, CHUNK - 1:CHUNK].broadcast_to([P, 2 * HG_H, CHUNK]),
                                  chunks(hg_b), ALU.subtract).then_inc(logf_to_end, 1)

            def hg_prep(i, with_q=True):
                dve.wait_ge(exp_ready, 3 * i + 3)
                f_pair = f_all[:, :, ds(i * P, P)]
                dve.wait_ge(hg_new_state, i + 1)
                dve.tensor_copy(dec.rearrange("p h c -> p (h c)").unsqueeze(2), chunks(hg_e1)[:, :, CHUNK - 1:CHUNK])\
                    .then_inc(decay_kept, 1)
                for e in (hg_e2, hg_e3):
                    dve.scalar_tensor_tensor(out=heads(e), in0=f_pair, scalar=1.0, in1=heads(e), op0=ALU.subtract,
                                             op1=ALU.mult)
                dve.wait_ge(decay_kept, i + 1)
                if with_q:
                    dve.scalar_tensor_tensor(out=heads(hg_e1), in0=q_all[:, :, ds(i * P, P)], scalar=-SCALE,
                                             in1=heads(hg_e1), op0=ALU.mult, op1=ALU.mult).then_inc(hg_prepared, 1)

            def first_q_dec(h, s, i):
                dve.wait_ge(cm_evac, N_Q + h + 3)
                dve.scalar_tensor_tensor(out=hg_e1[:, ds(h * P, P)], in0=flat(q_all, h)[:, 0:P], scalar=-SCALE,
                                         in1=hg_e1[:, ds(h * P, P)], op0=ALU.mult, op1=ALU.mult).then_inc(q_dec_first, 1)

            dve.memset(hg_sa, 0.0).then_inc(hg_new_state, 1)
            dve.wait_ge(hg_mask_ready, 2)
            hg_prep_b(0)
            hg_prep(0, False)
            columns(U_Q, NU_Q, first_q_dec)
            dve.wait_ge(q_dec_first, NU_Q)
            dve.sem_inc(hg_prepared, 1)
            un_ga = units_of(U_GA, 4)

            def hg_state(new, old, c, update):
                for h in range(HG_H):
                    ins = dve.scalar_tensor_tensor(out=heads(new)[:, h, :], in0=heads(old)[:, h, :], scalar=dec[:, h, c:c + 1],
                                                   in1=update[:, h, :], op0=ALU.mult, op1=ALU.add)
                return ins

            def hg_step(i, last):
                split_lo(*un_ga(i, 1))
                split_lo(*un_ga(i, 2))
                dve.wait_ge(hg_update0, i + 1)
                hg_state(hg_sb, hg_sa, 0, hT_).then_inc(hg_mid_state, 1)
                dve.wait_ge(hg_update1, i + 1)
                dve.wait_ge(hg_mid_state, i + 1)
                hg_state(hg_sa, hg_sb, 1, hA_).then_inc(hg_new_state, 1)
                split_lo(*un_ga(i, 3))
                dve.wait_ge(hg_squares, i + 1)
                dve.tensor_reduce(ss[:, 0:8], heads(hg_sb), AX.X, ALU.add).then_inc(hg_sums, 1)
                dve.wait_ge(hg_sums, i + 1)
                dve.tensor_scalar(ms[:, 0:8], ss[:, 0:8], 1.0 / P, EPS, ALU.mult, ALU.add).then_inc(hg_ms_ready, 1)
                if not last:
                    hg_prep_b(i + 1)
                dve.wait_ge(hg_rstd_ready, i + 1)
                dve.tensor_tensor(heads(hg_on), heads(hg_on), rstd[:, 0:8].unsqueeze(2).broadcast_to([P, HG_H, P]),
                                  ALU.mult).then_inc(hg_normed, 1)
                split_lo(*un_ga(i, 4))
                if not last:
                    hg_prep(i + 1)

            with dve.Fori(0, TT - 1) as i:
                hg_step(i, False)
            hg_step(TT - 1, True)

            def gating(src, gain0, y_h, y_l, n0, cm0, slot_of):
                def work(h, s, i):
                    dve.wait_ge(cm_evac, cm0 + h + 3)
                    dve.wait_ge(y_lo, n0 + h + 1)
                    dve.scalar_tensor_tensor(out=g_y, in0=flat(src, slot_of(s, i)), scalar=prm[:, ds(gain0 + h, 1)],
                                             in1=g_act[:, s, :], op0=ALU.mult, op1=ALU.mult).then_inc(y_mul, 1)
                    dve.wait_ge(y_hi, n0 + h + 1)
                    dve.tensor_tensor(flat(y_l, h), g_y, f32(flat(y_h, h)), ALU.subtract).then_inc(y_lo, 1)
                return work

            dve.wait_ge(hg_out_kept, TT + 1)
            columns(U_G, NU_G, gating(q_all, PHG, ya_hi, ya_lo, 0, N_G, lambda s, i: 2 * i + s))

            then(dve.memset(qk_pre[:, 0:3], 0.0))

            def qk_conv_tile(m, s, i):
                dve.wait_ge(cm_evac, N_QK + m + 3)
                dve.wait_ge(qk_ready, m + 1)
                dve.tensor_scalar(qk_conv, qk_pre[:, 3:3 + T], prm[:, ds(PCW + 24 + m, 1)], prm[:, ds(PCB + m, 1)],
                                  ALU.mult, ALU.add).then_inc(conv_tap, 1)
                for n, k in enumerate((2, 1, 0)):
                    dve.wait_ge(conv_tap, 3 * m + n + 1)
                    dve.scalar_tensor_tensor(out=qk_conv, in0=qk_pre[:, k:k + T], scalar=prm[:, ds(PCW + 8 * k + m, 1)],
                                             in1=qk_conv, op0=ALU.mult, op1=ALU.add)\
                        .then_inc(qk_conv_done if k == 0 else conv_tap, 1)

            dve.sem_inc(qk_ready, 1)
            dve.wait_ge(act_step, 2)
            dve.tensor_tensor(wg_lo, wg_raw, f32(wg_hi), ALU.subtract).then_inc(wg_split, 1)
            columns(U_QK, NU_QK, qk_conv_tile)

            def ml_chunks(t):
                return t.rearrange("p (c k) -> p c k", k=P)

            def rows_max(c):
                span, end = slice(c * P, (c + 1) * P), slice((c + 1) * P - 1, (c + 1) * P)
                then(dve.tensor_tensor_scan(row_m[:, span], row_a[:, span], row_a[:, span], m_prev[:, c:c + 1], ALU.max,
                                            ALU.max))
                then(dve.tensor_tensor(m_prev[:, c + 1:c + 2], row_b[:, end], row_m[:, end], ALU.add))

            def rows_step(q):
                if q == 0:
                    then(dve.memset(mask_row, 1.0))
                    then(dve.memset(ml_chunks(mask_row)[:, :, 0:1], 0.0))
                    dve.wait_ge(gates_done, 1)
                    dve.wait_ge(gbias_loaded, 32)
                    then(dve.tensor_scalar(row_a, ps[0:ML_H, 4, :], gbias[0:ML_H, :], None, ALU.add))
                    then(dve.tensor_scalar(row_t, ps[32:32 + ML_H, 4, :], gbias[32:32 + ML_H, :], None, ALU.add))
                    dve.scalar_tensor_tensor(out=row_w, in0=row_t, scalar=-1.0, in1=row_t, op0=ALU.mult,
                                             op1=ALU.min).then_inc(rows_ready, 1)
                elif q == 1:
                    dve.wait_ge(act_step, 4)
                    then(dve.scalar_tensor_tensor(out=row_t, in0=row_t, scalar=0.0, in1=row_w, op0=ALU.min,
                                                  op1=ALU.subtract))
                    then(dve.tensor_tensor_scan(row_b, mask_row, row_t, 0.0, ALU.mult, ALU.add))
                    then(dve.tensor_tensor(row_a, row_a, row_b, ALU.subtract))
                elif q == 2:
                    for c in range(TT):
                        rows_max(c)
                else:
                    dve.tensor_tensor(ml_chunks(row_r2), m_prev[:, 0:TT].unsqueeze(2).broadcast_to([ML_H, TT, P]),
                                      ml_chunks(row_m), ALU.subtract)
                    dve.tensor_tensor(ml_chunks(row_w), ml_chunks(row_a), ml_chunks(row_m)[:, :, P - 1:P]
                                      .broadcast_to([ML_H, TT, P]), ALU.subtract)
                    dve.tensor_tensor(row_r3, row_b, row_m, ALU.add).then_inc(rows_ready, 1)

            def cols_step(q):
                if q == 3:
                    dve.wait_ge(cols_turned, 1)
                    dve.tensor_copy(cols.rearrange("p n k c -> p (n k c)"), ps[:, 4, 0:48])

            dve.wait_ge(vbias_loaded, 32)
            v_block(0, U_V, v_ml, vbias_ml, 2, rows_step)
            v_block(1, U_V, v_ml, vbias_ml, 2, cols_step)

            hd = heads(ml_d, ML_H)
            dve.wait_ge(qk_ready, 1 + NU_QK)
            dve.memset(ml_c, 0.0).then_inc(ml_new_state, 1)
            dve.wait_ge(ml_new_state, 1)
            un_gb = units_of(U_GB, 4)

            def ml_state():
                for h in range(ML_H):
                    state = heads(ml_c, ML_H)[:, h, :]
                    dve.scalar_tensor_tensor(out=state, in0=state, scalar=decm[:, h:h + 1], in1=mX[:, h, :], op0=ALU.mult,
                                             op1=ALU.add)
                dve.tensor_tensor(nstate, nstate, decm, ALU.mult).then_inc(ml_sums_decayed, 1)

            def ml_step(i):
                split_lo(*un_gb(i, 1))
                dve.wait_ge(ml_scores_done, i + 2)
                col = cols[:, ds(i, 1), :, :].rearrange("p n k c -> p (n k) c")
                for h in range(ML_H):
                    ins = dve.tensor_scalar(hd[:, h, :], mM[:, h, :], col[:, 0, h:h + 1], 0.0, ALU.subtract, ALU.max)
                ins.then_inc(ml_exponents, 1)
                dve.tensor_copy(decm.unsqueeze(2), mR[:, :, P - 1:P])
                dve.tensor_tensor(heads(ml_q, ML_H), qk_all[:, 0:ML_H, ds(i * P, P)], mR, ALU.mult).then_inc(ml_queries_ready, 1)
                dve.tensor_tensor(heads(ml_kw, ML_H), mKT, col[:, 1, :].unsqueeze(2).broadcast_to([P, ML_H, P]),
                                  ALU.mult).then_inc(ml_weighted_keys, 1)
                dve.wait_ge(ml_weights_masked, i + 1)
                dve.tensor_tensor(hd, mKQ, hd, ALU.mult).then_inc(ml_scores_ready, 1)
                split_lo(*un_gb(i, 2))
                dve.wait_ge(ml_out_done, i + 1)
                dve.tensor_scalar(den[:, 0:4], ps[:, 3, 0:4], -1.0, None, ALU.mult).then_inc(den_step, 1)
                dve.wait_ge(den_step, 5 * i + 1)
                dve.tensor_tensor(den[:, 0:4], ps[:, 3, 0:4], den[:, 0:4], ALU.max).then_inc(den_step, 1)
                dve.wait_ge(den_step, 5 * i + 2)
                dve.tensor_tensor(den[:, 0:4], den[:, 0:4], col[:, 2, :], ALU.max).then_inc(den_step, 1)
                dve.wait_ge(den_step, 5 * i + 3)
                dve.reciprocal(den[:, 4:8], den[:, 0:4]).then_inc(den_step, 1)
                dve.wait_ge(den_step, 5 * i + 4)
                dve.tensor_tensor(heads(ml_h, ML_H), mN, den[:, 4:8].unsqueeze(2).broadcast_to([P, ML_H, ML_V]),
                                  ALU.mult).then_inc(ml_h_ready, 1)
                ml_state()
                dve.wait_ge(ml_sums_decayed, i + 1)
                dve.tensor_tensor(nstate, nstate, ps[:, 3, 4:4 + ML_H], ALU.add).then_inc(ml_new_state, 1)
                dve.wait_ge(ml_squares, i + 1)
                dve.tensor_reduce(ss[:, 0:4], heads(ml_sq, ML_H), AX.X, ALU.add).then_inc(den_step, 1)
                dve.wait_ge(den_step, 5 * i + 5)
                dve.tensor_scalar(ms[:, 0:4], ss[:, 0:4], 1.0 / ML_V, EPS, ALU.mult, ALU.add).then_inc(ml_ms_ready, 1)
                split_lo(*un_gb(i, 3))
                dve.wait_ge(ml_rstd_ready, i + 1)
                dve.tensor_tensor(heads(ml_h, ML_H), heads(ml_h, ML_H),
                                  rstd[:, 0:4].unsqueeze(2).broadcast_to([P, ML_H, ML_V]), ALU.mult).then_inc(ml_normed, 1)
                split_lo(*un_gb(i, 4))
                dve.wait_ge(ml_new_state, i + 2)

            with dve.Fori(0, TT) as i:
                ml_step(i)

            dve.wait_ge(ml_out_kept, TT + 1)
            columns(U_O, NU_O, gating(qk_all, PML, yb_hi, yb_lo, 8, N_O, lambda s, i: 4 * s + i))

            un_up = units_of(U_UP, 2)

            def merge(i, j, s):
                split_lo(U_UP + 2 * j + 1, U_UP // 2 + j, 1)
                split_lo(U_UP + 2 * j + 2, U_UP // 2 + j + 1, 0)
                dve.wait_ge(unit_done, U_UP + 2 * j + 2 + RING)
                dve.wait_ge(mg_loaded[s], 32 * i + 32)
                for d in range(2):
                    dve.wait_ge(m_lo, 2 * j + d + 1)
                    dve.tensor_tensor(m_a, ps[:, 4 * s + d, :], m_gates[:, s, 0, d, :], ALU.mult)
                    dve.tensor_tensor(m_b, ps[:, 4 * s + 2 + d, :], m_gates[:, s, 1, d, :], ALU.mult)\
                        .then_inc(merge_mul if d == 0 else up_evac, 1)
                    if d == 0:
                        dve.wait_ge(merge_mul, j + 1)
                    else:
                        dve.wait_ge(up_evac, j + 3)
                    dve.tensor_tensor(m_sum[:, d, :], m_a, m_b, ALU.add).then_inc(m_ready, 1)
                    dve.wait_ge(m_hi, 2 * j + d + 1)
                    dve.tensor_tensor(flat(h_lo, 2 * j + d), m_sum[:, d, :], f32(flat(h_hi, 2 * j + d)),
                                      ALU.subtract).then_inc(m_lo, 1)
                dve.sem_inc(mg_used, 1)

            dve.sem_inc(m_lo, 1)
            with dve.Fori(0, 4) as i:
                for s in range(2):
                    merge(i, 2 * i + s, s)

            un_out = units_of(U_OUT, 4)
            def out_evac(i, n):
                dve.wait_ge(o_sq, 1 + 4 * i + n + 1)
                dve.tensor_tensor(x1[:, n, ds(512 * i, 512)], ps[:, n, :], g_post[:, ds(512 * i, 512)], ALU.mult)\
                    .then_inc(o_evac, 1)

            with dve.Fori(0, 3) as i:
                for q in range(4):
                    split_lo(*un_out(i, q + 1))
                dve.wait_ge(g_post_loaded, 16)
                for n in range(TT):
                    out_evac(i, n)
            for q in range(4):
                split_lo(*un_out(3, q + 1))

            def mix_ms(n):
                out_evac(3, n)
                then(dve.tensor_reduce(ms[:, n:n + 1], ss[:, 4 * n:4 * n + 4], AX.X, ALU.add))
                dve.tensor_scalar(ms[:, n:n + 1], ms[:, n:n + 1], 1.0 / D, EPS, ALU.mult, ALU.add).then_inc(mix_ms_ready, 1)

            def x1_rows(n):
                dve.wait_ge(mix_rstd_ready, n + 1)
                dve.wait_ge(o_evac, 4 + 12 + n + 1)
                dve.scalar_tensor_tensor(out=x1[:, n, :], in0=x1[:, n, :], scalar=rstd[:, n:n + 1], in1=x_rows[:, n, :],
                                         op0=ALU.mult, op1=ALU.add).then_inc(x1_ready, 1)

            def x1_norm(n):
                row_ms(TT + n, ss2[:, n:n + 1], 4 + n)
                row_scale(TT + n, x1[:, n, :], g_pre2, x_rows[:, n, :], 4 + n)

            t_banks = (6, 7, 0, 1)
            dve.wait_ge(x2_loaded, 16 * (TT + 1))
            mix_ms(0)
            x1_rows(0)
            split_lo(*un_out(4, 1))
            mix_ms(1)
            x1_norm(0)
            split_lo(*un_out(4, 2))
            x1_rows(1)
            split_lo(*un_out(4, 3))
            x1_norm(1)
            turned_lo(TT, t_banks)
            turned_lo(TT + 1, t_banks)
            split_lo(*un_out(4, 4))
            mix_ms(2)
            x1_rows(2)
            split_lo(*un_out(4, 5))
            mix_ms(3)
            x1_rows(3)
            x1_norm(2)
            x1_norm(3)
            turned_lo(TT + 2, t_banks)
            turned_lo(TT + 3, t_banks)

            un_ff = units_of(U_FF, FF_UNITS)

            def mlp_step(i, first=False, last=False):
                u0 = U_FF + FF_UNITS * i
                for f in range(FG):
                    bank = (4, 6, 0, 2)[f]
                    t = FG * i + f
                    if not (first and f == 0):
                        split_lo(*un_ff(i, 2 * f + 1))
                    split_lo(*un_ff(i, 2 * f + 2))
                    dve.wait_ge(ff_gate, t + 1)
                    dve.tensor_scalar(ff_c, ff_pad[:, 0, 2:2 + T], prm[:, ds(PFW1 + FT + t, 1)], prm[:, ds(PFB + t, 1)],
                                      ALU.mult, ALU.add).then_inc(ff_chain, 1)
                    dve.wait_ge(ff_chain, 2 * t + 1)
                    dve.scalar_tensor_tensor(out=ff_c, in0=ff_pad[:, 0, 1:1 + T], scalar=prm[:, ds(PFW1 + t, 1)], in1=ff_c,
                                             op0=ALU.mult, op1=ALU.add).then_inc(ff_chain, 1)
                    dve.wait_ge(ff_chain, 2 * t + 2)
                    dve.scalar_tensor_tensor(out=ff_c, in0=ff_pad[:, 0, 0:T], scalar=prm[:, ds(PFW0 + t, 1)], in1=ff_c,
                                             op0=ALU.mult, op1=ALU.add).then_inc(ff_conv, 1)
                    dve.wait_ge(ff_gelu, t + 1)
                    dve.wait_ge(unit_done, u0 + 2 * f + 2 + RING)
                    dve.tensor_tensor(ff_v, ps[:, bank + 1, :], ff_c, ALU.mult).then_inc(ff_mul, 1)
                    dve.wait_ge(ff_hi, t + 1)
                    dve.tensor_tensor(act_lo[:, f, :], ff_v, f32(act_hi[:, f, :]), ALU.subtract).then_inc(ff_lo, 1)
                    dve.wait_ge(ff_lo, t + 1)
                for d in range(4):
                    if last:
                        break
                    split_lo(*un_ff(i, 2 * FG + d + 1))
                    b0 = 4 if d % 2 == 0 else 0
                    for n in range(TT):
                        if n < TT - 1:
                            dve.wait_ge(down_done, 3 * (4 * i + d) + n + 1)
                        else:
                            dve.wait_ge(unit_done, u0 + 2 * FG + d + 1 + RING)
                        part = acc[:, n, 512 * d:512 * d + 512]
                        if first:
                            dve.tensor_copy(part, ps[:, b0 + n, :]).then_inc(down_evac, 1)
                        else:
                            dve.tensor_tensor(part, part, ps[:, b0 + n, :], ALU.add).then_inc(down_evac, 1)

            def down_tile(e, k):
                if k == 0:
                    dve.wait_ge(down_done, 12 * (FF_STEPS - 1) + e + 1)
                else:
                    dve.wait_ge(unit_done, UNITS - 8 + e + 1 + RING)
                n, d = HALVES[e // 4][k], e % 4
                part = acc[:, n, 512 * d:512 * d + 512]
                dve.tensor_tensor(part, part, ps[:, (4 if d % 2 == 0 else 0) + n, :], ALU.add).then_inc(down_evac, 1)

            def final_mean(n):
                dve.wait_ge(fin_squares, 8 * (n // 2) + 6 + n % 2 + 1)
                then(dve.tensor_reduce(ms[:, n:n + 1], ss[:, 4 * n:4 * n + 4], AX.X, ALU.add))
                dve.tensor_scalar(ms[:, n:n + 1], ms[:, n:n + 1], 1.0 / D, EPS, ALU.mult, ALU.add).then_inc(fin_ms_ready, 1)
                cols = slice(3 * 512, D)
                dve.wait_ge(z_gain_loaded, 16)
                dve.tensor_tensor(acc[:, n, cols], acc[:, n, cols], z_gain[:, cols], ALU.mult).then_inc(fin_gain_dve, 1)

            def final_rows(n):
                dve.wait_ge(fin_rstd_ready, n + 1)
                dve.wait_ge(fin_gain_dve, (1, 2, 5, 6)[n])
                dve.wait_ge(fin_gain_pool, (6, 6, 10, 10)[n])
                for cols in (slice(ZQ, ZM), slice(ZM, D)):
                    dve.scalar_tensor_tensor(out=acc[:, n, cols], in0=acc[:, n, cols], scalar=rstd[:, n:n + 1],
                                             in1=x1[:, n, cols], op0=ALU.mult, op1=ALU.add).then_inc(fin_done_dve, 1)

            dve.wait_ge(pad_zero, 1)
            mlp_step(0, first=True)
            dve.wait_ge(down_evac, 16 * 2)
            with dve.Fori(1, FF_STEPS - 1) as i:
                mlp_step(i)
                dve.wait_ge(down_evac, 16 * (i + 2))
            mlp_step(FF_STEPS - 1, last=True)
            split_lo(*un_ff(FF_STEPS - 1, 2 * FG + 1))
            for e in range(7):
                down_tile(e, 0)
                down_tile(e, 1)
                if e < 6:
                    split_lo(*un_ff(FF_STEPS - 1, 2 * FG + e + 2))
                if e in (4, 5):
                    final_mean(e - 4)
                    final_rows(e - 4)
            down_tile(7, 0)
            dve.wait_ge(fin_squares, 14)
            for n in HALVES[1]:
                dve.tensor_tensor(acc[:, n, 1024:1536], acc[:, n, 1024:1536], z_gain[:, 1024:1536], ALU.mult)\
                    .then_inc(fin_gain_dve, 1)
            down_tile(7, 1)
            for n in HALVES[1]:
                final_mean(n)
                final_rows(n)


_INS = ["x", "norm_mix_pre", "norm_mix_post", "norm_ffn_pre", "norm_ffn_post", "w_in", "b_in", "hg_lb_logits", "hg_norm",
        "ml_conv_w", "ml_conv_b", "ml_norm", "w_up_a", "w_up_b", "w_out", "ffn_w_gate", "ffn_w_up", "ffn_conv_w",
        "ffn_conv_b", "ffn_w_down"]
_OUT_SHAPE = (1, T, D)


def kernel(**inputs):
    import numpy as np
    import concourse.bacc as bacc
    from concourse.bass_utils import run_bass_kernel_spmd

    nc = bacc.Bacc("TRN2", target_bir_lowering=False, num_devices=1)
    arrays, args = {}, []
    for name in _INS:
        a = np.ascontiguousarray(inputs[name])
        arrays[f"in_{name}"] = a
        args.append(nc.dram_tensor(f"in_{name}", a.shape, mybir.dt.from_np(a.dtype), kind="ExternalInput").ap())
    args.append(nc.dram_tensor("out", _OUT_SHAPE, F32, kind="ExternalOutput").ap())
    build(nc, *args)
    r = run_bass_kernel_spmd(nc, [arrays], core_ids=[0])
    return r.results[0]["out"]
```
